# Optimizing a Trainium2 kernel written in Bass

```python
import jax, jax.numpy as jnp
from jax import lax
import numpy as np

D_MODEL = 1024
BATCH = 1
SEQ = 512
DEPTH = 1
DEC_BATCH = 8
DEC_SEQ = 4
PAST_LEN = 2048
PAGE_SIZE = 128

EPS = 1e-6
N_MEM = 256
POOL_WINDOWS = (2, 4, 8, 16)
POOL_GROUP = 128
POOL_WIDTH = POOL_GROUP * len(POOL_WINDOWS)
POOL_HIST = max(POOL_WINDOWS) - 1
MLA_HEADS = 8
Q_LORA = 384
KV_LORA = 256
QK_NOPE = 64
QK_ROPE = 32
V_HEAD = 64
ROPE_BASE = 10000.0
ATTN_BLOCK = 128
X_HEADS = 4
X_HEAD_DIM = 128
X_WIDTH = X_HEADS * X_HEAD_DIM
N_BRANCH = 3
SPLITS = (POOL_WIDTH, Q_LORA, KV_LORA, QK_ROPE, X_WIDTH)
IN_WIDTH = sum(SPLITS) + N_BRANCH * D_MODEL
PEER_HEADS = 8
N_KEYS = 128
N_EXPERTS = N_KEYS * N_KEYS
PEER_QDIM = 256
PEER_HALF = PEER_QDIM // 2
PEER_TOPK = 16
PEER_CHUNK = 128

kernel_name = 'pool_mla_memory_peer_hybrid_step'

def rmsnorm(x, g):
    xf = x.astype(jnp.float32)
    y = xf * lax.rsqrt(jnp.mean(xf * xf, axis=-1, keepdims=True) + EPS)
    return (y * g.astype(jnp.float32)).astype(x.dtype)

def rope(x, start):
    T = x.shape[1]
    half = QK_ROPE // 2
    inv = jnp.power(ROPE_BASE, -jnp.arange(half, dtype=jnp.float32) / half)
    pos = (start + jnp.arange(T, dtype=jnp.int32)).astype(jnp.float32)
    ang = pos[:, None] * inv[None, :]
    shape = (T,) + (1,) * (x.ndim - 3) + (half,)
    cos = jnp.cos(ang).reshape(shape)
    sin = jnp.sin(ang).reshape(shape)
    xf = x.astype(jnp.float32)
    x1, x2 = xf[..., :half], xf[..., half:]
    return jnp.concatenate([x1 * cos - x2 * sin, x1 * sin + x2 * cos], axis=-1).astype(x.dtype)

def split_projection(xn, w_in):
    z = xn @ w_in
    offs = [int(o) for o in np.cumsum(SPLITS)]
    u, cq, ckv, kr, qx, gates = jnp.split(z, offs, axis=-1)
    return u, cq, ckv, kr, qx, gates

def pool_mix(u, hist, start, w_pool_grp, pool_scale):
    B, T, _ = u.shape
    zc = jnp.concatenate([hist, u], axis=1)
    z = zc.astype(jnp.float32)
    cs = jnp.concatenate([jnp.zeros_like(z[:, :1]), jnp.cumsum(z, axis=1)], axis=1)
    pos = start + jnp.arange(T, dtype=jnp.int32)
    end = cs[:, POOL_HIST + 1:]
    cur = z[:, POOL_HIST:]
    groups = []
    for g, w in enumerate(POOL_WINDOWS):
        sl = slice(g * POOL_GROUP, (g + 1) * POOL_GROUP)
        wsum = end[..., sl] - cs[:, POOL_HIST + 1 - w:POOL_HIST + 1 - w + T, sl]
        cnt = jnp.minimum(pos + 1, w).astype(jnp.float32)[None, :, None]
        groups.append(wsum / cnt - cur[..., sl])
    d = jnp.stack(groups, axis=2)
    y = jnp.einsum('btgc,gcd->btgd', d, w_pool_grp.astype(jnp.float32)).reshape(B, T, POOL_WIDTH)
    y = y * pool_scale.astype(jnp.float32)
    return y.astype(u.dtype), zc[:, -POOL_HIST:]

def mla_qkv(cq, ckv, kr, q_norm, kv_norm, w_q_up, start):
    q = jnp.einsum('btc,chd->bthd', rmsnorm(cq, q_norm), w_q_up)
    q_nope = q[..., :QK_NOPE]
    q_rope = rope(q[..., QK_NOPE:], start)
    c_kv = rmsnorm(ckv, kv_norm)
    k_rope = rope(kr, start)
    return q_nope, q_rope, c_kv, k_rope

def mla_prompt_attention(q_nope, q_rope, c_kv, k_rope, w_uk, w_uv):
    B, S = c_kv.shape[:2]
    k_nope = jnp.einsum('bsc,chd->bshd', c_kv, w_uk)
    v = jnp.einsum('bsc,chd->bshd', c_kv, w_uv)
    scale = (QK_NOPE + QK_ROPE) ** -0.5
    outs = []
    for i in range(S // ATTN_BLOCK):
        q0 = i * ATTN_BLOCK
        L = q0 + ATTN_BLOCK
        s = (jnp.einsum('bqhd,bkhd->bhqk', q_nope[:, q0:L], k_nope[:, :L])
             + jnp.einsum('bqhr,bkr->bhqk', q_rope[:, q0:L], k_rope[:, :L])).astype(jnp.float32) * scale
        qpos = q0 + jnp.arange(ATTN_BLOCK)
        kpos = jnp.arange(L)
        s = jnp.where(kpos[None, :] <= qpos[:, None], s, -jnp.inf)
        p = jax.nn.softmax(s, axis=-1).astype(v.dtype)
        outs.append(jnp.einsum('bhqk,bkhd->bqhd', p, v[:, :L]))
    return jnp.concatenate(outs, axis=1)

def mla_sample_attention(q_nope, q_rope, c_kv, k_rope, lat_past, kr_past, w_uk, w_uv):
    T = c_kv.shape[1]
    P = lat_past.shape[1]
    scale = (QK_NOPE + QK_ROPE) ** -0.5
    q_lat = jnp.einsum('bthd,chd->bthc', q_nope, w_uk)
    s_past = (jnp.einsum('bthc,bkc->bhtk', q_lat, lat_past)
              + jnp.einsum('bthr,bkr->bhtk', q_rope, kr_past)).astype(jnp.float32) * scale
    s_new = (jnp.einsum('bthc,bkc->bhtk', q_lat, c_kv)
             + jnp.einsum('bthr,bkr->bhtk', q_rope, k_rope)).astype(jnp.float32) * scale
    causal = jnp.arange(T)[None, :] <= jnp.arange(T)[:, None]
    s_new = jnp.where(causal, s_new, -jnp.inf)
    p = jax.nn.softmax(jnp.concatenate([s_past, s_new], axis=-1), axis=-1).astype(c_kv.dtype)
    o_lat = (jnp.einsum('bhtk,bkc->bthc', p[..., :P], lat_past)
             + jnp.einsum('bhtk,bkc->bthc', p[..., P:], c_kv))
    return jnp.einsum('bthc,chd->bthd', o_lat, w_uv)

def memory_kv(mem, mem_norm, w_mem_k, w_mem_v):
    mn = rmsnorm(mem, mem_norm)
    return (jnp.einsum('bmd,dhe->bmhe', mn, w_mem_k),
            jnp.einsum('bmd,dhe->bmhe', mn, w_mem_v))

def memory_attention(qx, mem_k, mem_v):
    B, T, _ = qx.shape
    q = qx.reshape(B, T, X_HEADS, X_HEAD_DIM)
    s = jnp.einsum('bthd,bmhd->bhtm', q, mem_k).astype(jnp.float32) * (X_HEAD_DIM ** -0.5)
    p = jax.nn.softmax(s, axis=-1).astype(mem_v.dtype)
    return jnp.einsum('bhtm,bmhd->bthd', p, mem_v).reshape(B, T, X_WIDTH)

def merge_branches(pool_y, mla_o, mem_o, gates, lp):
    B, T, _ = gates.shape
    g = jax.nn.sigmoid(gates.astype(jnp.float32)).reshape(B, T, N_BRANCH, D_MODEL).astype(pool_y.dtype)
    merged = (g[:, :, 0] * (pool_y @ lp['w_pool_out'])
              + g[:, :, 1] * (mla_o.reshape(B, T, MLA_HEADS * V_HEAD) @ lp['w_mla_out'])
              + g[:, :, 2] * (mem_o @ lp['w_x_out']))
    return merged @ lp['w_o']

def peer_ffn(h, lp):
    B, T, D = h.shape
    N = B * T
    hf = h.reshape(N, D)
    q = jnp.einsum('nd,dhc->nhc', hf, lp['w_peer_q'])
    s1 = jnp.einsum('nhc,kc->nhk', q[..., :PEER_HALF], lp['peer_k1']).astype(jnp.float32)
    s2 = jnp.einsum('nhc,kc->nhk', q[..., PEER_HALF:], lp['peer_k2']).astype(jnp.float32)
    v1, i1 = lax.top_k(s1, PEER_TOPK)
    v2, i2 = lax.top_k(s2, PEER_TOPK)
    cand = (v1[..., :, None] + v2[..., None, :]).reshape(N, PEER_HEADS, PEER_TOPK * PEER_TOPK)
    cidx = (i1[..., :, None] * N_KEYS + i2[..., None, :]).reshape(N, PEER_HEADS, PEER_TOPK * PEER_TOPK)
    sc, sel = lax.top_k(cand, PEER_TOPK)
    idx = jnp.take_along_axis(cidx, sel, axis=-1).reshape(N, PEER_HEADS * PEER_TOPK)
    gate = jax.nn.softmax(sc, axis=-1).reshape(N, PEER_HEADS * PEER_TOPK).astype(h.dtype)
    n_pad = (-N) % PEER_CHUNK
    nc = (N + n_pad) // PEER_CHUNK
    hp = jnp.pad(hf, ((0, n_pad), (0, 0))).reshape(nc, PEER_CHUNK, D)
    ip = jnp.pad(idx, ((0, n_pad), (0, 0))).reshape(nc, PEER_CHUNK, PEER_HEADS * PEER_TOPK)
    gp = jnp.pad(gate, ((0, n_pad), (0, 0))).reshape(nc, PEER_CHUNK, PEER_HEADS * PEER_TOPK)
    peer_u = lp['peer_u']
    peer_v = lp['peer_v']

    def chunk(args):
        hc, ic, gc = args
        a = jax.nn.gelu(jnp.einsum('cd,ckd->ck', hc, peer_u[ic]), approximate=False)
        return jnp.einsum('ck,ckd->cd', gc * a, peer_v[ic])

    out = lax.map(chunk, (hp, ip, gp))
    return out.reshape(nc * PEER_CHUNK, D)[:N].reshape(B, T, D)

def layer_prompt(x, mem, lp):
    xn = rmsnorm(x, lp['attn_norm'])
    u, cq, ckv, kr, qx, gates = split_projection(xn, lp['w_in'])
    hist0 = jnp.zeros((x.shape[0], POOL_HIST, POOL_WIDTH), u.dtype)
    pool_y, new_hist = pool_mix(u, hist0, 0, lp['w_pool_grp'], lp['pool_scale'])
    q_nope, q_rope, c_kv, k_rope = mla_qkv(cq, ckv, kr, lp['q_norm'], lp['kv_norm'], lp['w_q_up'], 0)
    mla_o = mla_prompt_attention(q_nope, q_rope, c_kv, k_rope, lp['w_uk'], lp['w_uv'])
    mem_k, mem_v = memory_kv(mem, lp['mem_norm'], lp['w_mem_k'], lp['w_mem_v'])
    mem_o = memory_attention(qx, mem_k, mem_v)
    h = x + merge_branches(pool_y, mla_o, mem_o, gates, lp)
    y = h + peer_ffn(rmsnorm(h, lp['ffn_norm']), lp)
    return y, c_kv, k_rope, new_hist, mem_k, mem_v

def layer_sample(x, lat_past, kr_past, hist, mem_k, mem_v, lp):
    xn = rmsnorm(x, lp['attn_norm'])
    u, cq, ckv, kr, qx, gates = split_projection(xn, lp['w_in'])
    pool_y, new_hist = pool_mix(u, hist, PAST_LEN, lp['w_pool_grp'], lp['pool_scale'])
    q_nope, q_rope, c_kv, k_rope = mla_qkv(cq, ckv, kr, lp['q_norm'], lp['kv_norm'], lp['w_q_up'], PAST_LEN)
    mla_o = mla_sample_attention(q_nope, q_rope, c_kv, k_rope, lat_past, kr_past, lp['w_uk'], lp['w_uv'])
    mem_o = memory_attention(qx, mem_k, mem_v)
    h = x + merge_branches(pool_y, mla_o, mem_o, gates, lp)
    y = h + peer_ffn(rmsnorm(h, lp['ffn_norm']), lp)
    return y, c_kv, k_rope, new_hist

def setup_inputs(seed: int = 0) -> dict:
    key = jax.random.key(seed)
    ks = iter(jax.random.split(key, 40))
    f32 = jnp.float32

    def nrm(shape, scale=1.0):
        return jax.random.normal(next(ks), shape, f32) * scale

    def gain(shape):
        return 1.0 + 0.02 * jax.random.normal(next(ks), shape, f32)

    n_pages = PAST_LEN // PAGE_SIZE
    n_used = DEC_BATCH * n_pages
    n_phys = n_used + n_used // 4
    x_prompt = nrm((BATCH, SEQ, D_MODEL))
    x_sample = nrm((DEC_BATCH, DEC_SEQ, D_MODEL))
    cache_kv_latent = nrm((DEPTH, n_phys, PAGE_SIZE, KV_LORA))
    cache_k_rope = nrm((DEPTH, n_phys, PAGE_SIZE, QK_ROPE))
    state_pool = nrm((DEPTH, DEC_BATCH, POOL_HIST, POOL_WIDTH))
    cache_mem_k = nrm((DEPTH, DEC_BATCH, N_MEM, X_HEADS, X_HEAD_DIM))
    cache_mem_v = nrm((DEPTH, DEC_BATCH, N_MEM, X_HEADS, X_HEAD_DIM))
    perm = jax.random.permutation(next(ks), n_phys)
    page_table = perm[:n_used].reshape(DEC_BATCH, n_pages).astype(jnp.int32)
    mem_prompt = nrm((BATCH, N_MEM, D_MODEL))
    return {
        'x_prompt': x_prompt,
        'x_sample': x_sample,
        'cache_kv_latent': cache_kv_latent,
        'cache_k_rope': cache_k_rope,
        'state_pool': state_pool,
        'cache_mem_k': cache_mem_k,
        'cache_mem_v': cache_mem_v,
        'page_table': page_table,
        'mem_prompt': mem_prompt,
        'attn_norm': gain((DEPTH, D_MODEL)),
        'w_in': nrm((DEPTH, D_MODEL, IN_WIDTH), D_MODEL ** -0.5),
        'q_norm': gain((DEPTH, Q_LORA)),
        'kv_norm': gain((DEPTH, KV_LORA)),
        'w_q_up': nrm((DEPTH, Q_LORA, MLA_HEADS, QK_NOPE + QK_ROPE), Q_LORA ** -0.5),
        'w_uk': nrm((DEPTH, KV_LORA, MLA_HEADS, QK_NOPE), KV_LORA ** -0.5),
        'w_uv': nrm((DEPTH, KV_LORA, MLA_HEADS, V_HEAD), KV_LORA ** -0.5),
        'w_pool_grp': nrm((DEPTH, len(POOL_WINDOWS), POOL_GROUP, POOL_GROUP), POOL_GROUP ** -0.5),
        'pool_scale': gain((DEPTH, POOL_WIDTH)),
        'mem_norm': gain((DEPTH, D_MODEL)),
        'w_mem_k': nrm((DEPTH, D_MODEL, X_HEADS, X_HEAD_DIM), D_MODEL ** -0.5),
        'w_mem_v': nrm((DEPTH, D_MODEL, X_HEADS, X_HEAD_DIM), D_MODEL ** -0.5),
        'w_pool_out': nrm((DEPTH, POOL_WIDTH, D_MODEL), POOL_WIDTH ** -0.5),
        'w_mla_out': nrm((DEPTH, MLA_HEADS * V_HEAD, D_MODEL), (MLA_HEADS * V_HEAD) ** -0.5),
        'w_x_out': nrm((DEPTH, X_WIDTH, D_MODEL), X_WIDTH ** -0.5),
        'w_o': nrm((DEPTH, D_MODEL, D_MODEL), D_MODEL ** -0.5),
        'ffn_norm': gain((DEPTH, D_MODEL)),
        'w_peer_q': nrm((DEPTH, D_MODEL, PEER_HEADS, PEER_QDIM), D_MODEL ** -0.5),
        'peer_k1': nrm((DEPTH, N_KEYS, PEER_HALF), PEER_HALF ** -0.5),
        'peer_k2': nrm((DEPTH, N_KEYS, PEER_HALF), PEER_HALF ** -0.5),
        'peer_u': nrm((DEPTH, N_EXPERTS, D_MODEL), D_MODEL ** -0.5),
        'peer_v': nrm((DEPTH, N_EXPERTS, D_MODEL), 0.25),
        'final_norm': gain((D_MODEL,)),
    }

def reference(x_prompt, x_sample, cache_kv_latent, cache_k_rope, state_pool, cache_mem_k, cache_mem_v,
              page_table, mem_prompt, attn_norm, w_in, q_norm, kv_norm, w_q_up, w_uk, w_uv, w_pool_grp,
              pool_scale, mem_norm, w_mem_k, w_mem_v, w_pool_out, w_mla_out, w_x_out, w_o, ffn_norm,
              w_peer_q, peer_k1, peer_k2, peer_u, peer_v, final_norm):
    n_pages = PAST_LEN // PAGE_SIZE
    yp, ys = x_prompt, x_sample
    lat_p, kr_p, pool_p, mk_p, mv_p = [], [], [], [], []
    lat_s, kr_s, pool_s = [], [], []
    for l in range(DEPTH):
        lp = dict(attn_norm=attn_norm[l], w_in=w_in[l], q_norm=q_norm[l], kv_norm=kv_norm[l],
                  w_q_up=w_q_up[l], w_uk=w_uk[l], w_uv=w_uv[l], w_pool_grp=w_pool_grp[l],
                  pool_scale=pool_scale[l], mem_norm=mem_norm[l], w_mem_k=w_mem_k[l], w_mem_v=w_mem_v[l],
                  w_pool_out=w_pool_out[l], w_mla_out=w_mla_out[l], w_x_out=w_x_out[l], w_o=w_o[l],
                  ffn_norm=ffn_norm[l], w_peer_q=w_peer_q[l], peer_k1=peer_k1[l], peer_k2=peer_k2[l],
                  peer_u=peer_u[l], peer_v=peer_v[l])
        yp, c_kv, k_rope, hist, mem_k, mem_v = layer_prompt(yp, mem_prompt, lp)
        lat_p.append(c_kv); kr_p.append(k_rope); pool_p.append(hist); mk_p.append(mem_k); mv_p.append(mem_v)
        lat_past = cache_kv_latent[l][page_table].reshape(DEC_BATCH, n_pages * PAGE_SIZE, KV_LORA)
        kr_past = cache_k_rope[l][page_table].reshape(DEC_BATCH, n_pages * PAGE_SIZE, QK_ROPE)
        ys, c_kv_s, k_rope_s, hist_s = layer_sample(ys, lat_past, kr_past, state_pool[l],
                                                    cache_mem_k[l], cache_mem_v[l], lp)
        lat_s.append(c_kv_s); kr_s.append(k_rope_s); pool_s.append(hist_s)
    y_prompt = rmsnorm(yp, final_norm)
    y_sample = rmsnorm(ys, final_norm)
    return (y_prompt, y_sample, jnp.stack(lat_p), jnp.stack(kr_p), jnp.stack(pool_p), jnp.stack(mk_p),
            jnp.stack(mv_p), jnp.stack(lat_s), jnp.stack(kr_s), jnp.stack(pool_s))


_drawn_inputs = setup_inputs


def setup_inputs(seed=0):
    import zlib

    import numpy as np

    out = dict(_drawn_inputs(seed))
    spreads = {}
    factors = {'cache_k_rope': 4.309,
     'attn_norm': 2.841,
     'q_norm': 8.0,
     'kv_norm': 2.987,
     'pool_scale': 11.564,
     'mem_norm': 8.369,
     'ffn_norm': 23.195,
     'final_norm': 8.398}
    for name, (base, spread) in spreads.items():
        noise = np.random.default_rng([zlib.crc32(name.encode()), seed]).standard_normal(out[name].shape)
        drawn = base * np.exp(spread * noise) if base else spread * noise
        out[name] = __import__('jax').numpy.asarray(drawn.astype(out[name].dtype))
    for name, factor in factors.items():
        out[name] = (out[name] * factor).astype(out[name].dtype)
    return out
```

```python
from contextlib import ExitStack

import concourse.bass as bass
from concourse import mybir
from concourse.bass import DynSlice, IndirectOffsetOnAxis

ALU = mybir.AluOpType
ACT = mybir.ActivationFunctionType
F32 = mybir.dt.float32
U32 = mybir.dt.uint32
AX_X = mybir.AxisListType.X

P = 128
D = 1024
DK = D // P
EPS = 1e-6
NS = 32
NB = 8
TS = 4
SEQ = 512
NT = NS + SEQ
HALF = NT // 2
TILES = 1 + SEQ // P
MEM = 256
HIST = 15
PG = 4
H = 8
NOPE, ROPE, VD = 64, 32, 64
QD = NOPE + ROPE
QL, KL = 384, 256
XH, XD = 4, 128
PAGES, PAGE = 16, 128
PGRP = 4
LATW = KL + ROPE
OFF_U, OFF_CQ, OFF_CKV, OFF_KR, OFF_QX, OFF_G = 0, 512, 896, 1152, 1184, 1696
EH, NKEY, TOPK = 8, 128, 16
ITS = 17
RING = 8
VCRED = 16 - RING
NEG = -3.0e38
MLA_SCALE = float(QD) ** -0.5
MEM_SCALE = float(XD) ** -0.5


def rows(t):
    return NS if t == 0 else P


def cols(t):
    return slice(0, NS) if t == 0 else slice(NS + (t - 1) * P, NS + t * P)


STREAM = [("qkv", 0, 256), ("qkv", 256, 256), ("qkv", 512, 160),
          ("u", 0, 256), ("u", 256, 256), ("qx", 0, 256), ("qx", 256, 256),
          ("mk", 0, 256), ("mk", 256, 256), ("mv", 0, 256), ("mv", 256, 256)]
WRING = 4


def stream_units():
    for j, (what, c, w) in enumerate(STREAM):
        if what == "qkv":
            for t in range(TILES):
                yield j, what, c, w, t
        elif what in ("u", "qx"):
            for f in range(w // P):
                for half in range(2):
                    yield j, what, c // P + f, f, half
        else:
            for m in range(2):
                yield j, what, c, w, m


UNITS = list(stream_units())
LAST_QKV = max(n for n, u in enumerate(UNITS) if u[1] == "qkv")
LAST_U = max(n for n, u in enumerate(UNITS) if u[1] == "u")
ATT = [("mla", q, h, P * (q + 1)) for q in range(4) for h in range(H)]
ATT += [("mem", q, h, MEM) for q in range(4) for h in range(XH)]


def att_groups():
    out = []
    for n, (kind, q, h, _) in enumerate(ATT):
        if h == 0:
            out.append([kind, q, n, n])
        out[-1][3] = n
    return out


GROUPS = att_groups()
GROUP_OF = {n: g for g, (_, _, a, b) in enumerate(GROUPS) for n in range(a, b + 1)}


def hybrid_step(nc, x_prompt, x_sample, cache_lat, cache_kr, state_pool, cache_mk, cache_mv, page_table,
                mem_prompt, attn_norm, w_in, q_norm, kv_norm, w_q_up, w_uk, w_uv, w_pool_grp, pool_scale,
                mem_norm, w_mem_k, w_mem_v, w_pool_out, w_mla_out, w_x_out, w_o, ffn_norm, w_peer_q,
                peer_k1, peer_k2, peer_u, peer_v, final_norm, c_ident, c_causal, c_smask, c_trig,
                c_cnt, c_iota, y_p, y_s, lat_p, kr_p, pool_p, mk_p, mv_p, lat_s, kr_s, pool_s):
    with ExitStack() as ctx:
        sem = lambda name: ctx.enter_context(nc.semaphore(name))
        ARENA = 207 * 1024
        arena = ctx.enter_context(nc.sbuf_tensor("arena", [P, ARENA // 4], F32))
        bank = ctx.enter_context(nc.psum_tensor("bank", [P, 8, 512], F32))

        def at(kb, shape, dt=F32):
            n = 1
            for s in shape:
                n *= s
            a = int(kb * 256)
            assert a == kb * 256 and a + n <= ARENA // 4, (kb, shape)
            v = arena[:, a:a + n]
            if dt != F32:
                v = v.bitcast(dt)
            if len(shape) > 1:
                names = "abcd"[:len(shape)]
                v = v.rearrange(f"p ({' '.join(names)}) -> p {' '.join(names)}",
                                **{n: s for n, s in zip(names, shape)})
            return v

        ident = at(0, [2, P])
        eye = ident[:, 1]
        causal = at(1, [P])
        smask = at(1.5, [NB, NS])
        trig = at(2.5, [TILES, 32])
        cntfix = at(3.25, [PG, 16])
        iota16 = at(3.5, [16])
        gattn = at(3.75, [DK])
        gmem = at(3.78125, [DK])
        gq = at(3.8125, [3])
        pscale = at(3.84375, [PG])
        ss = at(4, [16])
        std = at(4.0625, [16])
        rstd = at(4.125, [16])
        pagetab = at(4.25, [P], mybir.dt.int32)
        gkv = at(4.75, [KL])
        gfin = at(6, [D])
        gffn = at(10, [D])
        junk = at(14, [D])
        nmax, rsum, rinv, nmax0 = at(18, [64]), at(18.25, [64]), at(18.5, [64]), at(4.75 + 1, [64])
        smx, ssum, srec, smx0 = at(18.75, [16]), at(18.8125, [16]), at(18.875, [16]), at(18.9375, [16])
        mmx, mmx0, msum, mrec = at(19, [4]), at(19.015625, [4]), at(19.03125, [8]), at(19.0625, [4])
        eps = at(19.078125, [1])
        spare = at(19.09375, [8])
        unew = at(19.25, [PG, NS])
        xnT = at(20, [DK, NT])
        pyT = at(37, [4, NT])
        moT = at(45.5, [4, NT])
        xoT = at(54, [4, NT])
        qxT = at(62.5, [4, NT])
        qT = at(71, [H, NT])
        cT = at(88, [2, NT])
        krT = at(92.25, [NT])
        cqkv = at(94.5, [TILES, 672])
        wuk = at(107.75, [2, 512])
        wuv = at(111.75, [2, 512])
        wring = at(115.75, [WRING, DK, 256])
        mnT = at(147.75, [DK, MEM])
        wqup = at(155.75, [3, 768])
        xin = at(164.75, [3, D])
        krp = at(205, [TILES, 96])
        uP = at(178.75, [PG, HIST + SEQ])
        uS = at(187, [PG, NB, HIST + TS])
        hist = at(189.5, [512])
        uout = at(191.5, [2, 512])
        mkv = at(195.5, [2, 2, 512])
        rot_a, rot_b = at(203.5, [H, ROPE]), at(191.5, [H, ROPE])
        qnT = at(164.75, [3, NT])
        qtm = at(147.75, [2, 768])
        dT = at(155.75, [PG, NT])
        wpool = at(171.5, [PG, P])
        psum_a = at(115.75, [SEQ + HIST])
        psum_b = at(118, [SEQ + HIST])
        ssum_a = at(120.25, [NB, HIST + TS])
        ssum_b = at(121, [NB, HIST + TS])
        pages = at(115.75, [2 * 4, PGRP, LATW])
        wukT = at(153, [H, KL])
        qlat = at(161, [2, NB, H, TS])
        qrot = at(163, [NB, H, TS])
        latT = at(164, [2, 2, 512])
        krpT = at(172, [2, 512])
        scor = at(176, [2080])
        prob = at(184.25, [2080])
        probT = at(60, [17, NS])
        olat = at(203.5, [KL])
        olatT = at(62.5 - 8.5, [2, H, NB, TS])
        osmp = at(58, [512])
        smem = at(115.75, [2, 2, 2, 512])
        smT = at(131.75, [XH, MEM])
        sms = at(135.75, [XH, MEM])
        smpT = at(139.75, [XH, 2, TS])
        smo = at(140, [512])
        kT = at(142, [H, SEQ])
        vtm = at(158, [4, 512])
        mkT = at(166, [XH, MEM])
        prb = at(170, [3, 512])
        prbT = at(176, [2, 4, P])
        otm = at(180, [2, 512])
        wmg = at(62.5, [2, 3, 12, P])
        mgT = at(98.5, [DK, NT])
        sig = at(115.5, [2, 2, HALF])
        mtmp = at(119.75, [2, HALF])
        wo = at(122, [DK, D])
        hall = at(154, [TILES, D])
        hn = at(174, [TILES, D])
        hnT = at(20, [DK, NT])
        wpq = at(37, [4, DK, P])
        qp = at(53, [2, NT])
        keysT = at(57.5, [2, P])
        keys = at(58.5, [2, P])
        scores = at(60, [ITS, 4, NKEY])
        uring = at(98.5, [RING, D])
        vring = at(20, [RING, D])
        hA, hB = at(131, [D]), at(135, [D])
        diag = at(139, [16, P])
        sc = at(147, [4, NKEY])
        cand = at(149, [2, 256])
        onehot = at(151, [32, 16])
        val = at(153, [4, 16])
        vix = at(153.25, [4, 16], U32)
        vixf = at(153.5, [4, 16])
        top, top0 = at(153.75, [2, 16]), at(153.875, [2, 16])
        sel = at(52, [2, 16], U32)
        sela = at(52.125, [2, 16], U32)
        selb = at(52.25, [2, 16], U32)
        selaf = at(52.375, [2, 16])
        selbf = at(52.5, [2, 16])
        e1 = at(52.625, [2, 16])
        e2 = at(52.75, [2, 16])
        gexp = at(52.875, [2, 16])
        gs2 = at(53, [8])
        gr2 = at(53.125, [8])
        idN = at(53.25, [32], U32)
        idA = at(53.375, [32], U32)
        idB = at(53.5, [16], U32)
        gN = at(53.625, [32])
        gB = at(53.75, [16])
        act_a = at(53.875, [16])
        act_g = at(54, [16])
        wts = at(54.125, [16])
        trash = at(54.25, [D])
        outb = at(98.5, [2, D])

        ld_const, ld_gain, ld_w, ld_state = sem("ld_const"), sem("ld_gain"), sem("ld_w"), sem("ld_state")
        zeroed = sem("zeroed")
        ld_x = [sem(f"ld_x{i}") for i in range(3)]
        sqrt_done, xs_done, xT_mm, xT_ev = map(sem, ("sqrt_done", "xs_done", "xT_mm", "xT_ev"))
        ld_ring = [sem(f"ld_ring{i}") for i in range(WRING)]
        st_mm, st_ev = sem("st_mm"), sem("st_ev")
        rstd_read, q_sqrt, q_norm_done, kr_done, c_mm, c_ev_d, c_ev_a = map(
            sem, ("rstd_read", "q_sqrt", "q_norm_done", "kr_done", "c_mm", "c_ev_d", "c_ev_a"))
        qu_mm, qu_ev, qu_rope, qt_mm, qt_ev = map(sem, ("qu_mm", "qu_ev", "qu_rope", "qt_mm", "qt_ev"))
        hi_mm, hi_ev, uo_mm, uo_ev, pool_d, pool_mm, pool_ev = map(
            sem, ("hi_mm", "hi_ev", "uo_mm", "uo_ev", "pool_d", "pool_mm", "pool_ev"))
        ld_pool = sem("ld_pool")
        uk_mm, uk_ev, ql_mm, ql_ev = map(sem, ("uk_mm", "uk_ev", "ql_mm", "ql_ev"))
        ld_page = [sem(f"ld_page{i}") for i in range(8)]
        pt_mm, pt_ev, pt_ed, ps_mm, ps_ev, ps_max, ps_exp, pp_mm, pp_ev, pv_free, pv_mm, pv_ev, po_mm, po_ev = map(
            sem, ("pt_mm", "pt_ev", "pt_ed", "ps_mm", "ps_ev", "ps_max", "ps_exp", "pp_mm", "pp_ev", "pv_free",
                  "pv_mm", "pv_ev", "po_mm", "po_ev"))
        so_mm, so_ev, sot_mm, sot_ev = map(sem, ("so_mm", "so_ev", "sot_mm", "sot_ev"))
        ld_sm = [sem(f"ld_sm{i}") for i in range(2)]
        (mt_mm, mt_ev, ms_mm, ms_max, ms_exp, mp_mm, mp_ev, mo_mm, mo_ev, mx_mm, mx_ev) = map(
            sem, ("mt_mm", "mt_ev", "ms_mm", "ms_max", "ms_exp", "mp_mm", "mp_ev", "mo_mm", "mo_ev",
                  "mx_mm", "mx_ev"))
        kv_mm, kv_ev, krk_done = sem("kv_mm"), sem("kv_ev"), sem("krk_done")
        (at_mm, at_max, at_exp, at_tm, at_te, at_pv, at_oe, at_xm, at_xe) = map(
            sem, ("at_mm", "at_max", "at_exp", "at_tm", "at_te", "at_pv", "at_oe", "at_xm", "at_xe"))
        ld_mg = [sem(f"ld_mg{i}") for i in range(2)]
        mg_mm, mg_sig, mg_ev = sem("mg_mm"), sem("mg_sig"), sem("mg_ev")
        ld_wo, wo_mm, wo_ev = sem("ld_wo"), sem("wo_mm"), sem("wo_ev")
        hn_rep, h_sqrt, h_norm, hT_mm, hT_ev = map(sem, ("hn_rep", "h_sqrt", "h_norm", "hT_mm", "hT_ev"))
        ld_keys, key_mm, key_ev = sem("ld_keys"), sem("key_mm"), sem("key_ev")
        ld_pq = [sem(f"ld_pq{i}") for i in range(4)]
        pq_mm, pq_ev, sc_mm, sc_ev = map(sem, ("pq_mm", "pq_ev", "sc_mm", "sc_ev"))
        u_in = [sem(f"u_in{i}") for i in range(RING)]
        v_in = [sem(f"v_in{i}") for i in range(RING)]
        (tk_gap, tk_exp, id_next, id_a, id_b, g_b, gelu_done, w_done, diag_done, u_free, v_free,
         acc_free, h_a, h_b) = map(sem, (
            "tk_gap", "tk_exp", "id_next", "id_a", "id_b", "g_b", "gelu_done", "w_done", "diag_done",
            "u_free", "v_free", "acc_free", "h_a", "h_b"))
        f_sqrt, f_out = sem("f_sqrt"), sem("f_out")
        st_y = [sem("st_y0"), sem("st_y1")]
        stored, st_lat, st_pool = sem("stored"), sem("st_lat"), sem("st_pool")
        dve_chain, act_chain = sem("dve_chain"), sem("act_chain")
        carrier = sem("carrier")

        block = ctx.enter_context(nc.Block())

        @block.sync
        def _(sp):
            n_store = 0

            def store(dst, src):
                nonlocal n_store
                n_store += 1
                sp.dma_start(dst, src).then_inc(stored, 16)

            def load_x(i):
                if i >= 3:
                    sp.wait_ge(xT_mm, 2 * (i - 2))
                dst = xin[:, i % 3]
                if i == 0:
                    sp.dma_start(dst[0:NS], x_sample.rearrange("b t d -> (b t) d")).then_inc(ld_x[0], 16)
                elif i < TILES:
                    sp.dma_start(dst, x_prompt[0, (i - 1) * P:i * P]).then_inc(ld_x[i % 3], 16)
                else:
                    m = i - TILES
                    sp.dma_start(dst, mem_prompt[0, m * P:(m + 1) * P]).then_inc(ld_x[i % 3], 16)

            def load_stream(j):
                what, c, w = STREAM[j]
                if j >= WRING:
                    last = max(n for n, u in enumerate(UNITS) if u[0] == j - WRING)
                    sp.wait_ge(st_mm, last + 1)
                if what in ("qkv", "u", "qx"):
                    c += {"qkv": OFF_CQ, "u": OFF_U, "qx": OFF_QX}[what]
                    src = w_in[0][:, c:c + w]
                else:
                    src = (w_mem_k if what == "mk" else w_mem_v)[0].rearrange("d h e -> d (h e)")[:, c:c + w]
                sp.dma_start(wring[:, j % WRING, :, 0:w], src.rearrange("(k p) n -> p k n", p=P)).then_inc(
                    ld_ring[j % WRING], 16)

            sp.dma_start(ident[:], c_ident.rearrange("a p n -> p a n")).then_inc(ld_const, 16)
            sp.dma_start(gattn[:], attn_norm[0].rearrange("(k p) -> p k", p=P), allow_slow_non_contiguous=True).then_inc(ld_const, 16)
            sp.dma_start(gmem[:], mem_norm[0].rearrange("(k p) -> p k", p=P), allow_slow_non_contiguous=True).then_inc(ld_const, 16)
            for i in range(3):
                load_x(i)
            load_stream(0)
            load_stream(1)
            for i in range(3, 7):
                load_x(i)
                if i < 5:
                    load_stream(i - 1)
            sp.dma_start(causal[:], c_causal).then_inc(ld_gain, 16)
            sp.dma_start(smask[0:NS], c_smask).then_inc(ld_gain, 16)
            sp.dma_start(trig[:], c_trig).then_inc(ld_gain, 16)
            sp.dma_start(cntfix[:], c_cnt).then_inc(ld_gain, 16)
            sp.dma_start(iota16[:], c_iota).then_inc(ld_gain, 16)
            sp.dma_start(gq[:], q_norm[0].rearrange("(k p) -> p k", p=P), allow_slow_non_contiguous=True).then_inc(ld_gain, 16)
            sp.dma_start(pscale[:], pool_scale[0].rearrange("(k p) -> p k", p=P), allow_slow_non_contiguous=True).then_inc(ld_gain, 16)
            sp.dma_start(gkv[:], kv_norm.to_broadcast([P, KL])).then_inc(ld_gain, 16)
            sp.dma_start(gffn[:], ffn_norm.to_broadcast([P, D])).then_inc(ld_gain, 16)
            sp.dma_start(gfin[:], final_norm.rearrange("(a d) -> a d", a=1).to_broadcast([P, D])).then_inc(ld_gain, 16)
            sp.dma_start(pagetab[0:1], page_table.rearrange("(a b) n -> a (b n)", a=1)).then_inc(ld_gain, 16)
            sp.dma_start(hist[0:NB * HIST], state_pool[0].rearrange("b t c -> (b t) c")).then_inc(ld_state, 16)
            store(pool_s[0][:, 0:HIST - TS], state_pool[0][:, TS:HIST])
            sp.dma_start(wqup[:], w_q_up[0].rearrange("(k p) h e -> p k (h e)", p=P)).then_inc(ld_w, 16)
            sp.dma_start(wuk[:], w_uk[0].rearrange("(k p) h e -> p k (h e)", p=P)).then_inc(ld_w, 16)
            sp.dma_start(wuv[:], w_uv[0].rearrange("(k p) h e -> p k (h e)", p=P)).then_inc(ld_w, 16)
            for j in range(4, len(STREAM)):
                load_stream(j)
            sp.wait_ge(st_ev, len(UNITS))
            for k, dst in enumerate((mk_p, mv_p)):
                store(dst[0, 0].rearrange("(m p) h e -> p m (h e)", p=P), mkv[:, k])
            sp.wait_ge(q_norm_done, 10)
            sp.wait_ge(kr_done, 1)
            for dst, src in ((lat_s[0].rearrange("b t c -> (b t) c"), cqkv[0:NS, 0, QL:QL + KL]),
                             (lat_p[0, 0].rearrange("(t p) c -> p t c", p=P), cqkv[:, 1:, QL:QL + KL]),
                             (kr_s[0].rearrange("b t c -> (b t) c"), krp[0:NS, 0, NOPE:QD]),
                             (kr_p[0, 0].rearrange("(t p) c -> p t c", p=P), krp[:, 1:, NOPE:QD])):
                sp.dma_start(dst, src).then_inc(st_lat, 16)
            sp.wait_ge(qu_mm, 2 * TILES)
            sp.dma_start(wpool[:], w_pool_grp[0].rearrange("g c d -> c g d")).then_inc(ld_pool, 16)
            sp.wait_ge(uo_ev, 2)
            for b in range(NB):
                sp.dma_start(pool_s[0, b, HIST - TS:HIST], uout[b * TS:(b + 1) * TS, 0]).then_inc(st_pool, 16)
            sp.dma_start(pool_p[0, 0], uout[0:HIST, 1]).then_inc(st_pool, 16)
            sp.wait_ge(pool_d, PG)
            sp.wait_ge(qt_mm, 2 * TILES)

            def load_group(b, g):
                s = (b % 2) * 4 + g
                if b >= 2:
                    sp.wait_ge(pv_free, 4 * (b - 2) + g + 1)
                for k in range(PGRP):
                    n = b * PAGES + g * PGRP + k
                    page = sp.value_load(pagetab[0:1, n:n + 1], min_val=0, max_val=cache_lat.shape[1] - 1)
                    sp.dma_start(pages[:, s, k, 0:KL],
                                 cache_lat[0][DynSlice(page, 1)].rearrange("a p c -> (a p) c")).then_inc(ld_page[s], 16)
                    sp.dma_start(pages[:, s, k, KL:LATW],
                                 cache_kr[0][DynSlice(page, 1)].rearrange("a p c -> (a p) c")).then_inc(ld_page[s], 16)

            sp.wait_ge(ld_gain, 16 * 11)
            for b in range(NB):
                for g in range(4):
                    load_group(b, g)
            sp.wait_ge(pv_mm, NB)
            for b in range(NB):
                if b >= 2:
                    sp.wait_ge(mo_mm, b - 1)
                    sp.wait_ge(mt_mm, 2 * (b - 1))
                for k, src in enumerate((cache_mk, cache_mv)):
                    sp.dma_start(smem[:, b % 2, k], src[0, b].rearrange("(m p) h e -> p m (h e)", p=P)).then_inc(
                        ld_sm[b % 2], 16)
            def load_merge(f):
                if f >= 2:
                    sp.wait_ge(mg_mm, 3 * (f - 1))
                for i, wout in enumerate((w_pool_out, w_mla_out, w_x_out)):
                    c = OFF_G + i * D + f * P
                    sp.dma_start(wmg[:, f % 2, i, 0:8], w_in[0][:, c:c + P].rearrange("(k p) n -> p k n", p=P)).then_inc(
                        ld_mg[f % 2], 16)
                    sp.dma_start(wmg[:, f % 2, i, 8:12],
                                 wout[0][:, f * P:(f + 1) * P].rearrange("(k p) n -> p k n", p=P)).then_inc(
                        ld_mg[f % 2], 16)

            sp.wait_ge(at_mm, len(ATT))
            sp.wait_ge(at_pv, len(ATT))
            sp.wait_ge(at_xm, len(GROUPS))
            sp.wait_ge(st_lat, 16 * 4)
            load_merge(0)
            load_merge(1)
            sp.dma_start(wo[:], w_o[0].rearrange("(k p) n -> p k n", p=P)).then_inc(ld_wo, 16)
            sp.dma_start(hall[0:NS, 0], x_sample.rearrange("b t d -> (b t) d")).then_inc(ld_wo, 16)
            sp.dma_start(hall[:, 1:], x_prompt[0].rearrange("(t p) d -> p t d", p=P)).then_inc(ld_wo, 16)
            for f in range(2, DK):
                load_merge(f)
            sp.wait_ge(mg_mm, 3 * DK)
            sp.dma_start(keys[:, 0], peer_k1[0]).then_inc(ld_keys, 16)
            sp.dma_start(keys[:, 1], peer_k2[0]).then_inc(ld_keys, 16)
            wq = w_peer_q[0].rearrange("(k p) h (a c) -> p k (h a) c", p=P, a=2)
            for j in range(16):
                if j >= 4:
                    sp.wait_ge(pq_mm, j - 3)
                sp.dma_start(wpq[:, j % 4], wq[:, :, j]).then_inc(ld_pq[j % 4], 16)
            for t in range(TILES):
                sp.wait_ge(f_out, t + 1)
                dst = y_s.rearrange("b t d -> (b t) d") if t == 0 else y_p[0, (t - 1) * P:t * P]
                sp.dma_start(dst, outb[0:rows(t), t % 2]).then_inc(st_y[t % 2], 16)
            sp.wait_ge(st_y[0], 48)
            sp.wait_ge(st_y[1], 32)
            sp.wait_ge(st_pool, 16 * (NB + 1))
            sp.wait_ge(st_lat, 16 * 4)
            sp.wait_ge(stored, 16 * n_store)

        @block.gpsimd
        def _(pool):
            pool.memset(ss[:], 1.0).then_inc(zeroed, 1)
            pool.memset(cqkv[:, 0], 0.0).then_inc(zeroed, 1)
            pool.memset(krp[:], 0.0).then_inc(zeroed, 1)
            pool.memset(uP[:, :, 0:HIST], 0.0).then_inc(zeroed, 1)
            pool.memset(eps[:], EPS).then_inc(zeroed, 1)
            pool.memset(spare[:, 0:1], 0.0).then_inc(u_free, RING)
            pool.memset(spare[:, 1:2], 0.0).then_inc(v_free, 16)
            pool.memset(spare[:, 2:3], 0.0).then_inc(acc_free, 2)

            def gather(ring, land, k, table, ix):
                pool.sem_inc(carrier, 1)
                pool.indirect_dma_start(out=ring[:, k % RING], out_offset=None, in_=table[0],
                                        in_offset=IndirectOffsetOnAxis(ap=ix, axis=0)).then_inc(land[k % RING], 16)

            pool.wait_ge(id_next, 1)
            for k in range(16):
                pool.wait_ge(u_free, k + 1)
                gather(uring, u_in, k, peer_u, idN[:, k:k + 1])

            def half_1(it):
                pool.wait_ge(id_a, it + 1)
                for k in range(16):
                    pool.wait_ge(u_free, it * 32 + (16 + k + 1))
                    gather(uring, u_in, k, peer_u, idA[:, 16 + k:17 + k])
                    pool.wait_ge(v_free, it * 32 + (k + 1 + VCRED))
                    gather(vring, v_in, k, peer_v, idA[:, k:k + 1])

            def half_2(it, last):
                pool.wait_ge(id_b, it + 1)
                if not last:
                    pool.wait_ge(id_next, it + 2)
                for k in range(16):
                    if not last:
                        pool.wait_ge(u_free, it * 32 + (32 + k + 1))
                        gather(uring, u_in, k, peer_u, idN[:, k:k + 1])
                    pool.wait_ge(v_free, it * 32 + (16 + k + 1 + VCRED))
                    gather(vring, v_in, k, peer_v, idB[:, k:k + 1])

            with nc.gpsimd.Fori(0, ITS - 1) as it:
                half_1(it)
                half_2(it, False)
            half_1(ITS - 1)
            half_2(ITS - 1, True)

        @block.tensor
        def _(pe):
            def turn(dst, src, n):
                return pe.transpose(dst, src, eye[0:n, 0:n])

            def sum_k(dst, lhs, rhs, n):
                for k in range(n):
                    last = pe.matmul(dst, lhs(k), rhs(k), start=(k == 0), stop=(k == n - 1))
                return last

            pe.wait_ge(ld_const, 48)
            def turn_x(i):
                r = NS if i == 0 else P
                pe.wait_ge(xs_done, i + 1)
                for c in range(2):
                    n = 2 * i + c
                    if n >= 4:
                        pe.wait_ge(xT_ev, n - 3)
                    for k in range(4):
                        last = turn(bank[:, n % 4, k * P:k * P + r],
                                    xin[0:r, i % 3, (4 * c + k) * P:(4 * c + k + 1) * P], r)
                    last.then_inc(xT_mm, 1)

            def stream(n):
                j, what, c, w, m = UNITS[n]
                if n == 0 or UNITS[n - 1][0] != j:
                    pe.wait_ge(ld_ring[j % WRING], 16 * (j // WRING + 1))
                if n >= 4:
                    pe.wait_ge(st_ev, n - 3)
                b = 4 + n % 4
                wt = wring[:, j % WRING]
                if what == "qkv":
                    pe.wait_ge(xT_ev, 2 * (m + 1))
                    last = sum_k(bank[0:rows(m), b, 0:w], lambda k: xnT[:, k, cols(m)], lambda k: wt[:, k, 0:w], DK)
                elif what in ("u", "qx"):
                    last = sum_k(bank[:, b, 0:HALF], lambda k: wt[:, k, w * P:(w + 1) * P],
                                 lambda k: xnT[:, k, m * HALF:(m + 1) * HALF], DK)
                else:
                    last = sum_k(bank[:, b, 0:w], lambda k: mnT[:, k, m * P:(m + 1) * P], lambda k: wt[:, k, 0:w], DK)
                last.then_inc(st_mm, 1)

            for i in range(5):
                turn_x(i)
                stream(i)
            turn_x(5)
            for n in range(5, 10):
                stream(n)
            turn_x(6)
            pe.wait_ge(xT_ev, 14)
            for n in range(10, LAST_U + 1):
                stream(n)
            def turn_c(t):
                r = rows(t)
                pe.wait_ge(q_norm_done, 2 * (t + 1))
                pe.wait_ge(kr_done, 1)
                b = 2 * (t % 2)
                if t >= 2:
                    pe.wait_ge(c_ev_d, t - 1)
                    pe.wait_ge(c_ev_a, t - 1)
                for k in range(3):
                    last = turn(bank[:, b, k * P:k * P + r], cqkv[0:r, t, k * P:(k + 1) * P], r)
                last.then_inc(c_mm, 1)
                for k in range(2):
                    turn(bank[:, b + 1, k * P:k * P + r], cqkv[0:r, t, QL + k * P:QL + (k + 1) * P], r)
                turn(bank[0:QD, b + 1, 2 * P:2 * P + r], krp[0:r, t], r).then_inc(c_mm, 1)

            rest = list(range(LAST_U + 1, len(UNITS)))
            for t in range(TILES):
                stream(rest[t])
                turn_c(t)
            for n in rest[TILES:]:
                stream(n)
            pe.wait_ge(ld_w, 48)
            pe.wait_ge(st_ev, len(UNITS))
            pe.wait_ge(c_ev_d, TILES)
            pe.wait_ge(c_ev_a, TILES)
            for t in range(TILES + 1):
                if t < TILES:
                    for c in range(2):
                        n = 2 * t + c
                        if n >= 4:
                            pe.wait_ge(qu_ev, n - 3)
                        sum_k(bank[0:rows(t), 4 + n % 4, 0:384], lambda k: qnT[:, k, cols(t)],
                              lambda k: wqup[:, k, c * 384:(c + 1) * 384], 3).then_inc(qu_mm, 1)
                if t >= 1:
                    pe.wait_ge(qu_rope, t)
                    r = rows(t - 1)
                    for c in range(2):
                        n = 2 * (t - 1) + c
                        if n >= 4:
                            pe.wait_ge(qt_ev, n - 3)
                        for k in range(4):
                            h = 4 * c + k
                            last = turn(bank[0:QD, n % 4, k * P:k * P + r],
                                        qtm[0:r, (t - 1) % 2, h * QD:(h + 1) * QD], r)
                        last.then_inc(qt_mm, 1)
            pe.wait_ge(ld_state, 16)
            pe.wait_ge(qt_ev, 2 * TILES)
            for g in range(PG):
                last = turn(bank[:, 0, g * P:g * P + NB * HIST], hist[0:NB * HIST, g * P:(g + 1) * P], NB * HIST)
            last.then_inc(hi_mm, 1)
            for g in range(PG):
                last = turn(bank[0:NS, 1, g * P:(g + 1) * P], unew[:, g], P)
            last.then_inc(uo_mm, 1)
            for g in range(PG):
                last = turn(bank[0:HIST, 2, g * P:(g + 1) * P], uP[:, g, SEQ:SEQ + HIST], P)
            last.then_inc(uo_mm, 1)
            pe.wait_ge(hi_ev, 1)
            pe.wait_ge(uo_ev, 2)
            pe.wait_ge(ld_pool, 16)
            pe.wait_ge(qu_ev, 2 * TILES)
            for n in range(2 * PG):
                g, half = n // 2, n % 2
                pe.wait_ge(pool_d, g + 1)
                if n >= 4:
                    pe.wait_ge(pool_ev, n - 3)
                pe.matmul(bank[:, 4 + n % 4, 0:HALF], wpool[:, g], dT[:, g, half * HALF:(half + 1) * HALF],
                          start=True, stop=True).then_inc(pool_mm, 1)
            for n in range(4):
                for i in range(4):
                    h, c = 2 * n + i // 2, i % 2
                    last = turn(bank[0:NOPE, n, i * P:(i + 1) * P], wuk[:, c, h * NOPE:(h + 1) * NOPE], P)
                last.then_inc(uk_mm, 1)
            pe.wait_ge(pool_ev, 2 * PG)
            pe.wait_ge(uk_ev, 4)
            for h in range(H):
                for c in range(2):
                    last = pe.matmul(bank[:, 4, (h * 2 + c) * NS:(h * 2 + c + 1) * NS],
                                     wukT[0:NOPE, h, c * P:(c + 1) * P], qT[0:NOPE, h, 0:NS], start=True, stop=True)
            last.then_inc(ql_mm, 1)

            def page_turns(b, g):
                n = 4 * b + g
                pe.wait_ge(ld_page[n % 8], 16 * 8 * (b // 2 + 1))
                if n >= 1:
                    pe.wait_ge(pt_ev, n)
                    pe.wait_ge(pt_ed, 2 * n)
                for c in range(2):
                    for k in range(PGRP):
                        last = turn(bank[:, c, k * P:(k + 1) * P], pages[:, n % 8, k, c * P:(c + 1) * P], P)
                    last.then_inc(pt_mm, 1)
                for k in range(PGRP):
                    last = turn(bank[0:QD, 2, k * P:(k + 1) * P], pages[:, n % 8, k, LATW - QD:LATW], P)
                last.then_inc(pt_mm, 1)

            def page_scores(b, g):
                n, m = 4 * b + g, 5 * b + g
                if g < 4:
                    pe.wait_ge(pt_ev, n + 1)
                    pe.wait_ge(pt_ed, 2 * (n + 1))
                if m >= 2:
                    pe.wait_ge(ps_ev, m - 1)
                w = 512 if g < 4 else NS
                dst = bank[0:NS, 3 + m % 2, 0:w]
                kc = (lambda c: latT[:, n % 2, c]) if g < 4 else (lambda c: cT[:, c, 0:NS])
                kr = krpT[NOPE:QD, n % 2] if g < 4 else krT[NOPE:QD, 0:NS]
                for c in range(2):
                    pe.matmul(dst, qlat[:, c, b].rearrange("p h t -> p (h t)"), kc(c), start=(c == 0), stop=False)
                pe.matmul(dst, qrot[NOPE:QD, b].rearrange("p h t -> p (h t)"), kr, start=False,
                          stop=True).then_inc(ps_mm, 1)

            def page_values(b):
                pe.wait_ge(ps_exp, b + 1)
                if b >= 1:
                    pe.wait_ge(pp_ev, 2 * b)
                    pe.wait_ge(po_ev, b)
                for k in range(PAGES):
                    last = turn(bank[:, 5, k * NS:(k + 1) * NS], prob[0:NS, k * P:(k + 1) * P], NS)
                last.then_inc(pp_mm, 1)
                turn(bank[0:NS, 6, 0:NS], prob[0:NS, PAGES * P:PAGES * P + NS], NS).then_inc(pp_mm, 1)
                pe.wait_ge(pp_ev, 2 * (b + 1))
                if b >= 1:
                    pe.wait_ge(pv_ev, b)
                for k in range(PAGES):
                    s = (b % 2) * 4 + k // PGRP
                    last = pe.matmul(bank[0:NS, 7, 0:KL], probT[:, k], pages[:, s, k % PGRP, 0:KL],
                                     start=(k == 0), stop=False)
                    if k % PGRP == PGRP - 1:
                        last.then_inc(pv_free, 1)
                pe.matmul(bank[0:NS, 7, 0:KL], probT[0:NS, PAGES], cqkv[0:NS, 0, QL:QL + KL], start=False,
                          stop=True).then_inc(pv_mm, 1)
                pe.wait_ge(pv_ev, b + 1)
                for c in range(2):
                    last = turn(bank[:, 6, 64 + c * NS:64 + (c + 1) * NS], olat[0:NS, c * P:(c + 1) * P], NS)
                last.then_inc(po_mm, 1)

            pe.wait_ge(ql_ev, 3)
            for b in range(NB + 1):
                if b < NB:
                    for g in range(4):
                        page_turns(b, g)
                        if g >= 1:
                            page_scores(b, g - 1)
                    page_scores(b, 3)
                    page_scores(b, 4)
                if b >= 1:
                    page_values(b - 1)
            pe.wait_ge(po_ev, NB)
            pe.wait_ge(ps_ev, 5 * NB)
            for h in range(H):
                for c in range(2):
                    last = pe.matmul(bank[0:NS, 3, h * VD:(h + 1) * VD], olatT[:, c, h].rearrange("p b t -> p (b t)"),
                                     wuv[:, c, h * VD:(h + 1) * VD], start=(c == 0), stop=(c == 1))
            last.then_inc(so_mm, 1)
            pe.wait_ge(so_ev, 1)
            for c in range(4):
                last = turn(bank[:, 4, c * NS:(c + 1) * NS], osmp[0:NS, c * P:(c + 1) * P], NS)
            last.then_inc(sot_mm, 1)

            pe.wait_ge(pt_ev, 4 * NB)
            pe.wait_ge(pt_ed, 8 * NB)
            for b in range(NB + 1):
                if b < NB:
                    pe.wait_ge(ld_sm[b % 2], 32 * (b // 2 + 1))
                    if b >= 1:
                        pe.wait_ge(mt_ev, 2 * b)
                    for i in range(2):
                        for k in range(4):
                            h, m = 2 * i + k // 2, k % 2
                            last = turn(bank[:, i, k * P:(k + 1) * P], smem[:, b % 2, 0, m, h * XD:(h + 1) * XD], P)
                        last.then_inc(mt_mm, 1)
                if b >= 1:
                    pe.wait_ge(ms_exp, XH * b)
                    if b >= 2:
                        pe.wait_ge(mp_ev, b - 1)
                    for h in range(XH):
                        for m in range(2):
                            last = turn(bank[:, 5, (h * 2 + m) * TS:(h * 2 + m + 1) * TS],
                                        sms[0:TS, h, m * P:(m + 1) * P], TS)
                    last.then_inc(mp_mm, 1)
                if b < NB:
                    pe.wait_ge(mt_ev, 2 * (b + 1))
                    for h in range(XH):
                        last = pe.matmul(bank[0:TS, 2 + h // 2, (h % 2) * MEM:(h % 2 + 1) * MEM],
                                         qxT[:, h, b * TS:(b + 1) * TS], smT[:, h], start=True, stop=True)
                    last.then_inc(ms_mm, 1)
                if b >= 1:
                    pe.wait_ge(mp_ev, b)
                    if b >= 2:
                        pe.wait_ge(mo_ev, b - 1)
                    for h in range(XH):
                        for m in range(2):
                            last = pe.matmul(bank[0:TS, 6, h * XD:(h + 1) * XD], smpT[:, h, m],
                                             smem[:, (b - 1) % 2, 1, m, h * XD:(h + 1) * XD],
                                             start=(m == 0), stop=(m == 1))
                    last.then_inc(mo_mm, 1)
                    pe.wait_ge(mo_ev, b)
                    if b >= 2:
                        pe.wait_ge(mx_ev, b - 1)
                    for c in range(4):
                        last = turn(bank[:, 7, c * TS:(c + 1) * TS], smo[0:TS, c * P:(c + 1) * P], TS)
                    last.then_inc(mx_mm, 1)

            pe.wait_ge(mx_ev, NB)
            pe.wait_ge(sot_ev, 1)
            for n in range(14):
                if n >= 8:
                    pe.wait_ge(kv_ev, n - 7)
                b = n % 8
                if n < 2:
                    for k in range(4):
                        h, m = 2 * n + k // 2, k % 2
                        last = turn(bank[:, b, k * P:(k + 1) * P], mkv[:, 0, m, h * XD:(h + 1) * XD], P)
                elif n < 10:
                    h = n - 2
                    last = sum_k(bank[0:NOPE, b], lambda k: wuk[:, k, h * NOPE:(h + 1) * NOPE],
                                 lambda k: cT[:, k, NS:NT], 2)
                else:
                    t = n - 10
                    last = sum_k(bank[:, b], lambda k: cT[:, k, cols(t + 1)], lambda k: wuv[:, k], 2)
                last.then_inc(kv_mm, 1)

            def att_scores(u):
                kind, q, h, L = ATT[u]
                if u >= 3:
                    pe.wait_ge(at_exp, u - 2)
                dst = bank[:, u % 3, 0:L]
                if kind == "mla":
                    pe.matmul(dst, qT[0:QD, h, cols(q + 1)], kT[0:QD, h, 0:L], start=True, stop=True).then_inc(at_mm, 1)
                else:
                    pe.matmul(dst, qxT[:, h, cols(q + 1)], mkT[:, h], start=True, stop=True).then_inc(at_mm, 1)

            def att_turn(u):
                L = ATT[u][3]
                pe.wait_ge(at_exp, u + 1)
                if u >= 2:
                    pe.wait_ge(at_te, u - 1)
                for k in range(L // P):
                    last = turn(bank[:, 3 + u % 2, k * P:(k + 1) * P], prb[:, u % 3, k * P:(k + 1) * P], P)
                last.then_inc(at_tm, 1)

            def att_values(u):
                kind, q, h, L = ATT[u]
                g = GROUP_OF[u]
                pe.wait_ge(at_te, u + 1)
                if h == 0 and g >= 2:
                    pe.wait_ge(at_oe, g - 1)
                if kind == "mla":
                    last = sum_k(bank[:, 5 + g % 2, h * VD:(h + 1) * VD], lambda k: prbT[:, u % 2, k],
                                 lambda k: vtm[:, k, h * VD:(h + 1) * VD], L // P)
                else:
                    last = sum_k(bank[:, 5 + g % 2, h * XD:(h + 1) * XD], lambda k: prbT[:, u % 2, k],
                                 lambda k: mkv[:, 1, k, h * XD:(h + 1) * XD], L // P)
                last.then_inc(at_pv, 1)

            def att_out(g):
                pe.wait_ge(at_oe, g + 1)
                if g >= 1:
                    pe.wait_ge(at_xe, g)
                for c in range(4):
                    last = turn(bank[:, 7, c * P:(c + 1) * P], otm[:, g % 2, c * P:(c + 1) * P], P)
                last.then_inc(at_xm, 1)

            pe.wait_ge(kv_ev, 14)
            pe.wait_ge(krk_done, 1)
            for u in range(len(ATT) + 4):
                if u < len(ATT):
                    att_scores(u)
                if 1 <= u <= len(ATT):
                    att_turn(u - 1)
                if 2 <= u <= len(ATT) + 1:
                    att_values(u - 2)
                for g, (_, _, _, end) in enumerate(GROUPS):
                    if u - 4 + 1 == end + 1:
                        att_out(g)

            pe.wait_ge(at_xe, len(GROUPS))
            for n in range(3 * DK):
                f, i = n // 3, n % 3
                if i == 0:
                    pe.wait_ge(ld_mg[f % 2], 16 * 6 * (f // 2 + 1))
                if n >= 2:
                    pe.wait_ge(mg_ev, n - 1)
                src = (pyT, moT, xoT)[i]
                for half in range(2):
                    span = slice(half * HALF, (half + 1) * HALF)
                    sum_k(bank[:, 4 * (n % 2) + half, 0:HALF], lambda k: wmg[:, f % 2, i, k],
                          lambda k: xnT[:, k, span], DK)
                for half in range(2):
                    span = slice(half * HALF, (half + 1) * HALF)
                    last = sum_k(bank[:, 4 * (n % 2) + 2 + half, 0:HALF], lambda k: wmg[:, f % 2, i, 8 + k],
                                 lambda k: src[:, k, span], 4)
                last.then_inc(mg_mm, 1)
            pe.wait_ge(mg_ev, 3 * DK)
            pe.wait_ge(ld_wo, 48)
            for t in range(TILES + 1):
                if t < TILES:
                    for c in range(2):
                        n = 2 * t + c
                        if n >= 4:
                            pe.wait_ge(wo_ev, n - 3)
                        sum_k(bank[0:rows(t), n % 4], lambda k: mgT[:, k, cols(t)],
                              lambda k: wo[:, k, c * 512:(c + 1) * 512], DK).then_inc(wo_mm, 1)
                if t >= 1:
                    r = rows(t - 1)
                    pe.wait_ge(h_norm, t)
                    for c in range(2):
                        n = 2 * (t - 1) + c
                        if n >= 4:
                            pe.wait_ge(hT_ev, n - 3)
                        for k in range(4):
                            last = turn(bank[:, 4 + n % 4, k * P:k * P + r],
                                        hn[0:r, t - 1, (4 * c + k) * P:(4 * c + k + 1) * P], r)
                        last.then_inc(hT_mm, 1)
            pe.wait_ge(ld_keys, 32)
            pe.wait_ge(wo_ev, 2 * TILES)
            for a in range(2):
                last = turn(bank[:, 0, a * P:(a + 1) * P], keys[:, a], P)
            last.then_inc(key_mm, 1)
            pe.wait_ge(key_ev, 1)
            pe.wait_ge(hT_ev, 2 * TILES)
            for j in range(17):
                if j < 16:
                    pe.wait_ge(ld_pq[j % 4], 16 * (j // 4 + 1))
                    if j >= 2:
                        pe.wait_ge(pq_ev, j - 1)
                    for half in range(2):
                        last = sum_k(bank[:, 2 * (j % 2) + half, 0:HALF], lambda k: wpq[:, j % 4, k],
                                     lambda k: hnT[:, k, half * HALF:(half + 1) * HALF], DK)
                    last.then_inc(pq_mm, 1)
                if j >= 1:
                    i = j - 1
                    pe.wait_ge(pq_ev, i + 1)
                    if i >= 2:
                        pe.wait_ge(sc_ev, i - 1)
                    for t in range(1, TILES):
                        pe.matmul(bank[:, 4 + 2 * (i % 2), (t - 1) * P:t * P], qp[:, i % 2, cols(t)],
                                  keysT[:, i % 2], start=True, stop=True)
                    pe.matmul(bank[0:NS, 5 + 2 * (i % 2), 0:P], qp[:, i % 2, 0:NS], keysT[:, i % 2],
                              start=True, stop=True).then_inc(sc_mm, 1)

            def weigh(it, b):
                pe.wait_ge(acc_free, it * 2 + (b + 1))
                for k in range(16):
                    pe.wait_ge(diag_done, it * 32 + (16 * b + k + 1))
                    pe.wait_ge(v_in[k % RING], it * 64 + 16 * (2 * b + k // RING + 1))
                    for c in range(2):
                        last = pe.matmul(bank[:, 2 * b + c], diag[:, k], vring[:, k % RING, c * 512:(c + 1) * 512],
                                         start=(k == 0), stop=(k == 15))
                    last.then_inc(v_free, 1)

            with nc.tensor.Fori(0, ITS) as it:
                weigh(it, 0)
                weigh(it, 1)

        @block.scalar
        def _(act):
            chain = 0

            def link(ins):
                nonlocal chain
                chain += 1
                ins.then_inc(act_chain, 1)
                act.wait_ge(act_chain, chain)

            def copy(dst, src, scale=1.0):
                return act.activation(dst, src, ACT.Copy, scale=scale)

            def root_mean(r, col, src, width):
                link(act.activation(junk[0:r, 0:width], src, ACT.Square, accum_out=ss[0:r, col:col + 1]))
                return act.activation(std[0:r, col:col + 1], ss[0:r, col:col + 1], ACT.Sqrt, scale=1.0 / width,
                                      bias=eps[0:r])

            act.wait_ge(zeroed, 5)

            def squares(i):
                act.wait_ge(ld_x[i % 3], 16 * (i // 3 + 1))
                r = NS if i == 0 else P
                root_mean(r, i, xin[0:r, i % 3], D).then_inc(sqrt_done, 1)

            def stream_out(n):
                j, what, c, w, m = UNITS[n]
                act.wait_ge(st_mm, n + 1)
                b = 4 + n % 4
                if what == "qkv":
                    last = copy(cqkv[0:rows(m), m, c:c + w], bank[0:rows(m), b, 0:w])
                elif what == "qx":
                    last = copy(qxT[:, c, m * HALF:(m + 1) * HALF], bank[:, b, 0:HALF])
                elif what == "u":
                    if m == 0:
                        copy(uS[:, c, :, HIST:HIST + TS], bank[:, b, 0:NS].rearrange("p (b t) -> p b t", t=TS))
                        copy(unew[:, c], bank[:, b, 0:NS])
                        last = copy(uP[:, c, HIST:HIST + HALF - NS], bank[:, b, NS:HALF])
                    else:
                        last = copy(uP[:, c, HIST + HALF - NS:HIST + SEQ], bank[:, b, 0:HALF])
                else:
                    last = copy(mkv[:, 0 if what == "mk" else 1, m, c:c + w], bank[:, b, 0:w])
                last.then_inc(st_ev, 1)

            for i in range(3):
                squares(i)
            for i in range(3, 7):
                squares(i)
                stream_out(i - 3)
            for n in range(4, LAST_QKV + 1):
                stream_out(n)
            act.wait_ge(st_ev, LAST_QKV + 1)
            for t in range(TILES):
                root_mean(rows(t), 0, cqkv[0:rows(t), t, 0:QL], QL).then_inc(q_sqrt, 1)
                act.wait_ge(q_sqrt, 2 * t + 1)
                act.wait_ge(rstd_read, 2 * t + 1)
                root_mean(rows(t), 0, cqkv[0:rows(t), t, QL:QL + KL], KL).then_inc(q_sqrt, 1)
                act.wait_ge(rstd_read, 2 * t + 2)
            for n in range(LAST_QKV + 1, LAST_U + 1):
                stream_out(n)

            def out_c(t):
                r = rows(t)
                act.wait_ge(c_mm, 2 * (t + 1))
                b = 2 * (t % 2) + 1
                copy(cT[:, :, cols(t)], bank[:, b, 0:2 * P].rearrange("p (k r) -> p k r", k=2)[:, :, 0:r])
                copy(krT[NOPE:QD, cols(t)], bank[NOPE:QD, b, 2 * P:2 * P + r]).then_inc(c_ev_a, 1)

            rest = list(range(LAST_U + 1, len(UNITS)))
            for t in range(TILES):
                stream_out(rest[t])
                out_c(t)
            for n in rest[TILES:]:
                stream_out(n)
            for t in range(TILES + 1):
                if t < TILES:
                    r = rows(t)
                    if t >= 2:
                        act.wait_ge(qt_mm, 2 * (t - 1))
                    for c in range(2):
                        n = 2 * t + c
                        act.wait_ge(qu_mm, n + 1)
                        copy(qtm[0:r, t % 2, c * 384:(c + 1) * 384], bank[0:r, 4 + n % 4, 0:384]).then_inc(qu_ev, 1)
                if t >= 1:
                    r = rows(t - 1)
                    for c in range(2):
                        n = 2 * (t - 1) + c
                        act.wait_ge(qt_mm, n + 1)
                        copy(qT[0:QD, 4 * c:4 * c + 4, cols(t - 1)],
                             bank[0:QD, n % 4].rearrange("p (k r) -> p k r", k=4)[:, :, 0:r]).then_inc(qt_ev, 1)
            act.wait_ge(hi_mm, 1)
            for g in range(PG):
                last = copy(uS[:, g, :, 0:HIST], bank[:, 0, g * P:g * P + NB * HIST].rearrange("p (b t) -> p b t", b=NB))
            last.then_inc(hi_ev, 1)
            for n in range(2 * PG):
                act.wait_ge(pool_mm, n + 1)
                act.activation(pyT[:, n // 2, (n % 2) * HALF:(n % 2 + 1) * HALF], bank[:, 4 + n % 4, 0:HALF], ACT.Copy,
                               scale=pscale[:, n // 2:n // 2 + 1]).then_inc(pool_ev, 1)
            for n in range(4):
                act.wait_ge(uk_mm, n + 1)
                copy(wukT[0:NOPE, 2 * n:2 * n + 2].rearrange("p a b -> p (a b)"), bank[0:NOPE, n]).then_inc(uk_ev, 1)
            act.wait_ge(ql_mm, 1)
            for c in range(2):
                src = bank[:, 4].rearrange("p (h c b t) -> p c b h t", h=H, c=2, b=NB)[:, c]
                copy(qlat[:, c], src).then_inc(ql_ev, 1)

            def turn_out(n):
                act.wait_ge(pt_mm, 3 * n + 1)
                if n >= 2:
                    act.wait_ge(ps_mm, 5 * ((n - 2) // 4) + (n - 2) % 4 + 1)
                copy(latT[:, n % 2, 0], bank[:, 0]).then_inc(pt_ev, 1)

            def score_out(b, g):
                m = 5 * b + g
                act.wait_ge(ps_mm, m + 1)
                w = 512 if g < 4 else NS
                copy(scor[0:NS, g * 512:g * 512 + w], bank[0:NS, 3 + m % 2, 0:w]).then_inc(ps_ev, 1)

            act.wait_ge(st_pool, 16 * (NB + 1))
            for b in range(NB):
                for g in range(4):
                    turn_out(4 * b + g)
                    if g >= 1:
                        score_out(b, g - 1)
                score_out(b, 3)
                score_out(b, 4)
                act.wait_ge(ps_max, b + 1)
                if b >= 1:
                    act.wait_ge(pp_mm, 2 * b)
                act.activation(prob[0:NS], scor[0:NS], ACT.Exp, scale=MLA_SCALE, bias=smx[0:NS, b:b + 1],
                               accum_out=ssum[0:NS, b:b + 1]).then_inc(ps_exp, 1)
            act.wait_ge(sot_mm, 1)
            copy(moT[:, :, 0:NS], bank[:, 4, 0:4 * NS].rearrange("p (c n) -> p c n", c=4)).then_inc(sot_ev, 1)

            for b in range(NB + 1):
                if b < NB:
                    if b >= 1:
                        act.wait_ge(ms_mm, b)
                    for i in range(2):
                        act.wait_ge(mt_mm, 2 * b + i + 1)
                        copy(smT[:, 2 * i:2 * i + 2].rearrange("p a b -> p (a b)"), bank[:, i]).then_inc(mt_ev, 1)
                    act.wait_ge(ms_max, b + 1)
                    if b >= 1:
                        act.wait_ge(mp_mm, b)
                    for h in range(XH):
                        act.activation(sms[0:TS, h], bank[0:TS, 2 + h // 2, (h % 2) * MEM:(h % 2 + 1) * MEM], ACT.Exp,
                                       scale=MEM_SCALE, bias=mmx[0:TS, h:h + 1],
                                       accum_out=msum[0:TS, 4 * (b % 2) + h:4 * (b % 2) + h + 1]).then_inc(ms_exp, 1)
                if b >= 1:
                    act.wait_ge(mx_mm, b)
                    copy(xoT[:, :, (b - 1) * TS:b * TS], bank[:, 7, 0:4 * TS].rearrange("p (c n) -> p c n", c=4)).then_inc(
                        mx_ev, 1)

            for n in range(14):
                act.wait_ge(kv_mm, n + 1)
                if n < 2:
                    dst, r = mkT[:, 2 * n:2 * n + 2].rearrange("p a b -> p (a b)"), P
                elif n < 10:
                    dst, r = kT[0:NOPE, n - 2], NOPE
                else:
                    dst, r = vtm[:, n - 10], P
                copy(dst, bank[0:r, n % 8]).then_inc(kv_ev, 1)

            for u in range(len(ATT) + 5):
                if u < len(ATT):
                    kind, q, h, L = ATT[u]
                    act.wait_ge(at_max, u + 1)
                    if u >= 3:
                        act.wait_ge(at_tm, u - 2)
                    act.activation(prb[:, u % 3, 0:L], bank[:, u % 3, 0:L], ACT.Exp,
                                   scale=MLA_SCALE if kind == "mla" else MEM_SCALE, bias=nmax[:, u:u + 1],
                                   accum_out=rsum[:, u:u + 1]).then_inc(at_exp, 1)
                if 1 <= u <= len(ATT):
                    L = ATT[u - 1][3]
                    act.wait_ge(at_tm, u)
                    if u >= 3:
                        act.wait_ge(at_pv, u - 2)
                    copy(prbT[:, (u - 1) % 2, 0:L // P].rearrange("p a b -> p (a b)"),
                         bank[:, 3 + (u - 1) % 2, 0:L]).then_inc(at_te, 1)
                for g, (kind, q, _, end) in enumerate(GROUPS):
                    if u - 4 == end + 1:
                        act.wait_ge(at_xm, g + 1)
                        dst = moT if kind == "mla" else xoT
                        copy(dst[:, :, cols(q + 1)], bank[:, 7].rearrange("p (c n) -> p c n", c=4)).then_inc(at_xe, 1)

            for n in range(3 * DK):
                act.wait_ge(mg_mm, n + 1)
                if n >= 2:
                    act.wait_ge(mg_ev, n - 1)
                b = 4 * (n % 2)
                act.activation(sig[:, n % 2], bank[:, b:b + 2, 0:HALF], ACT.Sigmoid).then_inc(mg_sig, 1)

            for t in range(TILES + 1):
                if t < TILES:
                    act.wait_ge(wo_ev, 2 * (t + 1))
                    if t >= 1:
                        act.wait_ge(h_norm, t)
                    root_mean(rows(t), 0, hall[0:rows(t), t], D).then_inc(h_sqrt, 1)
                if t >= 1:
                    r = rows(t - 1)
                    for c in range(2):
                        n = 2 * (t - 1) + c
                        act.wait_ge(hT_mm, n + 1)
                        copy(hnT[:, 4 * c:4 * c + 4, cols(t - 1)],
                             bank[:, 4 + n % 4].rearrange("p (k r) -> p k r", k=4)[:, :, 0:r]).then_inc(hT_ev, 1)
            act.wait_ge(key_mm, 1)
            copy(keysT.rearrange("p a b -> p (a b)"), bank[:, 0, 0:2 * P]).then_inc(key_ev, 1)
            for j in range(16):
                act.wait_ge(pq_mm, j + 1)
                if j >= 2:
                    act.wait_ge(sc_mm, j - 1)
                copy(qp[:, j % 2].rearrange("p (a b) -> p a b", a=2),
                     bank[:, 2 * (j % 2):2 * (j % 2) + 2, 0:HALF]).then_inc(pq_ev, 1)

            def picked_exp(n):
                act.wait_ge(tk_gap, n)
                act.activation(gexp[:], top[:], ACT.Exp).then_inc(tk_exp, 1)

            def diagonals(it, b, lag):
                act.wait_ge(w_done, it * 2 + (b + 1))
                for k in range(16):
                    act.wait_ge(v_free, it * 32 + (16 * b + k + 1))
                    act.sem_inc(carrier, 1)
                    act.activation(diag[:, k], ident[:, DynSlice((it + 15) // 16, 1)], ACT.Copy,
                                   scale=wts[:, k:k + 1]).then_inc(diag_done, 1)

            def tile_copy(dst, it, done):
                act.sem_inc(carrier, 1)
                act.activation(dst, hn[:, DynSlice((it + 4) // 4, 1)].rearrange("p a d -> p (a d)"), ACT.Copy).then_inc(done, 1)

            act.wait_ge(hn_rep, 1)
            copy(hA[:], hn[:, 0]).then_inc(h_a, 1)
            copy(hB[:], hn[:, 0]).then_inc(h_b, 1)
            picked_exp(1)
            act.wait_ge(u_free, RING + 16)
            act.activation(act_g[:], act_a[:], ACT.Gelu).then_inc(gelu_done, 1)
            with nc.scalar.Fori(0, ITS - 1) as it:
                diagonals(it, 0, 0)
                tile_copy(hA[:], it, h_a)
                picked_exp(it + 2)
                act.wait_ge(u_free, it * 32 + (RING + 32))
                act.activation(act_g[:], act_a[:], ACT.Gelu).then_inc(gelu_done, 1)
                diagonals(it, 1, 0)
                tile_copy(hB[:], it, h_b)
                act.wait_ge(u_free, it * 32 + (RING + 48))
                act.activation(act_g[:], act_a[:], ACT.Gelu).then_inc(gelu_done, 1)
            last = ITS - 1
            diagonals(last, 0, 0)
            act.wait_ge(u_free, last * 32 + (RING + 32))
            act.activation(act_g[:], act_a[:], ACT.Gelu).then_inc(gelu_done, 1)
            diagonals(last, 1, 0)
            for t in range(TILES):
                act.wait_ge(acc_free, 2 + 2 * ITS)
                if t >= 1:
                    act.wait_ge(f_out, t)
                root_mean(rows(t), 0, hall[0:rows(t), t], D).then_inc(f_sqrt, 1)

        @block.vector
        def _(dve):
            chain = 0

            def link(ins):
                nonlocal chain
                chain += 1
                ins.then_inc(dve_chain, 1)
                dve.wait_ge(dve_chain, chain)

            tt, ts, stt = dve.tensor_tensor, dve.tensor_scalar, dve.scalar_tensor_tensor

            dve.wait_ge(zeroed, 5)
            dve.wait_ge(ld_const, 48)

            def scale_x(i):
                r = NS if i == 0 else P
                dve.wait_ge(sqrt_done, i + 1)
                link(dve.reciprocal(rstd[0:r, i:i + 1], std[0:r, i:i + 1]))
                ts(xin[0:r, i % 3], xin[0:r, i % 3], rstd[0:r, i:i + 1], None, ALU.mult).then_inc(xs_done, 1)

            def out_x(i):
                r = NS if i == 0 else P
                for c in range(2):
                    n = 2 * i + c
                    dve.wait_ge(xT_mm, n + 1)
                    src = bank[:, n % 4].rearrange("p (k r) -> p k r", k=4)[:, :, 0:r]
                    g = (gattn if i < TILES else gmem)[:, 4 * c:4 * c + 4].unsqueeze(2).to_broadcast([P, 4, r])
                    dst = xnT[:, 4 * c:4 * c + 4, cols(i)] if i < TILES else \
                        mnT[:, 4 * c:4 * c + 4, (i - TILES) * P:(i - TILES + 1) * P]
                    tt(dst, src, g, ALU.mult).then_inc(xT_ev, 1)

            for i in range(8):
                if i < 7:
                    scale_x(i)
                if i >= 1:
                    out_x(i - 1)

            dve.wait_ge(ld_gain, 16 * 11)
            for t in range(TILES):
                r = rows(t)
                dve.wait_ge(q_sqrt, 2 * t + 1)
                dve.reciprocal(rstd[0:r, 0:1], std[0:r, 0:1]).then_inc(rstd_read, 1)
                dve.wait_ge(rstd_read, 2 * t + 1)
                ts(cqkv[0:r, t, 0:QL], cqkv[0:r, t, 0:QL], rstd[0:r, 0:1], None, ALU.mult).then_inc(q_norm_done, 1)
                dve.wait_ge(q_sqrt, 2 * t + 2)
                dve.reciprocal(rstd[0:r, 1:2], std[0:r, 0:1]).then_inc(rstd_read, 1)
                dve.wait_ge(rstd_read, 2 * t + 2)
                stt(cqkv[0:r, t, QL:QL + KL], cqkv[0:r, t, QL:QL + KL], rstd[0:r, 1:2], gkv[0:r], ALU.mult,
                    ALU.mult).then_inc(q_norm_done, 1)

            def rope(dst, src, cos, sin, ta, tb):
                half = ROPE // 2
                x1, x2 = src[..., 0:half], src[..., half:ROPE]
                tt(ta[..., 0:half], x1, cos, ALU.mult)
                tt(ta[..., half:ROPE], x2, cos, ALU.mult)
                tt(tb[..., 0:half], x2, sin, ALU.mult)
                link(tt(tb[..., half:ROPE], x1, sin, ALU.mult))
                tt(dst[..., 0:half], ta[..., 0:half], tb[..., 0:half], ALU.subtract)
                return tt(dst[..., half:ROPE], ta[..., half:ROPE], tb[..., half:ROPE], ALU.add)

            rope(krp[:, :, NOPE:QD], cqkv[:, :, QL + KL:QL + KL + ROPE], trig[:, :, 0:16], trig[:, :, 16:32],
                 rot_a[:, 0:TILES], rot_b[:, 0:TILES]).then_inc(kr_done, 1)
            for t in range(TILES):
                r = rows(t)
                dve.wait_ge(c_mm, 2 * t + 1)
                src = bank[:, 2 * (t % 2), 0:3 * P].rearrange("p (k r) -> p k r", k=3)[:, :, 0:r]
                tt(qnT[:, :, cols(t)], src, gq.unsqueeze(2).to_broadcast([P, 3, r]), ALU.mult).then_inc(c_ev_d, 1)
            for t in range(TILES):
                r = rows(t)
                dve.wait_ge(qu_ev, 2 * (t + 1))
                q = qtm[0:r, t % 2].rearrange("p (h e) -> p h e", h=H)[:, :, NOPE:QD]
                cs = [trig[0:r, t, 16 * k:16 * k + 16].unsqueeze(1).to_broadcast([r, H, 16]) for k in range(2)]
                dve.wait_ge(*((qu_rope, t) if t else (kr_done, 1)))
                rope(q, q, cs[0], cs[1], rot_a[0:r], rot_b[0:r]).then_inc(qu_rope, 1)
            for k, r in enumerate((NS, HIST)):
                dve.wait_ge(uo_mm, k + 1)
                dve.tensor_copy(uout[0:r, k], bank[0:r, 1 + k]).then_inc(uo_ev, 1)
            dve.wait_ge(hi_ev, 1)
            dve.wait_ge(st_mm, len(UNITS))
            dve.wait_ge(qu_mm, 2 * TILES)
            for g in range(PG):
                n, w = HIST + SEQ, 2 << g
                sP, sS = uP[:, g], uS[:, g]
                if g:
                    dve.wait_ge(pool_d, g)
                for step in range(g + 1):
                    sh = 1 << step
                    lo = 2 * sh - 1
                    dP, dS = ((psum_a, ssum_a), (psum_b, ssum_b))[step % 2]
                    tt(dP[:, lo:n], sP[:, lo:n], sP[:, lo - sh:n - sh], ALU.add)
                    link(tt(dS[:, :, lo:], sS[:, :, lo:], sS[:, :, lo - sh:HIST + TS - sh], ALU.add))
                    sP, sS = dP, dS
                link(tt(sP[:, HIST:HIST + 16], sP[:, HIST:HIST + 16], cntfix[:, g], ALU.mult))
                stt(dT[:, g, NS:NT], sP[:, HIST:n], 1.0 / w, uP[:, g, HIST:n], ALU.mult, ALU.subtract)
                stt(dT[:, g, 0:NS].rearrange("p (b t) -> p b t", b=NB), sS[:, :, HIST:], 1.0 / w,
                    uS[:, g, :, HIST:], ALU.mult, ALU.subtract).then_inc(pool_d, 1)
            dve.wait_ge(qt_ev, 2 * TILES)
            dve.wait_ge(c_ev_a, TILES)
            dve.wait_ge(pool_mm, 2 * PG)
            dve.tensor_copy(qrot[NOPE:QD], qT[NOPE:QD, :, 0:NS].rearrange("p h (b t) -> p b h t", b=NB)).then_inc(ql_ev, 1)

            dve.wait_ge(st_pool, 16 * (NB + 1))
            for b in range(NB + 1):
                if b < NB:
                    for g in range(4):
                        n = 4 * b + g
                        dve.wait_ge(pt_mm, 3 * n + 2)
                        if n >= 2:
                            dve.wait_ge(ps_mm, 5 * ((n - 2) // 4) + (n - 2) % 4 + 1)
                        dve.tensor_copy(latT[:, n % 2, 1], bank[:, 1]).then_inc(pt_ed, 1)
                        dve.wait_ge(pt_mm, 3 * n + 3)
                        dve.tensor_copy(krpT[NOPE:QD, n % 2], bank[NOPE:QD, 2]).then_inc(pt_ed, 1)
                    dve.wait_ge(ps_ev, 5 * (b + 1))
                    new = scor[0:NS, PAGES * PAGE:PAGES * PAGE + NS]
                    link(tt(new, new, smask[0:NS, b], ALU.add))
                    link(dve.reduce_max(smx0[0:NS, b:b + 1], scor[0:NS], AX_X))
                    ts(smx[0:NS, b:b + 1], smx0[0:NS, b:b + 1], -MLA_SCALE, None, ALU.mult).then_inc(ps_max, 1)
                if b >= 1:
                    a = b - 1
                    dve.wait_ge(pp_mm, 2 * a + 1)
                    if a >= 1:
                        dve.wait_ge(pv_mm, a)
                    dve.tensor_copy(probT[:, 0:PAGES].rearrange("p a b -> p (a b)"), bank[:, 5]).then_inc(pp_ev, 1)
                    dve.wait_ge(pp_mm, 2 * a + 2)
                    dve.tensor_copy(probT[0:NS, PAGES], bank[0:NS, 6, 0:NS]).then_inc(pp_ev, 1)
                    link(dve.reciprocal(srec[0:NS, a:a + 1], ssum[0:NS, a:a + 1]))
                    dve.wait_ge(pv_mm, a + 1)
                    ts(olat[0:NS], bank[0:NS, 7, 0:KL], srec[0:NS, a:a + 1], None, ALU.mult).then_inc(pv_ev, 1)
                    dve.wait_ge(po_mm, a + 1)
                    dve.tensor_copy(olatT[:, :, :, a], bank[:, 6, 64:64 + 2 * NS].rearrange(
                        "p (c h t) -> p c h t", c=2, h=H)).then_inc(po_ev, 1)
            dve.wait_ge(so_mm, 1)
            dve.tensor_copy(osmp[0:NS], bank[0:NS, 3]).then_inc(so_ev, 1)

            for b in range(NB + 1):
                if b < NB:
                    dve.wait_ge(ms_mm, b + 1)
                    link(dve.reduce_max(mmx0[0:TS], bank[0:TS, 2:4].rearrange("p a (h m) -> p (a h) m", h=2), AX_X))
                    if b >= 1:
                        dve.wait_ge(ms_exp, XH * b)
                    ts(mmx[0:TS], mmx0[0:TS], -MEM_SCALE, None, ALU.mult).then_inc(ms_max, 1)
                if b >= 1:
                    dve.wait_ge(mp_mm, b)
                    if b >= 2:
                        dve.wait_ge(mo_mm, b - 1)
                    dve.tensor_copy(smpT.rearrange("p h m t -> p (h m t)"), bank[:, 5, 0:XH * 2 * TS]).then_inc(mp_ev, 1)
                    s = 4 * ((b - 1) % 2)
                    link(dve.reciprocal(mrec[0:TS], msum[0:TS, s:s + 4]))
                    dve.wait_ge(mo_mm, b)
                    if b >= 2:
                        dve.wait_ge(mx_mm, b - 1)
                    tt(smo[0:TS].rearrange("p (h e) -> p h e", h=XH), bank[0:TS, 6].rearrange("p (h e) -> p h e", h=XH),
                       mrec[0:TS].unsqueeze(2).to_broadcast([TS, XH, XD]), ALU.mult).then_inc(mo_ev, 1)

            dve.wait_ge(kv_mm, 2)
            dve.tensor_copy(kT[NOPE:QD], krT[NOPE:QD, NS:NT].unsqueeze(1).to_broadcast([ROPE, H, SEQ])).then_inc(krk_done, 1)

            for u in range(len(ATT) + 3):
                if u < len(ATT):
                    kind, q, h, L = ATT[u]
                    dve.wait_ge(at_mm, u + 1)
                    if kind == "mla":
                        d = bank[:, u % 3, L - P:L]
                        link(tt(d, d, causal[:], ALU.add))
                    link(dve.reduce_max(nmax0[:, u:u + 1], bank[:, u % 3, 0:L], AX_X))
                    ts(nmax[:, u:u + 1], nmax0[:, u:u + 1], -(MLA_SCALE if kind == "mla" else MEM_SCALE), None,
                       ALU.mult).then_inc(at_max, 1)
                for g, (kind, q, first, end) in enumerate(GROUPS):
                    if u - 3 == end:
                        n = end - first + 1
                        dve.wait_ge(at_exp, end + 1)
                        link(dve.reciprocal(rinv[:, first:end + 1], rsum[:, first:end + 1]))
                        dve.wait_ge(at_pv, end + 1)
                        if g >= 2:
                            dve.wait_ge(at_xm, g - 1)
                        tt(otm[:, g % 2].rearrange("p (h e) -> p h e", h=n),
                           bank[:, 5 + g % 2].rearrange("p (h e) -> p h e", h=n),
                           rinv[:, first:end + 1].unsqueeze(2).to_broadcast([P, n, 512 // n]), ALU.mult).then_inc(at_oe, 1)

            for n in range(3 * DK):
                f, i = n // 3, n % 3
                dve.wait_ge(mg_sig, n + 1)
                b = 4 * (n % 2) + 2
                out = mgT[:, f].rearrange("p (a b) -> p a b", a=2)
                if i == 0:
                    if f == 0:
                        dve.wait_ge(st_lat, 16 * 4)
                    tt(out, sig[:, n % 2], bank[:, b:b + 2, 0:HALF], ALU.mult).then_inc(mg_ev, 1)
                    dve.wait_ge(mg_ev, n + 1)
                else:
                    link(tt(mtmp[:], sig[:, n % 2], bank[:, b:b + 2, 0:HALF], ALU.mult))
                    tt(out, out, mtmp[:], ALU.add).then_inc(mg_ev, 1)
                    dve.wait_ge(mg_ev, n + 1)
            dve.wait_ge(ld_wo, 48)
            for q in range(1, 4):
                dve.memset(hall[32 * q:32 * q + 32, 0], 0.0)
            for t in range(TILES + 1):
                if t < TILES:
                    r = rows(t)
                    for c in range(2):
                        n = 2 * t + c
                        dve.wait_ge(wo_mm, n + 1)
                        part = hall[0:r, t, c * 512:(c + 1) * 512]
                        tt(part, part, bank[0:r, n % 4], ALU.add).then_inc(wo_ev, 1)
                if t >= 1:
                    r = rows(t - 1)
                    dve.wait_ge(h_sqrt, t)
                    link(dve.reciprocal(rstd[0:r, t:t + 1], std[0:r, 0:1]))
                    stt(hn[0:r, t - 1], hall[0:r, t - 1], rstd[0:r, t:t + 1], gffn[0:r], ALU.mult, ALU.mult).then_inc(
                        h_norm, 1)
            dve.wait_ge(h_norm, 1)
            for q in range(1, 4):
                last = dve.tensor_copy(hn[32 * q:32 * q + 32, 0], hn[0:32, 0])
            last.then_inc(hn_rep, 1)
            for j in range(16):
                pair, s = j // 4, j % 4
                b = 4 + 2 * (j % 2)
                dve.wait_ge(sc_mm, j + 1)
                dve.tensor_copy(scores[:, 1 + pair:ITS:4, s], bank[:, b].rearrange("p (t k) -> p t k", t=4))
                dve.tensor_copy(scores[32 * pair:32 * pair + 32, 0, s], bank[0:NS, b + 1, 0:P]).then_inc(sc_ev, 1)

            def step(ins):
                dve.drain()

            def top16(values, indices, source):
                step(dve.max(values[:, 0:8], source))
                step(dve.max_index(indices[:, 0:8], values[:, 0:8], source))
                step(dve.match_replace(source, values[:, 0:8], source, NEG))
                step(dve.max(values[:, 8:16], source))
                step(dve.max_index(indices[:, 8:16], values[:, 8:16], source))

            def pick(n, at_step):
                step(dve.tensor_copy(sc.rearrange("p a b -> p (a b)"),
                                     scores[:, DynSlice(at_step, 1)].rearrange("p x a b -> p (x a b)")))
                for q in range(4):
                    top16(val[:, q], vix[:, q], sc[:, q])
                step(dve.tensor_copy(vixf[:], vix[:]))
                for h in range(2):
                    step(tt(cand[:, h].rearrange("p (a b) -> p a b", a=16), val[:, 2 * h].unsqueeze(2).to_broadcast([P, 16, 16]),
                            val[:, 2 * h + 1].unsqueeze(1).to_broadcast([P, 16, 16]), ALU.add))
                for h in range(2):
                    top16(top0[:, h], sel[:, h], cand[:, h])
                tt(top[:], top0[:], top0[:, :, 0:1].to_broadcast([P, 2, 16]), ALU.subtract).then_inc(tk_gap, 1)
                ts(sela[:], sel[:], 4, None, ALU.logical_shift_right)
                step(ts(selb[:], sel[:], 15, None, ALU.bitwise_and))
                dve.tensor_copy(selaf[:], sela[:])
                step(dve.tensor_copy(selbf[:], selb[:]))
                for side, pos, dst in ((0, selaf, e1), (1, selbf, e2)):
                    step(tt(onehot[:], pos.rearrange("p a b -> p (a b)").unsqueeze(2).to_broadcast([P, 32, 16]),
                            iota16.unsqueeze(1).to_broadcast([P, 32, 16]), ALU.is_equal))
                    for h in range(2):
                        part = onehot[:, 16 * h:16 * h + 16]
                        last = tt(part, part, vixf[:, 2 * h + side].unsqueeze(1).to_broadcast([P, 16, 16]), ALU.mult)
                    step(last)
                    step(dve.reduce_sum(dst.rearrange("p a b -> p (a b)"), onehot[:], AX_X))
                stt(idN[:].rearrange("p (a b) -> p a b", a=2), e1[:], float(NKEY), e2[:], ALU.mult, ALU.add).then_inc(id_next, 1)
                dve.wait_ge(tk_exp, n)
                step(dve.reduce_sum(gs2[:, 0:2], gexp[:], AX_X))
                step(dve.reciprocal(gr2[:, 0:2], gs2[:, 0:2]))
                step(tt(gN.rearrange("p (a b) -> p a b", a=2), gexp[:], gr2[:, 0:2].unsqueeze(2).to_broadcast([P, 2, 16]),
                        ALU.mult))

            def products(row0, land0, h, ready, n):
                dve.wait_ge(ready, n)
                for k in range(16):
                    dve.wait_ge(u_in[k % RING], land0 + 16 * (k // RING + 1))
                    dve.tensor_tensor_reduce(uring[:, k % RING], uring[:, k % RING], h[:], 1.0, 0.0, ALU.mult, ALU.add,
                                             act_a[:, k:k + 1]).then_inc(u_free, 1)

            def weights(n, diags, gates):
                dve.wait_ge(gelu_done, n)
                if diags is not None:
                    dve.wait_ge(diag_done, diags)
                tt(wts[:], act_g[:], gates, ALU.mult).then_inc(w_done, 1)

            def add_sum(it, b):
                dve.wait_ge(v_free, it * 32 + 16 * (b + 2))
                dve.wait_ge(acc_free, it * 2 + (b + 2))
                y = hall[:, DynSlice((it + 3) // 4, 1)].rearrange("p a d -> p (a d)")
                tt(y, y, bank[:, 2 * b:2 * b + 2].rearrange("p a b -> p (a b)"), ALU.add).then_inc(acc_free, 1)

            def hand_over(n):
                dve.tensor_copy(idA[:], idN[:]).then_inc(id_a, 1)
                dve.tensor_copy(gB[:], gN[:, 16:32]).then_inc(g_b, 1)

            dve.wait_ge(sc_ev, 16)
            dve.wait_ge(ld_gain, 16 * 11)
            pick(1, 0)
            hand_over(1)
            products(0, 0, hA, h_a, 1)
            weights(1, None, gN[:, 0:16])
            dve.wait_ge(id_a, 1)
            dve.tensor_copy(idB[:], idA[:, 16:32]).then_inc(id_b, 1)
            with nc.vector.Fori(0, ITS - 1) as it:
                dve.wait_ge(w_done, it * 2 + 1)
                dve.wait_ge(g_b, it + 1)
                pick(it + 2, it + 1)
                products(0, it * 64 + 32, hB, h_b, it + 1)
                weights(it * 2 + 2, it * 32 + 16, gB[:])
                add_sum(it, 0)
                dve.wait_ge(w_done, it * 2 + 2)
                hand_over(0)
                products(0, it * 64 + 64, hA, h_a, it + 2)
                weights(it * 2 + 3, it * 32 + 32, gN[:, 0:16])
                add_sum(it, 1)
                dve.wait_ge(id_a, it + 2)
                dve.tensor_copy(idB[:], idA[:, 16:32]).then_inc(id_b, 1)
            last = ITS - 1
            products(0, last * 64 + 32, hB, h_b, last + 1)
            dve.wait_ge(g_b, last + 1)
            weights(last * 2 + 2, last * 32 + 16, gB[:])
            add_sum(last, 0)
            add_sum(last, 1)
            for t in range(TILES):
                r = rows(t)
                dve.wait_ge(f_sqrt, t + 1)
                link(dve.reciprocal(rstd[0:r, 8 + t % 2:9 + t % 2], std[0:r, 0:1]))
                if t >= 2:
                    dve.wait_ge(st_y[t % 2], 16 * (t // 2))
                stt(outb[0:r, t % 2], hall[0:r, t], rstd[0:r, 8 + t % 2:9 + t % 2], gfin[0:r], ALU.mult, ALU.mult).then_inc(
                    f_out, 1)


_INS = ["x_prompt", "x_sample", "cache_kv_latent", "cache_k_rope", "state_pool", "cache_mem_k", "cache_mem_v",
        "page_table", "mem_prompt", "attn_norm", "w_in", "q_norm", "kv_norm", "w_q_up", "w_uk", "w_uv",
        "w_pool_grp", "pool_scale", "mem_norm", "w_mem_k", "w_mem_v", "w_pool_out", "w_mla_out", "w_x_out",
        "w_o", "ffn_norm", "w_peer_q", "peer_k1", "peer_k2", "peer_u", "peer_v", "final_norm"]
_OUTS = [(1, SEQ, D), (NB, TS, D), (1, 1, SEQ, KL), (1, 1, SEQ, ROPE), (1, 1, HIST, 512),
         (1, 1, MEM, XH, XD), (1, 1, MEM, XH, XD), (1, NB, TS, KL), (1, NB, TS, ROPE), (1, NB, HIST, 512)]


def shape_constants():
    import numpy as np
    f = np.float32
    p = np.arange(P)
    fold = ((p[:, None] % NS == p[None, :]) & (p[None, :] < NS)).astype(f)
    ident = np.stack([fold, np.eye(P, dtype=f)])
    causal = np.where(p[None, :] <= p[:, None], 0.0, -1.0e30).astype(f)
    row_t, col = np.arange(NS) % TS, np.arange(NS)
    smask = np.full((NS, NB, NS), -1.0e30, f)
    for b in range(NB):
        own = (col[None, :] // TS == b) & (col[None, :] % TS <= row_t[:, None])
        smask[:, b][own] = 0.0
    inv = np.power(f(10000.0), -np.arange(16, dtype=f) / f(16)).astype(f)
    pos = np.zeros((TILES, P), f)
    pos[0, :NS] = 2048 + np.arange(NS) % TS
    pos[1:] = np.arange(SEQ).reshape(TILES - 1, P)
    ang = (pos[:, :, None] * inv).astype(f)
    trig = np.ascontiguousarray(np.concatenate([np.cos(ang), np.sin(ang)], -1).astype(f).transpose(1, 0, 2))
    w = np.array([2, 4, 8, 16], f)[:, None]
    cnt = np.broadcast_to((w / np.minimum(np.arange(16, dtype=f) + 1, w)).astype(f), (P, PG, 16)).copy()
    iota = np.broadcast_to(np.arange(16, dtype=f), (P, 16)).copy()
    return {"c_ident": ident, "c_causal": causal, "c_smask": smask, "c_trig": trig,
            "c_cnt": cnt, "c_iota": iota}


def kernel(**inputs):
    import numpy as _np
    import concourse.bacc as _bacc
    from concourse import mybir as _mybir
    from concourse.bass_utils import run_bass_kernel_spmd as _run

    nc = _bacc.Bacc("TRN2", target_bir_lowering=False, num_devices=1)
    arrays, args = {}, []
    for name in _INS:
        a = _np.ascontiguousarray(inputs[name])
        arrays[f"in_{name}_dram"] = a
        args.append(nc.dram_tensor(f"in_{name}_dram", a.shape, _mybir.dt.from_np(a.dtype), kind="ExternalInput").ap())
    for name, a in shape_constants().items():
        arrays[f"in_{name}_dram"] = a
        args.append(nc.dram_tensor(f"in_{name}_dram", a.shape, _mybir.dt.from_np(a.dtype), kind="ExternalInput").ap())
    for i, shape in enumerate(_OUTS):
        args.append(nc.dram_tensor(f"out_{i}_dram", shape, F32, kind="ExternalOutput").ap())
    hybrid_step(nc, *args)
    r = _run(nc, [arrays], core_ids=[0])
    return tuple(r.results[0][f"out_{i}_dram"] for i in range(len(_OUTS)))
```

```python
from contextlib import ExitStack

import concourse.bass as bass
from concourse import mybir
from concourse.bass import DynSlice, IndirectOffsetOnAxis

ALU = mybir.AluOpType
ACT = mybir.ActivationFunctionType
F32 = mybir.dt.float32
U32 = mybir.dt.uint32
AX_X = mybir.AxisListType.X

P = 128
D = 1024
DK = D // P
EPS = 1e-6
NS = 32
NB = 8
TS = 4
SEQ = 512
NT = NS + SEQ
HALF = NT // 2
TILES = 1 + SEQ // P
MEM = 256
HIST = 15
PG = 4
H = 8
NOPE, ROPE, VD = 64, 32, 64
QD = NOPE + ROPE
QL, KL = 384, 256
XH, XD = 4, 128
PAGES, PAGE = 16, 128
PGRP = 4
LATW = KL + ROPE
OFF_U, OFF_CQ, OFF_CKV, OFF_KR, OFF_QX, OFF_G = 0, 512, 896, 1152, 1184, 1696
EH, NKEY, TOPK = 8, 128, 16
ITS = 17
RING = 8
VCRED = 16 - RING
PICK_AT, GELU_AT = 9, 14
PICK_ROW = 10
NEG = -3.0e38
MLA_SCALE = float(QD) ** -0.5
MEM_SCALE = float(XD) ** -0.5


def rows(t):
    return NS if t == 0 else P


def cols(t):
    return slice(0, NS) if t == 0 else slice(NS + (t - 1) * P, NS + t * P)


def slot(t):
    return (t - 1) % TILES


STREAM = [("qkv", 0, 256), ("qkv", 256, 256), ("qkv", 512, 160),
          ("u", 0, 256), ("u", 256, 256), ("qx", 0, 256), ("qx", 256, 256),
          ("mk", 0, 256), ("mk", 256, 256), ("mv", 0, 256), ("mv", 256, 256)]
WRING = 4


def stream_units():
    for j, (what, c, w) in enumerate(STREAM):
        if what == "qkv":
            for t in range(TILES):
                yield j, what, c, w, t
        elif what in ("u", "qx"):
            for f in range(w // P):
                for half in range(2):
                    yield j, what, c // P + f, f, half
        else:
            for m in range(2):
                yield j, what, c, w, m


UNITS = list(stream_units())
LAST_QKV = max(n for n, u in enumerate(UNITS) if u[1] == "qkv")
LAST_U = max(n for n, u in enumerate(UNITS) if u[1] == "u")
ATT = [("mla", q, h, P * (q + 1)) for q in range(4) for h in range(H)]
ATT += [("mem", q, h, MEM) for q in range(4) for h in range(XH)]


def att_groups():
    out = []
    for n, (kind, q, h, _) in enumerate(ATT):
        if h == 0:
            out.append([kind, q, n, n])
        out[-1][3] = n
    return out


GROUPS = att_groups()
GROUP_OF = {n: g for g, (_, _, a, b) in enumerate(GROUPS) for n in range(a, b + 1)}


def hybrid_step(nc, x_prompt, x_sample, cache_lat, cache_kr, state_pool, cache_mk, cache_mv, page_table,
                mem_prompt, attn_norm, w_in, q_norm, kv_norm, w_q_up, w_uk, w_uv, w_pool_grp, pool_scale,
                mem_norm, w_mem_k, w_mem_v, w_pool_out, w_mla_out, w_x_out, w_o, ffn_norm, w_peer_q,
                peer_k1, peer_k2, peer_u, peer_v, final_norm, c_ident, c_causal, c_smask, c_trig,
                c_cnt, c_iota, y_p, y_s, lat_p, kr_p, pool_p, mk_p, mv_p, lat_s, kr_s, pool_s):
    with ExitStack() as ctx:
        sem = lambda name: ctx.enter_context(nc.semaphore(name))
        ARENA = 207 * 1024
        arena = ctx.enter_context(nc.sbuf_tensor("arena", [P, ARENA // 4], F32))
        bank = ctx.enter_context(nc.psum_tensor("bank", [P, 8, 512], F32))

        def at(kb, shape, dt=F32):
            n = 1
            for s in shape:
                n *= s
            a = int(kb * 256)
            assert a == kb * 256 and a + n <= ARENA // 4, (kb, shape)
            v = arena[:, a:a + n]
            if dt != F32:
                v = v.bitcast(dt)
            if len(shape) > 1:
                names = "abcd"[:len(shape)]
                v = v.rearrange(f"p ({' '.join(names)}) -> p {' '.join(names)}",
                                **{n: s for n, s in zip(names, shape)})
            return v

        ident = at(0, [2, P])
        eye = ident[:, 0]
        causal = at(1, [P])
        smask = at(1.5, [NB, NS])
        trig = at(2.5, [TILES, 32])
        cntfix = at(3.25, [PG, 16])
        iota16 = at(3.5, [16])
        gattn = at(3.75, [DK])
        gmem = at(3.78125, [DK])
        gq = at(3.8125, [3])
        pscale = at(3.84375, [PG])
        ss = at(4, [16])
        std = at(4.0625, [16])
        rstd = at(4.125, [16])
        pagetab = at(4.25, [P], mybir.dt.int32)
        gkv = at(4.75, [KL])
        gfin = at(6, [D])
        gffn = at(10, [D])
        junk = at(14, [D])
        nmax, rsum, rinv, nmax0 = at(18, [64]), at(18.25, [64]), at(18.5, [64]), at(4.75 + 1, [64])
        smx, ssum, srec, smx0 = at(18.75, [16]), at(18.8125, [16]), at(18.875, [16]), at(18.9375, [16])
        mmx, mmx0, msum, mrec = at(19, [4]), at(19.015625, [4]), at(19.03125, [8]), at(19.0625, [4])
        eps = at(19.078125, [1])
        spare = at(19.09375, [8])
        unew = at(19.25, [PG, NS])
        xnT = at(20, [DK, NT])
        pyT = at(37, [4, NT])
        moT = at(45.5, [4, NT])
        xoT = at(54, [4, NT])
        qxT = at(62.5, [4, NT])
        qT = at(71, [H, NT])
        cT = at(88, [2, NT])
        krT = at(92.25, [NT])
        cqkv = at(94.5, [TILES, 672])
        wuk = at(107.75, [2, 512])
        wuv = at(111.75, [2, 512])
        wring = at(115.75, [WRING, DK, 256])
        mnT = at(147.75, [DK, MEM])
        wqup = at(155.75, [3, 768])
        xin = at(164.75, [3, D])
        krp = at(205, [TILES, 96])
        uP = at(178.75, [PG, HIST + SEQ])
        uS = at(187, [PG, NB, HIST + TS])
        hist = at(189.5, [512])
        uout = at(191.5, [2, 512])
        mkv = at(195.5, [2, 2, 512])
        rot_a, rot_b = at(203.5, [H, ROPE]), at(191.5, [H, ROPE])
        qnT = at(164.75, [3, NT])
        qtm = at(147.75, [2, 768])
        dT = at(155.75, [PG, NT])
        wpool = at(171.5, [PG, P])
        psum_a = at(115.75, [SEQ + HIST])
        psum_b = at(118, [SEQ + HIST])
        ssum_a = at(120.25, [NB, HIST + TS])
        ssum_b = at(121, [NB, HIST + TS])
        pages = at(115.75, [2 * 4, PGRP, LATW])
        wukT = at(153, [H, KL])
        qlat = at(161, [2, NB, H, TS])
        qrot = at(163, [NB, H, TS])
        latT = at(164, [2, 2, 512])
        krpT = at(172, [2, 512])
        scor = at(176, [2080])
        prob = at(184.25, [2080])
        probT = at(60, [17, NS])
        olat = at(203.5, [KL])
        olatT = at(62.5 - 8.5, [2, H, NB, TS])
        osmp = at(58, [512])
        smem = at(115.75, [3, 2, 2, 512])
        smT = at(139.75, [XH, MEM])
        sms = at(143.75, [XH, MEM])
        smpT = at(147.75, [XH, 2, TS])
        smo = at(148, [512])
        kT = at(142, [H, SEQ])
        vtm = at(158, [4, 512])
        mkT = at(166, [XH, MEM])
        prb = at(170, [3, 512])
        prbT = at(176, [2, 4, P])
        otm = at(180, [2, 512])
        wmg = at(62.5, [2, 3, 12, P])
        mgT = at(98.5, [DK, NT])
        sig = at(115.5, [2, 2, HALF])
        mtmp = at(119.75, [2, HALF])
        wo = at(122, [DK, D])
        hall = at(154, [TILES, D])
        hn = at(174, [TILES, D])
        hnT = at(20, [DK, NT])
        wpq = at(37, [4, DK, P])
        qp = at(53, [2, NT])
        keysT = at(57.5, [2, P])
        keys = at(58.5, [2, P])
        scores = at(60, [ITS, 4, NKEY])
        uring = at(98.5, [RING, D])
        vring = at(20, [RING, D])
        hA, hB = at(131, [D]), at(135, [D])
        diag = at(139, [16, P])
        sc = at(147, [4, NKEY])
        cand = at(149, [2, 256])
        onehot = at(151, [32, 16])
        val = at(153, [4, 16])
        vix = at(153.25, [4, 16], U32)
        vixf = at(153.5, [4, 16])
        top, top0 = at(153.75, [2, 16]), at(153.875, [2, 16])
        sel = at(195, [2, 16], U32)
        sela = at(195.125, [2, 16], U32)
        selb = at(195.25, [2, 16], U32)
        selaf = at(195.375, [2, 16])
        selbf = at(195.5, [2, 16])
        e1 = at(195.625, [2, 16])
        e2 = at(195.75, [2, 16])
        gexp = at(195.875, [2, 16])
        gs2 = at(196, [8])
        gr2 = at(196.125, [8])
        idN = at(196.25, [32], U32)
        idA = at(196.375, [32], U32)
        idB = at(196.5, [16], U32)
        gN = at(196.625, [32])
        gB = at(196.75, [16])
        act_a = at(196.875, [16])
        act_g = at(197, [16])
        wts = at(197.125, [16])
        outb = at(98.5, [2, D])

        ld_const, ld_gain, ld_w, ld_state = sem("ld_const"), sem("ld_gain"), sem("ld_w"), sem("ld_state")
        zeroed = sem("zeroed")
        ld_x = [sem(f"ld_x{i}") for i in range(3)]
        sqrt_done, xs_done, xT_mm, xT_ev = map(sem, ("sqrt_done", "xs_done", "xT_mm", "xT_ev"))
        ld_ring = [sem(f"ld_ring{i}") for i in range(WRING)]
        st_mm, st_ev = sem("st_mm"), sem("st_ev")
        rstd_read, q_sqrt, q_norm_done, kr_done, c_mm, c_ev_d, c_ev_a = map(
            sem, ("rstd_read", "q_sqrt", "q_norm_done", "kr_done", "c_mm", "c_ev_d", "c_ev_a"))
        qu_mm, qu_ev, qu_rope, qt_mm, qt_ev = map(sem, ("qu_mm", "qu_ev", "qu_rope", "qt_mm", "qt_ev"))
        hi_mm, hi_ev, uo_mm, uo_ev, pool_d, pool_mm, pool_ev = map(
            sem, ("hi_mm", "hi_ev", "uo_mm", "uo_ev", "pool_d", "pool_mm", "pool_ev"))
        ld_pool = sem("ld_pool")
        uk_mm, uk_ev, ql_mm, ql_ev = map(sem, ("uk_mm", "uk_ev", "ql_mm", "ql_ev"))
        ld_page = [sem(f"ld_page{i}") for i in range(8)]
        pt_mm, pt_ev, pt_ed, ps_mm, ps_ev, ps_max, ps_exp, pp_mm, pp_ev, pv_free, pv_mm, pv_ev, po_mm, po_ev = map(
            sem, ("pt_mm", "pt_ev", "pt_ed", "ps_mm", "ps_ev", "ps_max", "ps_exp", "pp_mm", "pp_ev", "pv_free",
                  "pv_mm", "pv_ev", "po_mm", "po_ev"))
        so_mm, so_ev, sot_mm, sot_ev = map(sem, ("so_mm", "so_ev", "sot_mm", "sot_ev"))
        ld_sm0 = 16 * PGRP * NB // 2
        (mt_mm, mt_ev, ms_mm, ms_max, ms_exp, mp_mm, mp_ev, mo_mm, mo_ev, mx_mm, mx_ev) = map(
            sem, ("mt_mm", "mt_ev", "ms_mm", "ms_max", "ms_exp", "mp_mm", "mp_ev", "mo_mm", "mo_ev",
                  "mx_mm", "mx_ev"))
        kv_mm, kv_ev, krk_done = sem("kv_mm"), sem("kv_ev"), sem("krk_done")
        (at_mm, at_max, at_exp, at_tm, at_te, at_pv, at_oe, at_xm, at_xe) = map(
            sem, ("at_mm", "at_max", "at_exp", "at_tm", "at_te", "at_pv", "at_oe", "at_xm", "at_xe"))
        ld_mg = [sem(f"ld_mg{i}") for i in range(2)]
        mg_mm, mg_sig, mg_ev = sem("mg_mm"), sem("mg_sig"), sem("mg_ev")
        ld_wo, wo_mm, wo_ev = sem("ld_wo"), sem("wo_mm"), sem("wo_ev")
        hn_rep, h_sqrt, h_norm, hT_mm, hT_ev = map(sem, ("hn_rep", "h_sqrt", "h_norm", "hT_mm", "hT_ev"))
        ld_keys, key_mm, key_ev = sem("ld_keys"), sem("key_mm"), sem("key_ev")
        ld_pq = [sem(f"ld_pq{i}") for i in range(4)]
        pq_mm, pq_ev, sc_mm, sc_ev = map(sem, ("pq_mm", "pq_ev", "sc_mm", "sc_ev"))
        u_in = [sem(f"u_in{i}") for i in range(RING)]
        U0 = 16 * PGRP * NB // 2
        v_in = [sem(f"v_in{i}") for i in range(RING)]
        (tk_gap, tk_exp, id_next, id_a, id_b, g_b, gelu_done, w_done, diag_done, u_free, v_free,
         acc_free, h_a, h_b) = map(sem, (
            "tk_gap", "tk_exp", "id_next", "id_a", "id_b", "g_b", "gelu_done", "w_done", "diag_done",
            "u_free", "v_free", "acc_free", "h_a", "h_b"))
        f_sqrt, f_out = sem("f_sqrt"), sem("f_out")
        st_y = [sem("st_y0"), sem("st_y1")]
        stored, st_lat, st_pool = sem("stored"), sem("st_lat"), sem("st_pool")
        dve_chain, act_chain = sem("dve_chain"), sem("act_chain")
        carrier = sem("carrier")

        block = ctx.enter_context(nc.Block())

        @block.sync
        def _(sp):
            n_store = 0

            def store(dst, src):
                nonlocal n_store
                n_store += 1
                sp.dma_start(dst, src).then_inc(stored, 16)

            def load_x(i):
                if i >= 3:
                    sp.wait_ge(xT_mm, 2 * (i - 2))
                dst = xin[:, i % 3]
                if i == 0:
                    sp.dma_start(dst[0:NS], x_sample.rearrange("b t d -> (b t) d")).then_inc(ld_x[0], 16)
                elif i < TILES:
                    sp.dma_start(dst, x_prompt[0, (i - 1) * P:i * P]).then_inc(ld_x[i % 3], 16)
                else:
                    m = i - TILES
                    sp.dma_start(dst, mem_prompt[0, m * P:(m + 1) * P]).then_inc(ld_x[i % 3], 16)

            def load_stream(j):
                what, c, w = STREAM[j]
                if j >= WRING:
                    last = max(n for n, u in enumerate(UNITS) if u[0] == j - WRING)
                    sp.wait_ge(st_mm, last + 1)
                if what in ("qkv", "u", "qx"):
                    c += {"qkv": OFF_CQ, "u": OFF_U, "qx": OFF_QX}[what]
                    src = w_in[0][:, c:c + w]
                else:
                    src = (w_mem_k if what == "mk" else w_mem_v)[0].rearrange("d h e -> d (h e)")[:, c:c + w]
                sp.dma_start(wring[:, j % WRING, :, 0:w], src.rearrange("(k p) n -> p k n", p=P)).then_inc(
                    ld_ring[j % WRING], 16)

            sp.dma_start(ident[:], c_ident.rearrange("a p n -> p a n")).then_inc(ld_const, 16)
            sp.dma_start(gattn[:], attn_norm[0].rearrange("(k p) -> p k", p=P), allow_slow_non_contiguous=True).then_inc(ld_const, 16)
            sp.dma_start(gmem[:], mem_norm[0].rearrange("(k p) -> p k", p=P), allow_slow_non_contiguous=True).then_inc(ld_const, 16)
            for i in range(3):
                load_x(i)
            load_stream(0)
            load_stream(1)
            for i in range(3, 7):
                load_x(i)
                if i < 5:
                    load_stream(i - 1)
            sp.dma_start(causal[:], c_causal).then_inc(ld_gain, 16)
            sp.dma_start(smask[0:NS], c_smask).then_inc(ld_gain, 16)
            sp.dma_start(trig[:], c_trig).then_inc(ld_gain, 16)
            sp.dma_start(cntfix[:], c_cnt).then_inc(ld_gain, 16)
            sp.dma_start(iota16[:], c_iota).then_inc(ld_gain, 16)
            sp.dma_start(gq[:], q_norm[0].rearrange("(k p) -> p k", p=P), allow_slow_non_contiguous=True).then_inc(ld_gain, 16)
            sp.dma_start(pscale[:], pool_scale[0].rearrange("(k p) -> p k", p=P), allow_slow_non_contiguous=True).then_inc(ld_gain, 16)
            sp.dma_start(gkv[:], kv_norm.to_broadcast([P, KL])).then_inc(ld_gain, 16)
            sp.dma_start(gffn[:], ffn_norm.to_broadcast([P, D])).then_inc(ld_gain, 16)
            sp.dma_start(gfin[:], final_norm.rearrange("(a d) -> a d", a=1).to_broadcast([P, D])).then_inc(ld_gain, 16)
            sp.dma_start(pagetab[0:1], page_table.rearrange("(a b) n -> a (b n)", a=1)).then_inc(ld_gain, 16)
            sp.dma_start(hist[0:NB * HIST], state_pool[0].rearrange("b t c -> (b t) c")).then_inc(ld_state, 16)
            store(pool_s[0][:, 0:HIST - TS], state_pool[0][:, TS:HIST])
            sp.dma_start(wqup[:], w_q_up[0].rearrange("(k p) h e -> p k (h e)", p=P)).then_inc(ld_w, 16)
            sp.dma_start(wuk[:], w_uk[0].rearrange("(k p) h e -> p k (h e)", p=P)).then_inc(ld_w, 16)
            sp.dma_start(wuv[:], w_uv[0].rearrange("(k p) h e -> p k (h e)", p=P)).then_inc(ld_w, 16)
            for j in range(4, len(STREAM)):
                load_stream(j)
            sp.wait_ge(st_ev, len(UNITS))
            for k, dst in enumerate((mk_p, mv_p)):
                store(dst[0, 0].rearrange("(m p) h e -> p m (h e)", p=P), mkv[:, k])
            sp.wait_ge(q_norm_done, 10)
            sp.wait_ge(kr_done, 1)
            for dst, src in ((lat_s[0].rearrange("b t c -> (b t) c"), cqkv[0:NS, 0, QL:QL + KL]),
                             (lat_p[0, 0].rearrange("(t p) c -> p t c", p=P), cqkv[:, 1:, QL:QL + KL]),
                             (kr_s[0].rearrange("b t c -> (b t) c"), krp[0:NS, 0, NOPE:QD]),
                             (kr_p[0, 0].rearrange("(t p) c -> p t c", p=P), krp[:, 1:, NOPE:QD])):
                sp.dma_start(dst, src).then_inc(st_lat, 16)
            sp.wait_ge(qu_mm, 2 * TILES)
            sp.dma_start(wpool[:], w_pool_grp[0].rearrange("g c d -> c g d")).then_inc(ld_pool, 16)
            sp.wait_ge(uo_ev, 2)
            for b in range(NB):
                sp.dma_start(pool_s[0, b, HIST - TS:HIST], uout[b * TS:(b + 1) * TS, 0]).then_inc(st_pool, 16)
            sp.dma_start(pool_p[0, 0], uout[0:HIST, 1]).then_inc(st_pool, 16)
            sp.wait_ge(pool_d, PG)
            sp.wait_ge(qt_mm, 2 * TILES)

            def load_group(b, g):
                s = (b % 2) * 4 + g
                if b >= 2:
                    sp.wait_ge(pv_free, 4 * (b - 2) + g + 1)
                for k in range(PGRP):
                    n = b * PAGES + g * PGRP + k
                    page = sp.value_load(pagetab[0:1, n:n + 1], min_val=0, max_val=cache_lat.shape[1] - 1)
                    sp.dma_start(pages[:, s, k, 0:KL],
                                 cache_lat[0][DynSlice(page, 1)].rearrange("a p c -> (a p) c")).then_inc(ld_page[s], 16)

            sp.wait_ge(ld_gain, 16 * 11)
            for b in range(NB):
                for g in range(4):
                    load_group(b, g)
            sp.wait_ge(pv_mm, NB)
            for b in range(NB):
                if b >= 3:
                    sp.wait_ge(mo_mm, b - 2)
                    sp.wait_ge(mt_mm, 2 * (b - 2))
                for k, src in enumerate((cache_mk, cache_mv)):
                    sp.dma_start(smem[:, b % 3, k], src[0, b].rearrange("(m p) h e -> p m (h e)", p=P)).then_inc(
                        ld_page[b % 3], 16)
            def load_merge(f):
                if f >= 2:
                    sp.wait_ge(mg_mm, 3 * (f - 1))
                for i, wout in enumerate((w_pool_out, w_mla_out, w_x_out)):
                    c = OFF_G + i * D + f * P
                    sp.dma_start(wmg[:, f % 2, i, 0:8], w_in[0][:, c:c + P].rearrange("(k p) n -> p k n", p=P)).then_inc(
                        ld_mg[f % 2], 16)
                    sp.dma_start(wmg[:, f % 2, i, 8:12],
                                 wout[0][:, f * P:(f + 1) * P].rearrange("(k p) n -> p k n", p=P)).then_inc(
                        ld_mg[f % 2], 16)

            sp.wait_ge(at_mm, len(ATT))
            sp.wait_ge(at_pv, len(ATT))
            sp.wait_ge(at_xm, len(GROUPS))
            sp.wait_ge(st_lat, 16 * 4)
            load_merge(0)
            load_merge(1)
            sp.dma_start(wo[:], w_o[0].rearrange("(k p) n -> p k n", p=P)).then_inc(ld_wo, 16)
            sp.dma_start(hall[0:NS, slot(0)], x_sample.rearrange("b t d -> (b t) d")).then_inc(ld_wo, 16)
            sp.dma_start(hall[:, 0:TILES - 1], x_prompt[0].rearrange("(t p) d -> p t d", p=P)).then_inc(ld_wo, 16)
            for f in range(2, DK):
                load_merge(f)
            sp.wait_ge(mg_mm, 3 * DK)
            sp.dma_start(keys[:, 0], peer_k1[0]).then_inc(ld_keys, 16)
            sp.dma_start(keys[:, 1], peer_k2[0]).then_inc(ld_keys, 16)
            wq = w_peer_q[0].rearrange("(k p) h (a c) -> p k (h a) c", p=P, a=2)
            for j in range(16):
                if j >= 4:
                    sp.wait_ge(pq_mm, j - 3)
                sp.dma_start(wpq[:, j % 4], wq[:, :, j]).then_inc(ld_pq[j % 4], 16)
            for n in range(TILES):
                t = (n + 1) % TILES
                sp.wait_ge(f_out, n + 1)
                dst = y_s.rearrange("b t d -> (b t) d") if t == 0 else y_p[0, (t - 1) * P:t * P]
                sp.dma_start(dst, outb[0:rows(t), n % 2]).then_inc(st_y[n % 2], 16)
            sp.wait_ge(st_y[0], 48)
            sp.wait_ge(st_y[1], 32)
            sp.wait_ge(st_pool, 16 * (NB + 1))
            sp.wait_ge(st_lat, 16 * 4)
            sp.wait_ge(stored, 16 * n_store)

        @block.gpsimd
        def _(pool):
            pool.memset(ss[:], 1.0).then_inc(zeroed, 1)
            pool.memset(cqkv[:, 0], 0.0).then_inc(zeroed, 1)
            pool.memset(krp[:], 0.0).then_inc(zeroed, 1)
            pool.memset(uP[:, :, 0:HIST], 0.0).then_inc(zeroed, 1)
            pool.memset(eps[:], EPS).then_inc(zeroed, 1)
            pool.memset(spare[:, 0:1], 0.0).then_inc(u_free, RING)
            pool.memset(spare[:, 1:2], 0.0).then_inc(v_free, 16)
            pool.memset(spare[:, 2:3], 0.0).then_inc(acc_free, 2)

            pool.wait_ge(ld_gain, 16 * 11)
            pool.wait_ge(pool_d, PG)
            pool.wait_ge(qt_mm, 2 * TILES)
            for b in range(NB):
                for g in range(4):
                    s = (b % 2) * 4 + g
                    if b >= 2:
                        pool.wait_ge(pv_free, 4 * (b - 2) + g + 1)
                    for k in range(PGRP):
                        n = b * PAGES + g * PGRP + k
                        page = pool.value_load(pagetab[0:1, n:n + 1], min_val=0, max_val=cache_kr.shape[1] - 1)
                        pool.dma_start(pages[:, s, k, KL:LATW],
                                       cache_kr[0][DynSlice(page, 1)].rearrange("a p c -> (a p) c")).then_inc(
                            u_in[s], 16)

            def gather(ring, land, k, table, ix):
                pool.sem_inc(carrier, 1)
                pool.indirect_dma_start(out=ring[:, k % RING], out_offset=None, in_=table[0],
                                        in_offset=IndirectOffsetOnAxis(ap=ix, axis=0)).then_inc(land[k % RING], 16)

            pool.wait_ge(id_next, 1)
            for k in range(16):
                pool.wait_ge(u_free, k + 1)
                gather(uring, u_in, k, peer_u, idN[:, k:k + 1])

            def half_1(it):
                pool.wait_ge(id_a, it + 1)
                for k in range(16):
                    pool.wait_ge(u_free, it * 32 + (16 + k + 1))
                    gather(uring, u_in, k, peer_u, idA[:, 16 + k:17 + k])
                    pool.wait_ge(v_free, it * 32 + (k + 1 + VCRED))
                    gather(vring, v_in, k, peer_v, idA[:, k:k + 1])

            def half_2(it, last):
                pool.wait_ge(id_b, it + 1)
                if not last:
                    pool.wait_ge(id_next, it + 2)
                for k in range(16):
                    if not last:
                        pool.wait_ge(u_free, it * 32 + (32 + k + 1))
                        gather(uring, u_in, k, peer_u, idN[:, k:k + 1])
                    pool.wait_ge(v_free, it * 32 + (16 + k + 1 + VCRED))
                    gather(vring, v_in, k, peer_v, idB[:, k:k + 1])

            pool.wait_ge(id_a, 1)
            for k in range(16):
                pool.wait_ge(u_free, 16 + k + 1)
                gather(uring, u_in, k, peer_u, idA[:, 16 + k:17 + k])
            pool.wait_ge(pq_mm, 16)
            for k in range(16):
                pool.wait_ge(v_free, k + 1 + VCRED)
                gather(vring, v_in, k, peer_v, idA[:, k:k + 1])
            half_2(0, False)
            with nc.gpsimd.Fori(1, ITS - 1) as it:
                half_1(it)
                half_2(it, False)
            half_1(ITS - 1)
            half_2(ITS - 1, True)

        @block.tensor
        def _(pe):
            def turn(dst, src, n):
                return pe.transpose(dst, src, eye[0:n, 0:n])

            def sum_k(dst, lhs, rhs, n):
                for k in range(n):
                    last = pe.matmul(dst, lhs(k), rhs(k), start=(k == 0), stop=(k == n - 1))
                return last

            pe.wait_ge(ld_const, 48)
            def turn_x(i):
                r = NS if i == 0 else P
                pe.wait_ge(xs_done, i + 1)
                for c in range(2):
                    n = 2 * i + c
                    if n >= 4:
                        pe.wait_ge(xT_ev, n - 3)
                    for k in range(4):
                        last = turn(bank[:, n % 4, k * P:k * P + r],
                                    xin[0:r, i % 3, (4 * c + k) * P:(4 * c + k + 1) * P], r)
                    last.then_inc(xT_mm, 1)

            def stream(n):
                j, what, c, w, m = UNITS[n]
                if n == 0 or UNITS[n - 1][0] != j:
                    pe.wait_ge(ld_ring[j % WRING], 16 * (j // WRING + 1))
                if n >= 4:
                    pe.wait_ge(st_ev, n - 3)
                b = 4 + n % 4
                wt = wring[:, j % WRING]
                if what == "qkv":
                    pe.wait_ge(xT_ev, 2 * (m + 1))
                    last = sum_k(bank[0:rows(m), b, 0:w], lambda k: xnT[:, k, cols(m)], lambda k: wt[:, k, 0:w], DK)
                elif what in ("u", "qx"):
                    last = sum_k(bank[:, b, 0:HALF], lambda k: wt[:, k, w * P:(w + 1) * P],
                                 lambda k: xnT[:, k, m * HALF:(m + 1) * HALF], DK)
                else:
                    last = sum_k(bank[:, b, 0:w], lambda k: mnT[:, k, m * P:(m + 1) * P], lambda k: wt[:, k, 0:w], DK)
                last.then_inc(st_mm, 1)

            for i in range(5):
                turn_x(i)
                stream(i)
            turn_x(5)
            for n in range(5, 10):
                stream(n)
            turn_x(6)
            pe.wait_ge(xT_ev, 14)
            for n in range(10, LAST_U + 1):
                stream(n)
            def turn_c(t):
                r = rows(t)
                pe.wait_ge(q_norm_done, 2 * (t + 1))
                pe.wait_ge(kr_done, 1)
                b = 2 * (t % 2)
                if t >= 2:
                    pe.wait_ge(c_ev_d, t - 1)
                    pe.wait_ge(c_ev_a, t - 1)
                for k in range(3):
                    last = turn(bank[:, b, k * P:k * P + r], cqkv[0:r, t, k * P:(k + 1) * P], r)
                last.then_inc(c_mm, 1)
                for k in range(2):
                    turn(bank[:, b + 1, k * P:k * P + r], cqkv[0:r, t, QL + k * P:QL + (k + 1) * P], r)
                turn(bank[0:QD, b + 1, 2 * P:2 * P + r], krp[0:r, t], r).then_inc(c_mm, 1)

            rest = list(range(LAST_U + 1, len(UNITS)))
            for t in range(TILES):
                stream(rest[t])
                turn_c(t)
            for n in rest[TILES:]:
                stream(n)
            pe.wait_ge(ld_w, 48)
            pe.wait_ge(st_ev, len(UNITS))
            pe.wait_ge(c_ev_d, TILES)
            pe.wait_ge(c_ev_a, TILES)
            for t in range(TILES + 1):
                if t < TILES:
                    for c in range(2):
                        n = 2 * t + c
                        if n >= 4:
                            pe.wait_ge(qu_ev, n - 3)
                        sum_k(bank[0:rows(t), 4 + n % 4, 0:384], lambda k: qnT[:, k, cols(t)],
                              lambda k: wqup[:, k, c * 384:(c + 1) * 384], 3).then_inc(qu_mm, 1)
                if t >= 1:
                    pe.wait_ge(qu_rope, t)
                    r = rows(t - 1)
                    for c in range(2):
                        n = 2 * (t - 1) + c
                        if n >= 4:
                            pe.wait_ge(qt_ev, n - 3)
                        for k in range(4):
                            h = 4 * c + k
                            last = turn(bank[0:QD, n % 4, k * P:k * P + r],
                                        qtm[0:r, (t - 1) % 2, h * QD:(h + 1) * QD], r)
                        last.then_inc(qt_mm, 1)
            pe.wait_ge(ld_state, 16)
            pe.wait_ge(qt_ev, 2 * TILES)
            for g in range(PG):
                last = turn(bank[:, 0, g * P:g * P + NB * HIST], hist[0:NB * HIST, g * P:(g + 1) * P], NB * HIST)
            last.then_inc(hi_mm, 1)
            for g in range(PG):
                last = turn(bank[0:NS, 1, g * P:(g + 1) * P], unew[:, g], P)
            last.then_inc(uo_mm, 1)
            for g in range(PG):
                last = turn(bank[0:HIST, 2, g * P:(g + 1) * P], uP[:, g, SEQ:SEQ + HIST], P)
            last.then_inc(uo_mm, 1)
            pe.wait_ge(hi_ev, 1)
            pe.wait_ge(uo_ev, 2)
            pe.wait_ge(ld_pool, 16)
            pe.wait_ge(qu_ev, 2 * TILES)
            for n in range(2 * PG):
                g, half = n // 2, n % 2
                pe.wait_ge(pool_d, g + 1)
                if n >= 4:
                    pe.wait_ge(pool_ev, n - 3)
                pe.matmul(bank[:, 4 + n % 4, 0:HALF], wpool[:, g], dT[:, g, half * HALF:(half + 1) * HALF],
                          start=True, stop=True).then_inc(pool_mm, 1)
            for n in range(4):
                for i in range(4):
                    h, c = 2 * n + i // 2, i % 2
                    last = turn(bank[0:NOPE, n, i * P:(i + 1) * P], wuk[:, c, h * NOPE:(h + 1) * NOPE], P)
                last.then_inc(uk_mm, 1)
            pe.wait_ge(pool_ev, 2 * PG)
            pe.wait_ge(uk_ev, 4)
            for h in range(H):
                for c in range(2):
                    last = pe.matmul(bank[:, 4, (h * 2 + c) * NS:(h * 2 + c + 1) * NS],
                                     wukT[0:NOPE, h, c * P:(c + 1) * P], qT[0:NOPE, h, 0:NS], start=True, stop=True)
            last.then_inc(ql_mm, 1)

            def page_turns(b, g):
                n = 4 * b + g
                pe.wait_ge(ld_page[n % 8], 16 * PGRP * (b // 2 + 1))
                pe.wait_ge(u_in[n % 8], 16 * PGRP * (b // 2 + 1))
                if n >= 1:
                    pe.wait_ge(pt_ev, n)
                    pe.wait_ge(pt_ed, 2 * n)
                for c in range(2):
                    for k in range(PGRP):
                        last = turn(bank[:, c, k * P:(k + 1) * P], pages[:, n % 8, k, c * P:(c + 1) * P], P)
                    last.then_inc(pt_mm, 1)
                for k in range(PGRP):
                    last = turn(bank[0:QD, 2, k * P:(k + 1) * P], pages[:, n % 8, k, LATW - QD:LATW], P)
                last.then_inc(pt_mm, 1)

            def page_scores(b, g):
                n, m = 4 * b + g, 5 * b + g
                if g < 4:
                    pe.wait_ge(pt_ev, n + 1)
                    pe.wait_ge(pt_ed, 2 * (n + 1))
                if m >= 2:
                    pe.wait_ge(ps_ev, m - 1)
                w = 512 if g < 4 else NS
                dst = bank[0:NS, 3 + m % 2, 0:w]
                kc = (lambda c: latT[:, n % 2, c]) if g < 4 else (lambda c: cT[:, c, 0:NS])
                kr = krpT[NOPE:QD, n % 2] if g < 4 else krT[NOPE:QD, 0:NS]
                for c in range(2):
                    pe.matmul(dst, qlat[:, c, b].rearrange("p h t -> p (h t)"), kc(c), start=(c == 0), stop=False)
                pe.matmul(dst, qrot[NOPE:QD, b].rearrange("p h t -> p (h t)"), kr, start=False,
                          stop=True).then_inc(ps_mm, 1)

            def page_probs(b):
                pe.wait_ge(ps_exp, b + 1)
                if b >= 1:
                    pe.wait_ge(pp_ev, 2 * b)
                    pe.wait_ge(po_ev, b)
                for k in range(PAGES):
                    last = turn(bank[:, 5, k * NS:(k + 1) * NS], prob[0:NS, k * P:(k + 1) * P], NS)
                last.then_inc(pp_mm, 1)
                turn(bank[0:NS, 6, 0:NS], prob[0:NS, PAGES * P:PAGES * P + NS], NS).then_inc(pp_mm, 1)

            def page_values(b):
                pe.wait_ge(pp_ev, 2 * (b + 1))
                if b >= 1:
                    pe.wait_ge(pv_ev, b)
                for k in range(PAGES):
                    s = (b % 2) * 4 + k // PGRP
                    last = pe.matmul(bank[0:NS, 7, 0:KL], probT[:, k], pages[:, s, k % PGRP, 0:KL],
                                     start=(k == 0), stop=False)
                    if k % PGRP == PGRP - 1:
                        last.then_inc(pv_free, 1)
                pe.matmul(bank[0:NS, 7, 0:KL], probT[0:NS, PAGES], cqkv[0:NS, 0, QL:QL + KL], start=False,
                          stop=True).then_inc(pv_mm, 1)

            def page_out(b):
                pe.wait_ge(pv_ev, b + 1)
                for c in range(2):
                    last = turn(bank[:, 6, 64 + c * NS:64 + (c + 1) * NS], olat[0:NS, c * P:(c + 1) * P], NS)
                last.then_inc(po_mm, 1)

            pe.wait_ge(ql_ev, 3)
            for b in range(NB + 1):
                if b < NB:
                    page_turns(b, 0)
                    page_turns(b, 1)
                    page_scores(b, 0)
                    page_turns(b, 2)
                    page_scores(b, 1)
                if b >= 1:
                    page_probs(b - 1)
                if b < NB:
                    page_turns(b, 3)
                    page_scores(b, 2)
                if b >= 1:
                    page_values(b - 1)
                if b < NB:
                    page_scores(b, 3)
                if b >= 1:
                    page_out(b - 1)
                if b < NB:
                    page_scores(b, 4)
            pe.wait_ge(po_ev, NB)
            pe.wait_ge(ps_ev, 5 * NB)
            for h in range(H):
                for c in range(2):
                    last = pe.matmul(bank[0:NS, 3, h * VD:(h + 1) * VD], olatT[:, c, h].rearrange("p b t -> p (b t)"),
                                     wuv[:, c, h * VD:(h + 1) * VD], start=(c == 0), stop=(c == 1))
            last.then_inc(so_mm, 1)
            pe.wait_ge(so_ev, 1)
            for c in range(4):
                last = turn(bank[:, 4, c * NS:(c + 1) * NS], osmp[0:NS, c * P:(c + 1) * P], NS)
            last.then_inc(sot_mm, 1)

            pe.wait_ge(pt_ev, 4 * NB)
            pe.wait_ge(pt_ed, 8 * NB)
            def mem_turns(b):
                pe.wait_ge(ld_page[b % 3], ld_sm0 + 32 * (b // 3 + 1))
                if b >= 1:
                    pe.wait_ge(mt_ev, 2 * b)
                for i in range(2):
                    for k in range(4):
                        h, m = 2 * i + k // 2, k % 2
                        last = turn(bank[:, i, k * P:(k + 1) * P], smem[:, b % 3, 0, m, h * XD:(h + 1) * XD], P)
                    last.then_inc(mt_mm, 1)

            def mem_scores(b):
                pe.wait_ge(mt_ev, 2 * (b + 1))
                if b >= 1:
                    pe.wait_ge(ms_exp, XH * b)
                for h in range(XH):
                    last = pe.matmul(bank[0:TS, 2 + h // 2, (h % 2) * MEM:(h % 2 + 1) * MEM],
                                     qxT[:, h, b * TS:(b + 1) * TS], smT[:, h], start=True, stop=True)
                last.then_inc(ms_mm, 1)

            def mem_probs(b):
                pe.wait_ge(ms_exp, XH * (b + 1))
                if b >= 1:
                    pe.wait_ge(mp_ev, b)
                for h in range(XH):
                    for m in range(2):
                        last = turn(bank[:, 5, (h * 2 + m) * TS:(h * 2 + m + 1) * TS],
                                    sms[0:TS, h, m * P:(m + 1) * P], TS)
                last.then_inc(mp_mm, 1)

            def mem_values(b):
                pe.wait_ge(mp_ev, b + 1)
                if b >= 1:
                    pe.wait_ge(mo_ev, b)
                for h in range(XH):
                    for m in range(2):
                        last = pe.matmul(bank[0:TS, 6, h * XD:(h + 1) * XD], smpT[:, h, m],
                                         smem[:, b % 3, 1, m, h * XD:(h + 1) * XD],
                                         start=(m == 0), stop=(m == 1))
                last.then_inc(mo_mm, 1)

            def mem_out(b):
                pe.wait_ge(mo_ev, b + 1)
                if b >= 1:
                    pe.wait_ge(mx_ev, b)
                for c in range(4):
                    last = turn(bank[:, 7, c * TS:(c + 1) * TS], smo[0:TS, c * P:(c + 1) * P], TS)
                last.then_inc(mx_mm, 1)

            mem_turns(0)
            for b in range(NB + 2):
                if b < NB:
                    mem_scores(b)
                if 1 <= b <= NB:
                    mem_probs(b - 1)
                if b + 1 < NB:
                    mem_turns(b + 1)
                if b >= 2:
                    mem_out(b - 2)
                if 1 <= b <= NB:
                    mem_values(b - 1)

            pe.wait_ge(mx_ev, NB)
            pe.wait_ge(sot_ev, 1)
            for n in range(14):
                if n >= 8:
                    pe.wait_ge(kv_ev, n - 7)
                b = n % 8
                if n < 2:
                    for k in range(4):
                        h, m = 2 * n + k // 2, k % 2
                        last = turn(bank[:, b, k * P:(k + 1) * P], mkv[:, 0, m, h * XD:(h + 1) * XD], P)
                elif n < 10:
                    h = n - 2
                    last = sum_k(bank[0:NOPE, b], lambda k: wuk[:, k, h * NOPE:(h + 1) * NOPE],
                                 lambda k: cT[:, k, NS:NT], 2)
                else:
                    t = n - 10
                    last = sum_k(bank[:, b], lambda k: cT[:, k, cols(t + 1)], lambda k: wuv[:, k], 2)
                last.then_inc(kv_mm, 1)

            def att_scores(u):
                kind, q, h, L = ATT[u]
                if u >= 3:
                    pe.wait_ge(at_exp, u - 2)
                dst = bank[:, u % 3, 0:L]
                if kind == "mla":
                    pe.matmul(dst, qT[0:QD, h, cols(q + 1)], kT[0:QD, h, 0:L], start=True, stop=True).then_inc(at_mm, 1)
                else:
                    pe.matmul(dst, qxT[:, h, cols(q + 1)], mkT[:, h], start=True, stop=True).then_inc(at_mm, 1)

            def att_turn(u):
                L = ATT[u][3]
                pe.wait_ge(at_exp, u + 1)
                if u >= 2:
                    pe.wait_ge(at_te, u - 1)
                for k in range(L // P):
                    last = turn(bank[:, 3 + u % 2, k * P:(k + 1) * P], prb[:, u % 3, k * P:(k + 1) * P], P)
                last.then_inc(at_tm, 1)

            def att_values(u):
                kind, q, h, L = ATT[u]
                g = GROUP_OF[u]
                pe.wait_ge(at_te, u + 1)
                if h == 0 and g >= 2:
                    pe.wait_ge(at_oe, g - 1)
                if kind == "mla":
                    last = sum_k(bank[:, 5 + g % 2, h * VD:(h + 1) * VD], lambda k: prbT[:, u % 2, k],
                                 lambda k: vtm[:, k, h * VD:(h + 1) * VD], L // P)
                else:
                    last = sum_k(bank[:, 5 + g % 2, h * XD:(h + 1) * XD], lambda k: prbT[:, u % 2, k],
                                 lambda k: mkv[:, 1, k, h * XD:(h + 1) * XD], L // P)
                last.then_inc(at_pv, 1)

            def att_out(g):
                pe.wait_ge(at_oe, g + 1)
                if g >= 1:
                    pe.wait_ge(at_xe, g)
                for c in range(4):
                    last = turn(bank[:, 7, c * P:(c + 1) * P], otm[:, g % 2, c * P:(c + 1) * P], P)
                last.then_inc(at_xm, 1)

            pe.wait_ge(kv_ev, 14)
            pe.wait_ge(krk_done, 1)
            for u in range(len(ATT) + 4):
                if u < len(ATT):
                    att_scores(u)
                if 1 <= u <= len(ATT):
                    att_turn(u - 1)
                if 2 <= u <= len(ATT) + 1:
                    att_values(u - 2)
                for g, (_, _, _, end) in enumerate(GROUPS):
                    if u - 4 + 1 == end + 1:
                        att_out(g)

            pe.wait_ge(at_xe, len(GROUPS))
            for n in range(3 * DK):
                f, i = n // 3, n % 3
                if i == 0:
                    pe.wait_ge(ld_mg[f % 2], 16 * 6 * (f // 2 + 1))
                if n >= 2:
                    pe.wait_ge(mg_ev, n - 1)
                src = (pyT, moT, xoT)[i]
                for half in range(2):
                    span = slice(half * HALF, (half + 1) * HALF)
                    sum_k(bank[:, 4 * (n % 2) + half, 0:HALF], lambda k: wmg[:, f % 2, i, k],
                          lambda k: xnT[:, k, span], DK)
                for half in range(2):
                    span = slice(half * HALF, (half + 1) * HALF)
                    last = sum_k(bank[:, 4 * (n % 2) + 2 + half, 0:HALF], lambda k: wmg[:, f % 2, i, 8 + k],
                                 lambda k: src[:, k, span], 4)
                last.then_inc(mg_mm, 1)
            pe.wait_ge(mg_ev, 3 * DK)
            pe.wait_ge(ld_wo, 48)
            for t in range(TILES + 1):
                if t < TILES:
                    for c in range(2):
                        n = 2 * t + c
                        if n >= 4:
                            pe.wait_ge(wo_ev, n - 3)
                        sum_k(bank[0:rows(t), n % 4], lambda k: mgT[:, k, cols(t)],
                              lambda k: wo[:, k, c * 512:(c + 1) * 512], DK).then_inc(wo_mm, 1)
                if t >= 1:
                    r = rows(t - 1)
                    pe.wait_ge(h_norm, t)
                    for c in range(2):
                        n = 2 * (t - 1) + c
                        if n >= 4:
                            pe.wait_ge(hT_ev, n - 3)
                        for k in range(4):
                            last = turn(bank[:, 4 + n % 4, k * P:k * P + r],
                                        hn[0:r, slot(t - 1), (4 * c + k) * P:(4 * c + k + 1) * P], r)
                        last.then_inc(hT_mm, 1)
            pe.wait_ge(ld_keys, 32)
            pe.wait_ge(wo_ev, 2 * TILES)
            for a in range(2):
                last = turn(bank[:, 0, a * P:(a + 1) * P], keys[:, a], P)
            last.then_inc(key_mm, 1)
            pe.wait_ge(key_ev, 1)
            pe.wait_ge(hT_ev, 2 * TILES)
            for j in range(17):
                if j < 16:
                    pe.wait_ge(ld_pq[j % 4], 16 * (j // 4 + 1))
                    if j >= 2:
                        pe.wait_ge(pq_ev, j - 1)
                    for half in range(2):
                        last = sum_k(bank[:, 2 * (j % 2) + half, 0:HALF], lambda k: wpq[:, j % 4, k],
                                     lambda k: hnT[:, k, half * HALF:(half + 1) * HALF], DK)
                    last.then_inc(pq_mm, 1)
                if j >= 1:
                    i = j - 1
                    pe.wait_ge(pq_ev, i + 1)
                    if i >= 2:
                        pe.wait_ge(sc_ev, i - 1)
                    for t in range(1, TILES):
                        pe.matmul(bank[:, 4 + 2 * (i % 2), (t - 1) * P:t * P], qp[:, i % 2, cols(t)],
                                  keysT[:, i % 2], start=True, stop=True)
                    pe.matmul(bank[0:NS, 5 + 2 * (i % 2), 0:P], qp[:, i % 2, 0:NS], keysT[:, i % 2],
                              start=True, stop=True).then_inc(sc_mm, 1)

            def weigh(it, b):
                pe.wait_ge(acc_free, it * 2 + (b + 1))
                for k in range(16):
                    pe.wait_ge(diag_done, it * 32 + (16 * b + k + 1))
                    pe.wait_ge(v_in[k % RING], it * 64 + 16 * (2 * b + k // RING + 1))
                    for c in range(2):
                        last = pe.matmul(bank[:, 2 * b + c], diag[:, k], vring[:, k % RING, c * 512:(c + 1) * 512],
                                         start=(k == 0), stop=(k == 15))
                    last.then_inc(v_free, 1)

            with nc.tensor.Fori(0, ITS) as it:
                weigh(it, 0)
                weigh(it, 1)

        @block.scalar
        def _(act):
            chain = 0

            def link(ins):
                nonlocal chain
                chain += 1
                ins.then_inc(act_chain, 1)
                act.wait_ge(act_chain, chain)

            def copy(dst, src, scale=1.0):
                return act.activation(dst, src, ACT.Copy, scale=scale)

            def root_mean(r, col, src, width):
                link(act.activation(junk[0:r, 0:width], src, ACT.Square, accum_out=ss[0:r, col:col + 1]))
                return act.activation(std[0:r, col:col + 1], ss[0:r, col:col + 1], ACT.Sqrt, scale=1.0 / width,
                                      bias=eps[0:r])

            act.wait_ge(zeroed, 5)

            def squares(i):
                act.wait_ge(ld_x[i % 3], 16 * (i // 3 + 1))
                r = NS if i == 0 else P
                root_mean(r, i, xin[0:r, i % 3], D).then_inc(sqrt_done, 1)

            def stream_out(n):
                j, what, c, w, m = UNITS[n]
                act.wait_ge(st_mm, n + 1)
                b = 4 + n % 4
                if what == "qkv":
                    last = copy(cqkv[0:rows(m), m, c:c + w], bank[0:rows(m), b, 0:w])
                elif what == "qx":
                    last = copy(qxT[:, c, m * HALF:(m + 1) * HALF], bank[:, b, 0:HALF])
                elif what == "u":
                    if m == 0:
                        copy(uS[:, c, :, HIST:HIST + TS], bank[:, b, 0:NS].rearrange("p (b t) -> p b t", t=TS))
                        copy(unew[:, c], bank[:, b, 0:NS])
                        last = copy(uP[:, c, HIST:HIST + HALF - NS], bank[:, b, NS:HALF])
                    else:
                        last = copy(uP[:, c, HIST + HALF - NS:HIST + SEQ], bank[:, b, 0:HALF])
                else:
                    last = copy(mkv[:, 0 if what == "mk" else 1, m, c:c + w], bank[:, b, 0:w])
                last.then_inc(st_ev, 1)

            for i in range(3):
                squares(i)
            for i in range(3, 7):
                squares(i)
                stream_out(i - 3)
            for n in range(4, LAST_QKV + 1):
                stream_out(n)
            act.wait_ge(st_ev, LAST_QKV + 1)
            for t in range(TILES):
                root_mean(rows(t), 0, cqkv[0:rows(t), t, 0:QL], QL).then_inc(q_sqrt, 1)
                act.wait_ge(q_sqrt, 2 * t + 1)
                act.wait_ge(rstd_read, 2 * t + 1)
                root_mean(rows(t), 0, cqkv[0:rows(t), t, QL:QL + KL], KL).then_inc(q_sqrt, 1)
                act.wait_ge(rstd_read, 2 * t + 2)
            for n in range(LAST_QKV + 1, LAST_U + 1):
                stream_out(n)

            def out_c(t):
                r = rows(t)
                act.wait_ge(c_mm, 2 * (t + 1))
                b = 2 * (t % 2) + 1
                copy(cT[:, :, cols(t)], bank[:, b, 0:2 * P].rearrange("p (k r) -> p k r", k=2)[:, :, 0:r])
                copy(krT[NOPE:QD, cols(t)], bank[NOPE:QD, b, 2 * P:2 * P + r]).then_inc(c_ev_a, 1)

            rest = list(range(LAST_U + 1, len(UNITS)))
            for t in range(TILES):
                stream_out(rest[t])
                out_c(t)
            for n in rest[TILES:]:
                stream_out(n)
            for t in range(TILES + 1):
                if t < TILES:
                    r = rows(t)
                    if t >= 2:
                        act.wait_ge(qt_mm, 2 * (t - 1))
                    for c in range(2):
                        n = 2 * t + c
                        act.wait_ge(qu_mm, n + 1)
                        copy(qtm[0:r, t % 2, c * 384:(c + 1) * 384], bank[0:r, 4 + n % 4, 0:384]).then_inc(qu_ev, 1)
                if t >= 1:
                    r = rows(t - 1)
                    for c in range(2):
                        n = 2 * (t - 1) + c
                        act.wait_ge(qt_mm, n + 1)
                        copy(qT[0:QD, 4 * c:4 * c + 4, cols(t - 1)],
                             bank[0:QD, n % 4].rearrange("p (k r) -> p k r", k=4)[:, :, 0:r]).then_inc(qt_ev, 1)
            act.wait_ge(hi_mm, 1)
            for g in range(PG):
                last = copy(uS[:, g, :, 0:HIST], bank[:, 0, g * P:g * P + NB * HIST].rearrange("p (b t) -> p b t", b=NB))
            last.then_inc(hi_ev, 1)
            for n in range(2 * PG):
                act.wait_ge(pool_mm, n + 1)
                act.activation(pyT[:, n // 2, (n % 2) * HALF:(n % 2 + 1) * HALF], bank[:, 4 + n % 4, 0:HALF], ACT.Copy,
                               scale=pscale[:, n // 2:n // 2 + 1]).then_inc(pool_ev, 1)
            for n in range(4):
                act.wait_ge(uk_mm, n + 1)
                copy(wukT[0:NOPE, 2 * n:2 * n + 2].rearrange("p a b -> p (a b)"), bank[0:NOPE, n]).then_inc(uk_ev, 1)
            act.wait_ge(ql_mm, 1)
            for c in range(2):
                src = bank[:, 4].rearrange("p (h c b t) -> p c b h t", h=H, c=2, b=NB)[:, c]
                copy(qlat[:, c], src).then_inc(ql_ev, 1)

            def turn_out(n):
                act.wait_ge(pt_mm, 3 * n + 1)
                if n >= 2:
                    act.wait_ge(ps_mm, 5 * ((n - 2) // 4) + (n - 2) % 4 + 1)
                copy(latT[:, n % 2, 0], bank[:, 0]).then_inc(pt_ev, 1)

            def score_out(b, g):
                m = 5 * b + g
                act.wait_ge(ps_mm, m + 1)
                w = 512 if g < 4 else NS
                copy(scor[0:NS, g * 512:g * 512 + w], bank[0:NS, 3 + m % 2, 0:w]).then_inc(ps_ev, 1)

            act.wait_ge(st_pool, 16 * (NB + 1))
            def page_exp(b):
                act.wait_ge(ps_max, b + 1)
                if b >= 1:
                    act.wait_ge(pp_mm, 2 * b)
                act.activation(prob[0:NS], scor[0:NS], ACT.Exp, scale=MLA_SCALE, bias=smx[0:NS, b:b + 1],
                               accum_out=ssum[0:NS, b:b + 1]).then_inc(ps_exp, 1)

            for b in range(NB + 1):
                if b < NB:
                    turn_out(4 * b)
                    turn_out(4 * b + 1)
                if b >= 1:
                    page_exp(b - 1)
                if b < NB:
                    if b >= 1:
                        act.wait_ge(ps_exp, b)
                    score_out(b, 0)
                    turn_out(4 * b + 2)
                    score_out(b, 1)
                    turn_out(4 * b + 3)
                    for g in range(2, 5):
                        score_out(b, g)
            act.wait_ge(sot_mm, 1)
            copy(moT[:, :, 0:NS], bank[:, 4, 0:4 * NS].rearrange("p (c n) -> p c n", c=4)).then_inc(sot_ev, 1)

            def mem_keys_out(b):
                if b >= 1:
                    act.wait_ge(ms_mm, b)
                for i in range(2):
                    act.wait_ge(mt_mm, 2 * b + i + 1)
                    copy(smT[:, 2 * i:2 * i + 2].rearrange("p a b -> p (a b)"), bank[:, i]).then_inc(mt_ev, 1)

            mem_keys_out(0)
            for b in range(NB + 2):
                if b < NB:
                    act.wait_ge(ms_max, b + 1)
                    if b >= 1:
                        act.wait_ge(mp_mm, b)
                    for h in range(XH):
                        act.activation(sms[0:TS, h], bank[0:TS, 2 + h // 2, (h % 2) * MEM:(h % 2 + 1) * MEM], ACT.Exp,
                                       scale=MEM_SCALE, bias=mmx[0:TS, h:h + 1],
                                       accum_out=msum[0:TS, 4 * (b % 2) + h:4 * (b % 2) + h + 1]).then_inc(ms_exp, 1)
                if b + 1 < NB:
                    mem_keys_out(b + 1)
                if b >= 2:
                    act.wait_ge(mx_mm, b - 1)
                    copy(xoT[:, :, (b - 2) * TS:(b - 1) * TS], bank[:, 7, 0:4 * TS].rearrange("p (c n) -> p c n", c=4)).then_inc(
                        mx_ev, 1)

            for n in range(14):
                act.wait_ge(kv_mm, n + 1)
                if n < 2:
                    dst, r = mkT[:, 2 * n:2 * n + 2].rearrange("p a b -> p (a b)"), P
                elif n < 10:
                    dst, r = kT[0:NOPE, n - 2], NOPE
                else:
                    dst, r = vtm[:, n - 10], P
                copy(dst, bank[0:r, n % 8]).then_inc(kv_ev, 1)

            for u in range(len(ATT) + 5):
                if u < len(ATT):
                    kind, q, h, L = ATT[u]
                    act.wait_ge(at_max, u + 1)
                    if u >= 3:
                        act.wait_ge(at_tm, u - 2)
                    act.activation(prb[:, u % 3, 0:L], bank[:, u % 3, 0:L], ACT.Exp,
                                   scale=MLA_SCALE if kind == "mla" else MEM_SCALE, bias=nmax[:, u:u + 1],
                                   accum_out=rsum[:, u:u + 1]).then_inc(at_exp, 1)
                if 1 <= u <= len(ATT):
                    L = ATT[u - 1][3]
                    act.wait_ge(at_tm, u)
                    if u >= 3:
                        act.wait_ge(at_pv, u - 2)
                    copy(prbT[:, (u - 1) % 2, 0:L // P].rearrange("p a b -> p (a b)"),
                         bank[:, 3 + (u - 1) % 2, 0:L]).then_inc(at_te, 1)
                for g, (kind, q, _, end) in enumerate(GROUPS):
                    if u - 4 == end + 1:
                        act.wait_ge(at_xm, g + 1)
                        dst = moT if kind == "mla" else xoT
                        copy(dst[:, :, cols(q + 1)], bank[:, 7].rearrange("p (c n) -> p c n", c=4)).then_inc(at_xe, 1)

            for n in range(3 * DK):
                act.wait_ge(mg_mm, n + 1)
                if n >= 2:
                    act.wait_ge(mg_ev, n - 1)
                b = 4 * (n % 2)
                act.activation(sig[:, n % 2], bank[:, b:b + 2, 0:HALF], ACT.Sigmoid).then_inc(mg_sig, 1)

            for t in range(TILES + 1):
                if t < TILES:
                    act.wait_ge(wo_ev, 2 * (t + 1))
                    if t >= 1:
                        act.wait_ge(h_norm, t)
                    root_mean(rows(t), 0, hall[0:rows(t), slot(t)], D).then_inc(h_sqrt, 1)
                if t >= 1:
                    r = rows(t - 1)
                    for c in range(2):
                        n = 2 * (t - 1) + c
                        act.wait_ge(hT_mm, n + 1)
                        copy(hnT[:, 4 * c:4 * c + 4, cols(t - 1)],
                             bank[:, 4 + n % 4].rearrange("p (k r) -> p k r", k=4)[:, :, 0:r]).then_inc(hT_ev, 1)
            act.wait_ge(key_mm, 1)
            copy(keysT.rearrange("p a b -> p (a b)"), bank[:, 0, 0:2 * P]).then_inc(key_ev, 1)
            def query_out(j):
                act.wait_ge(pq_mm, j + 1)
                if j >= 2:
                    act.wait_ge(sc_mm, j - 1)
                copy(qp[:, j % 2].rearrange("p (a b) -> p a b", a=2),
                     bank[:, 2 * (j % 2):2 * (j % 2) + 2, 0:HALF]).then_inc(pq_ev, 1)

            def scores_out(j):
                pair, s = j // 4, j % 4
                b = 4 + 2 * (j % 2)
                act.wait_ge(sc_mm, j + 1)
                copy(scores[:, 4 * pair:4 * pair + 4, s], bank[:, b].rearrange("p (t k) -> p t k", t=4))
                copy(scores[32 * pair:32 * pair + 32, ITS - 1, s], bank[0:NS, b + 1, 0:P]).then_inc(
                    sc_ev, 1 if j < 15 else 5)

            def picked_exp(n):
                act.wait_ge(tk_gap, n)
                act.activation(gexp[:], top[:], ACT.Exp).then_inc(tk_exp, 1)

            def diagonals(it, b, last_step=False):
                act.wait_ge(w_done, it * 2 + (b + 1))
                for k in range(16):
                    act.wait_ge(v_free, it * 32 + (16 * b + k + 1))
                    act.sem_inc(carrier, 1)
                    act.activation(diag[:, k], ident[:, 1 if last_step else 0], ACT.Copy,
                                   scale=wts[:, k:k + 1]).then_inc(diag_done, 1)

            def tile_copy(dst, it, done):
                act.sem_inc(carrier, 1)
                act.activation(dst, hn[:, DynSlice((it + 1) % 4, 1)].rearrange("p a d -> p (a d)") if not isinstance(it, int) else hn[:, slot(0)], ACT.Copy).then_inc(done, 1)

            def turn_queries(j0, j1):
                for j in range(j0, j1):
                    if j < 16:
                        query_out(j)
                    if j >= 1:
                        scores_out(j - 1)

            act.wait_ge(hn_rep, 1)
            copy(hA[:], hn[:, 0]).then_inc(h_a, 1)
            copy(hB[:], hn[:, 0]).then_inc(h_b, 1)
            turn_queries(0, PICK_AT)
            picked_exp(1)
            turn_queries(PICK_AT, GELU_AT)
            act.wait_ge(u_free, RING + 16)
            act.activation(act_g[:], act_a[:], ACT.Gelu).then_inc(gelu_done, 1)
            turn_queries(GELU_AT, 17)
            def one_step(it):
                diagonals(it, 0)
                tile_copy(hA[:], it, h_a)
                picked_exp(it + 2)
                act.wait_ge(u_free, it * 32 + (RING + 32))
                act.activation(act_g[:], act_a[:], ACT.Gelu).then_inc(gelu_done, 1)
                diagonals(it, 1)
                tile_copy(hB[:], it, h_b)
                act.wait_ge(u_free, it * 32 + (RING + 48))
                act.activation(act_g[:], act_a[:], ACT.Gelu).then_inc(gelu_done, 1)
            with nc.scalar.Fori(0, ITS - 2) as it:
                one_step(it)
            one_step(ITS - 2)
            last = ITS - 1
            diagonals(last, 0, True)
            act.wait_ge(u_free, last * 32 + (RING + 32))
            act.activation(act_g[:], act_a[:], ACT.Gelu).then_inc(gelu_done, 1)
            diagonals(last, 1, True)
            for n in range(TILES):
                t = (n + 1) % TILES
                act.wait_ge(acc_free, 2 * ITS + (2 if t == 0 else 0))
                if n >= 1:
                    act.wait_ge(f_out, n)
                root_mean(rows(t), 0, hall[0:rows(t), slot(t)], D).then_inc(f_sqrt, 1)

        @block.vector
        def _(dve):
            chain = 0

            def link(ins):
                nonlocal chain
                chain += 1
                ins.then_inc(dve_chain, 1)
                dve.wait_ge(dve_chain, chain)

            tt, ts, stt = dve.tensor_tensor, dve.tensor_scalar, dve.scalar_tensor_tensor

            dve.wait_ge(zeroed, 5)
            dve.wait_ge(ld_const, 48)

            def scale_x(i):
                r = NS if i == 0 else P
                dve.wait_ge(sqrt_done, i + 1)
                link(dve.reciprocal(rstd[0:r, i:i + 1], std[0:r, i:i + 1]))
                ts(xin[0:r, i % 3], xin[0:r, i % 3], rstd[0:r, i:i + 1], None, ALU.mult).then_inc(xs_done, 1)

            def out_x(i):
                r = NS if i == 0 else P
                for c in range(2):
                    n = 2 * i + c
                    dve.wait_ge(xT_mm, n + 1)
                    src = bank[:, n % 4].rearrange("p (k r) -> p k r", k=4)[:, :, 0:r]
                    g = (gattn if i < TILES else gmem)[:, 4 * c:4 * c + 4].unsqueeze(2).to_broadcast([P, 4, r])
                    dst = xnT[:, 4 * c:4 * c + 4, cols(i)] if i < TILES else \
                        mnT[:, 4 * c:4 * c + 4, (i - TILES) * P:(i - TILES + 1) * P]
                    tt(dst, src, g, ALU.mult).then_inc(xT_ev, 1)

            for i in range(8):
                if i < 7:
                    scale_x(i)
                if i >= 1:
                    out_x(i - 1)

            dve.wait_ge(ld_gain, 16 * 11)
            for t in range(TILES):
                r = rows(t)
                dve.wait_ge(q_sqrt, 2 * t + 1)
                dve.reciprocal(rstd[0:r, 0:1], std[0:r, 0:1]).then_inc(rstd_read, 1)
                dve.wait_ge(rstd_read, 2 * t + 1)
                ts(cqkv[0:r, t, 0:QL], cqkv[0:r, t, 0:QL], rstd[0:r, 0:1], None, ALU.mult).then_inc(q_norm_done, 1)
                dve.wait_ge(q_sqrt, 2 * t + 2)
                dve.reciprocal(rstd[0:r, 1:2], std[0:r, 0:1]).then_inc(rstd_read, 1)
                dve.wait_ge(rstd_read, 2 * t + 2)
                stt(cqkv[0:r, t, QL:QL + KL], cqkv[0:r, t, QL:QL + KL], rstd[0:r, 1:2], gkv[0:r], ALU.mult,
                    ALU.mult).then_inc(q_norm_done, 1)

            def rope(dst, src, cos, sin, ta, tb):
                half = ROPE // 2
                x1, x2 = src[..., 0:half], src[..., half:ROPE]
                tt(ta[..., 0:half], x1, cos, ALU.mult)
                tt(ta[..., half:ROPE], x2, cos, ALU.mult)
                tt(tb[..., 0:half], x2, sin, ALU.mult)
                link(tt(tb[..., half:ROPE], x1, sin, ALU.mult))
                tt(dst[..., 0:half], ta[..., 0:half], tb[..., 0:half], ALU.subtract)
                return tt(dst[..., half:ROPE], ta[..., half:ROPE], tb[..., half:ROPE], ALU.add)

            rope(krp[:, :, NOPE:QD], cqkv[:, :, QL + KL:QL + KL + ROPE], trig[:, :, 0:16], trig[:, :, 16:32],
                 rot_a[:, 0:TILES], rot_b[:, 0:TILES]).then_inc(kr_done, 1)
            for t in range(TILES):
                r = rows(t)
                dve.wait_ge(c_mm, 2 * t + 1)
                src = bank[:, 2 * (t % 2), 0:3 * P].rearrange("p (k r) -> p k r", k=3)[:, :, 0:r]
                tt(qnT[:, :, cols(t)], src, gq.unsqueeze(2).to_broadcast([P, 3, r]), ALU.mult).then_inc(c_ev_d, 1)
            for t in range(TILES):
                r = rows(t)
                dve.wait_ge(qu_ev, 2 * (t + 1))
                q = qtm[0:r, t % 2].rearrange("p (h e) -> p h e", h=H)[:, :, NOPE:QD]
                cs = [trig[0:r, t, 16 * k:16 * k + 16].unsqueeze(1).to_broadcast([r, H, 16]) for k in range(2)]
                dve.wait_ge(*((qu_rope, t) if t else (kr_done, 1)))
                rope(q, q, cs[0], cs[1], rot_a[0:r], rot_b[0:r]).then_inc(qu_rope, 1)
            for k, r in enumerate((NS, HIST)):
                dve.wait_ge(uo_mm, k + 1)
                dve.tensor_copy(uout[0:r, k], bank[0:r, 1 + k]).then_inc(uo_ev, 1)
            dve.wait_ge(hi_ev, 1)
            dve.wait_ge(st_mm, len(UNITS))
            dve.wait_ge(qu_mm, 2 * TILES)
            for g in range(PG):
                n, w = HIST + SEQ, 2 << g
                sP, sS = uP[:, g], uS[:, g]
                if g:
                    dve.wait_ge(pool_d, g)
                for step in range(g + 1):
                    sh = 1 << step
                    lo = 2 * sh - 1
                    dP, dS = ((psum_a, ssum_a), (psum_b, ssum_b))[step % 2]
                    tt(dP[:, lo:n], sP[:, lo:n], sP[:, lo - sh:n - sh], ALU.add)
                    link(tt(dS[:, :, lo:], sS[:, :, lo:], sS[:, :, lo - sh:HIST + TS - sh], ALU.add))
                    sP, sS = dP, dS
                link(tt(sP[:, HIST:HIST + 16], sP[:, HIST:HIST + 16], cntfix[:, g], ALU.mult))
                stt(dT[:, g, NS:NT], sP[:, HIST:n], 1.0 / w, uP[:, g, HIST:n], ALU.mult, ALU.subtract)
                stt(dT[:, g, 0:NS].rearrange("p (b t) -> p b t", b=NB), sS[:, :, HIST:], 1.0 / w,
                    uS[:, g, :, HIST:], ALU.mult, ALU.subtract).then_inc(pool_d, 1)
            dve.wait_ge(qt_ev, 2 * TILES)
            dve.wait_ge(c_ev_a, TILES)
            dve.wait_ge(pool_mm, 2 * PG)
            dve.tensor_copy(qrot[NOPE:QD], qT[NOPE:QD, :, 0:NS].rearrange("p h (b t) -> p b h t", b=NB)).then_inc(ql_ev, 1)

            dve.wait_ge(st_pool, 16 * (NB + 1))
            def keys_out(b, g):
                n = 4 * b + g
                dve.wait_ge(pt_mm, 3 * n + 2)
                if n >= 2:
                    dve.wait_ge(ps_mm, 5 * ((n - 2) // 4) + (n - 2) % 4 + 1)
                dve.tensor_copy(latT[:, n % 2, 1], bank[:, 1]).then_inc(pt_ed, 1)
                dve.wait_ge(pt_mm, 3 * n + 3)
                dve.tensor_copy(krpT[NOPE:QD, n % 2], bank[NOPE:QD, 2]).then_inc(pt_ed, 1)

            def largest(b):
                dve.wait_ge(ps_ev, 5 * (b + 1))
                new = scor[0:NS, PAGES * PAGE:PAGES * PAGE + NS]
                link(tt(new, new, smask[0:NS, b], ALU.add))
                link(dve.reduce_max(smx0[0:NS, b:b + 1], scor[0:NS], AX_X))
                ts(smx[0:NS, b:b + 1], smx0[0:NS, b:b + 1], -MLA_SCALE, None, ALU.mult).then_inc(ps_max, 1)

            for b in range(NB + 1):
                a = b - 1
                if b < NB:
                    keys_out(b, 0)
                if b >= 1:
                    largest(a)
                if b < NB:
                    keys_out(b, 1)
                    keys_out(b, 2)
                if b >= 1:
                    dve.wait_ge(pp_mm, 2 * a + 1)
                    if a >= 1:
                        dve.wait_ge(pv_mm, a)
                    dve.tensor_copy(probT[:, 0:PAGES].rearrange("p a b -> p (a b)"), bank[:, 5]).then_inc(pp_ev, 1)
                    dve.wait_ge(pp_mm, 2 * a + 2)
                    dve.tensor_copy(probT[0:NS, PAGES], bank[0:NS, 6, 0:NS]).then_inc(pp_ev, 1)
                if b < NB:
                    keys_out(b, 3)
                if b >= 1:
                    link(dve.reciprocal(srec[0:NS, a:a + 1], ssum[0:NS, a:a + 1]))
                    dve.wait_ge(pv_mm, a + 1)
                    ts(olat[0:NS], bank[0:NS, 7, 0:KL], srec[0:NS, a:a + 1], None, ALU.mult).then_inc(pv_ev, 1)
                    dve.wait_ge(po_mm, a + 1)
                    dve.tensor_copy(olatT[:, :, :, a], bank[:, 6, 64:64 + 2 * NS].rearrange(
                        "p (c h t) -> p c h t", c=2, h=H)).then_inc(po_ev, 1)
            dve.wait_ge(so_mm, 1)
            dve.tensor_copy(osmp[0:NS], bank[0:NS, 3]).then_inc(so_ev, 1)

            for b in range(NB + 1):
                if b < NB:
                    dve.wait_ge(ms_mm, b + 1)
                    link(dve.reduce_max(mmx0[0:TS], bank[0:TS, 2:4].rearrange("p a (h m) -> p (a h) m", h=2), AX_X))
                    if b >= 1:
                        dve.wait_ge(ms_exp, XH * b)
                    ts(mmx[0:TS], mmx0[0:TS], -MEM_SCALE, None, ALU.mult).then_inc(ms_max, 1)
                if b >= 1:
                    dve.wait_ge(mp_mm, b)
                    if b >= 2:
                        dve.wait_ge(mo_mm, b - 1)
                    dve.tensor_copy(smpT.rearrange("p h m t -> p (h m t)"), bank[:, 5, 0:XH * 2 * TS]).then_inc(mp_ev, 1)
                    s = 4 * ((b - 1) % 2)
                    if b >= 2:
                        dve.wait_ge(mo_ev, b - 1)
                    link(dve.reciprocal(mrec[0:TS], msum[0:TS, s:s + 4]))
                    dve.wait_ge(mo_mm, b)
                    if b >= 2:
                        dve.wait_ge(mx_mm, b - 1)
                    tt(smo[0:TS].rearrange("p (h e) -> p h e", h=XH), bank[0:TS, 6].rearrange("p (h e) -> p h e", h=XH),
                       mrec[0:TS].unsqueeze(2).to_broadcast([TS, XH, XD]), ALU.mult).then_inc(mo_ev, 1)

            dve.wait_ge(kv_mm, 2)
            dve.tensor_copy(kT[NOPE:QD], krT[NOPE:QD, NS:NT].unsqueeze(1).to_broadcast([ROPE, H, SEQ])).then_inc(krk_done, 1)

            for u in range(len(ATT) + 3):
                if u < len(ATT):
                    kind, q, h, L = ATT[u]
                    dve.wait_ge(at_mm, u + 1)
                    if kind == "mla":
                        d = bank[:, u % 3, L - P:L]
                        link(tt(d, d, causal[:], ALU.add))
                    link(dve.reduce_max(nmax0[:, u:u + 1], bank[:, u % 3, 0:L], AX_X))
                    ts(nmax[:, u:u + 1], nmax0[:, u:u + 1], -(MLA_SCALE if kind == "mla" else MEM_SCALE), None,
                       ALU.mult).then_inc(at_max, 1)
                for g, (kind, q, first, end) in enumerate(GROUPS):
                    if u - 3 == end:
                        n = end - first + 1
                        dve.wait_ge(at_exp, end + 1)
                        link(dve.reciprocal(rinv[:, first:end + 1], rsum[:, first:end + 1]))
                        dve.wait_ge(at_pv, end + 1)
                        if g >= 2:
                            dve.wait_ge(at_xm, g - 1)
                        tt(otm[:, g % 2].rearrange("p (h e) -> p h e", h=n),
                           bank[:, 5 + g % 2].rearrange("p (h e) -> p h e", h=n),
                           rinv[:, first:end + 1].unsqueeze(2).to_broadcast([P, n, 512 // n]), ALU.mult).then_inc(at_oe, 1)

            for n in range(3 * DK):
                f, i = n // 3, n % 3
                dve.wait_ge(mg_sig, n + 1)
                b = 4 * (n % 2) + 2
                out = mgT[:, f].rearrange("p (a b) -> p a b", a=2)
                if i == 0:
                    if f == 0:
                        dve.wait_ge(st_lat, 16 * 4)
                    tt(out, sig[:, n % 2], bank[:, b:b + 2, 0:HALF], ALU.mult).then_inc(mg_ev, 1)
                    dve.wait_ge(mg_ev, n + 1)
                else:
                    link(tt(mtmp[:], sig[:, n % 2], bank[:, b:b + 2, 0:HALF], ALU.mult))
                    tt(out, out, mtmp[:], ALU.add).then_inc(mg_ev, 1)
                    dve.wait_ge(mg_ev, n + 1)
            dve.wait_ge(ld_wo, 48)
            for q in range(1, 4):
                dve.memset(hall[32 * q:32 * q + 32, slot(0)], 0.0)
            for t in range(TILES + 1):
                if t < TILES:
                    r = rows(t)
                    for c in range(2):
                        n = 2 * t + c
                        dve.wait_ge(wo_mm, n + 1)
                        part = hall[0:r, slot(t), c * 512:(c + 1) * 512]
                        tt(part, part, bank[0:r, n % 4], ALU.add).then_inc(wo_ev, 1)
                if t >= 1:
                    r = rows(t - 1)
                    dve.wait_ge(h_sqrt, t)
                    link(dve.reciprocal(rstd[0:r, t:t + 1], std[0:r, 0:1]))
                    stt(hn[0:r, slot(t - 1)], hall[0:r, slot(t - 1)], rstd[0:r, t:t + 1], gffn[0:r], ALU.mult, ALU.mult).then_inc(
                        h_norm, 1)
            dve.wait_ge(h_norm, 1)
            for q in range(1, 4):
                last = dve.tensor_copy(hn[32 * q:32 * q + 32, slot(0)], hn[0:32, slot(0)])
            last.then_inc(hn_rep, 1)
            def step(ins):
                dve.drain()

            def top16(values, indices, source):
                step(dve.max(values[:, 0:8], source))
                step(dve.max_index(indices[:, 0:8], values[:, 0:8], source))
                step(dve.match_replace(source, values[:, 0:8], source, NEG))
                step(dve.max(values[:, 8:16], source))
                step(dve.max_index(indices[:, 8:16], values[:, 8:16], source))

            def pick_sides(at_step):
                step(dve.tensor_copy(sc.rearrange("p a b -> p (a b)"),
                                     scores[:, DynSlice(at_step, 1)].rearrange("p x a b -> p (x a b)")))
                for q in range(4):
                    top16(val[:, q], vix[:, q], sc[:, q])
                step(dve.tensor_copy(vixf[:], vix[:]))

            def pick_pairs(n):
                for h in range(2):
                    step(tt(cand[:, h].rearrange("p (a b) -> p a b", a=16), val[:, 2 * h].unsqueeze(2).to_broadcast([P, 16, 16]),
                            val[:, 2 * h + 1].unsqueeze(1).to_broadcast([P, 16, 16]), ALU.add))
                for h in range(2):
                    top16(top0[:, h], sel[:, h], cand[:, h])
                tt(top[:], top0[:], top0[:, :, 0:1].to_broadcast([P, 2, 16]), ALU.subtract).then_inc(tk_gap, 1)
                ts(sela[:], sel[:], 4, None, ALU.logical_shift_right)
                step(ts(selb[:], sel[:], 15, None, ALU.bitwise_and))
                dve.tensor_copy(selaf[:], sela[:])
                step(dve.tensor_copy(selbf[:], selb[:]))
                for side, pos, dst in ((0, selaf, e1), (1, selbf, e2)):
                    step(tt(onehot[:], pos.rearrange("p a b -> p (a b)").unsqueeze(2).to_broadcast([P, 32, 16]),
                            iota16.unsqueeze(1).to_broadcast([P, 32, 16]), ALU.is_equal))
                    for h in range(2):
                        part = onehot[:, 16 * h:16 * h + 16]
                        last = tt(part, part, vixf[:, 2 * h + side].unsqueeze(1).to_broadcast([P, 16, 16]), ALU.mult)
                    step(last)
                    step(dve.reduce_sum(dst.rearrange("p a b -> p (a b)"), onehot[:], AX_X))
                stt(idN[:].rearrange("p (a b) -> p a b", a=2), e1[:], float(NKEY), e2[:], ALU.mult, ALU.add).then_inc(id_next, 1)
                dve.wait_ge(tk_exp, n)
                step(dve.reduce_sum(gs2[:, 0:2], gexp[:], AX_X))
                step(dve.reciprocal(gr2[:, 0:2], gs2[:, 0:2]))
                step(tt(gN.rearrange("p (a b) -> p a b", a=2), gexp[:], gr2[:, 0:2].unsqueeze(2).to_broadcast([P, 2, 16]),
                        ALU.mult))

            def products(land0, h, ready, n, k0=0, k1=16):
                if k0 == 0:
                    dve.wait_ge(ready, n)
                for k in range(k0, k1):
                    dve.wait_ge(u_in[k % RING], land0 + U0 + 16 * (k // RING + 1))
                    dve.tensor_tensor_reduce(uring[:, k % RING], uring[:, k % RING], h[:], 1.0, 0.0, ALU.mult, ALU.add,
                                             act_a[:, k:k + 1]).then_inc(u_free, 1)

            def weights(n, diags, gates):
                dve.wait_ge(gelu_done, n)
                if diags is not None:
                    dve.wait_ge(diag_done, diags)
                tt(wts[:], act_g[:], gates, ALU.mult).then_inc(w_done, 1)

            def add_sum(it, b):
                dve.wait_ge(v_free, it * 32 + 16 * (b + 2))
                dve.wait_ge(acc_free, it * 2 + (b + 2))
                if isinstance(it, int):
                    y = hall[:, it % 4 if it < ITS - 1 else slot(0)]
                else:
                    y = hall[:, DynSlice(it % 4, 1)].rearrange("p a d -> p (a d)")
                tt(y, y, bank[:, 2 * b:2 * b + 2].rearrange("p a b -> p (a b)"), ALU.add).then_inc(acc_free, 1)

            def hand_over(n):
                dve.tensor_copy(idA[:], idN[:]).then_inc(id_a, 1)
                dve.tensor_copy(gB[:], gN[:, 16:32]).then_inc(g_b, 1)

            dve.wait_ge(sc_ev, 4)
            pick_sides(0)
            pick_pairs(1)
            hand_over(1)
            products(0, hA, h_a, 1)
            weights(1, None, gN[:, 0:16])
            dve.wait_ge(id_a, 1)
            dve.tensor_copy(idB[:], idA[:, 16:32]).then_inc(id_b, 1)
            def one_step(it):
                dve.wait_ge(w_done, it * 2 + 1)
                dve.wait_ge(sc_ev, (it + 1) // 4 * 4 + 4)
                dve.wait_ge(g_b, it + 1)
                pick_sides(it + 1)
                products(it * 64 + 32, hB, h_b, it + 1, 0, PICK_ROW)
                pick_pairs(it + 2)
                products(it * 64 + 32, hB, h_b, it + 1, PICK_ROW, 16)
                weights(it * 2 + 2, it * 32 + 16, gB[:])
                add_sum(it, 0)
                dve.wait_ge(w_done, it * 2 + 2)
                hand_over(0)
                products(it * 64 + 64, hA, h_a, it + 2)
                weights(it * 2 + 3, it * 32 + 32, gN[:, 0:16])
                add_sum(it, 1)
                dve.wait_ge(id_a, it + 2)
                dve.tensor_copy(idB[:], idA[:, 16:32]).then_inc(id_b, 1)
            with nc.vector.Fori(0, ITS - 2) as it:
                one_step(it)
            one_step(ITS - 2)
            last = ITS - 1
            products(last * 64 + 32, hB, h_b, last + 1)
            dve.wait_ge(g_b, last + 1)
            weights(last * 2 + 2, last * 32 + 16, gB[:])
            def final(n):
                t = (n + 1) % TILES
                r = rows(t)
                dve.wait_ge(f_sqrt, n + 1)
                link(dve.reciprocal(rstd[0:r, 8 + n % 2:9 + n % 2], std[0:r, 0:1]))
                if n >= 2:
                    dve.wait_ge(st_y[n % 2], 16 * (n // 2))
                stt(outb[0:r, n % 2], hall[0:r, slot(t)], rstd[0:r, 8 + n % 2:9 + n % 2], gfin[0:r], ALU.mult,
                    ALU.mult).then_inc(f_out, 1)

            for n in range(TILES - 1):
                final(n)
            add_sum(last, 0)
            add_sum(last, 1)
            final(TILES - 1)

_INS = ["x_prompt", "x_sample", "cache_kv_latent", "cache_k_rope", "state_pool", "cache_mem_k", "cache_mem_v",
        "page_table", "mem_prompt", "attn_norm", "w_in", "q_norm", "kv_norm", "w_q_up", "w_uk", "w_uv",
        "w_pool_grp", "pool_scale", "mem_norm", "w_mem_k", "w_mem_v", "w_pool_out", "w_mla_out", "w_x_out",
        "w_o", "ffn_norm", "w_peer_q", "peer_k1", "peer_k2", "peer_u", "peer_v", "final_norm"]
_OUTS = [(1, SEQ, D), (NB, TS, D), (1, 1, SEQ, KL), (1, 1, SEQ, ROPE), (1, 1, HIST, 512),
         (1, 1, MEM, XH, XD), (1, 1, MEM, XH, XD), (1, NB, TS, KL), (1, NB, TS, ROPE), (1, NB, HIST, 512)]


def shape_constants():
    import numpy as np
    f = np.float32
    p = np.arange(P)
    fold = ((p[:, None] % NS == p[None, :]) & (p[None, :] < NS)).astype(f)
    ident = np.stack([np.eye(P, dtype=f), fold])
    causal = np.where(p[None, :] <= p[:, None], 0.0, -1.0e30).astype(f)
    row_t, col = np.arange(NS) % TS, np.arange(NS)
    smask = np.full((NS, NB, NS), -1.0e30, f)
    for b in range(NB):
        own = (col[None, :] // TS == b) & (col[None, :] % TS <= row_t[:, None])
        smask[:, b][own] = 0.0
    inv = np.power(f(10000.0), -np.arange(16, dtype=f) / f(16)).astype(f)
    pos = np.zeros((TILES, P), f)
    pos[0, :NS] = 2048 + np.arange(NS) % TS
    pos[1:] = np.arange(SEQ).reshape(TILES - 1, P)
    ang = (pos[:, :, None] * inv).astype(f)
    trig = np.ascontiguousarray(np.concatenate([np.cos(ang), np.sin(ang)], -1).astype(f).transpose(1, 0, 2))
    w = np.array([2, 4, 8, 16], f)[:, None]
    cnt = np.broadcast_to((w / np.minimum(np.arange(16, dtype=f) + 1, w)).astype(f), (P, PG, 16)).copy()
    iota = np.broadcast_to(np.arange(16, dtype=f), (P, 16)).copy()
    return {"c_ident": ident, "c_causal": causal, "c_smask": smask, "c_trig": trig,
            "c_cnt": cnt, "c_iota": iota}


def kernel(**inputs):
    import numpy as _np
    import concourse.bacc as _bacc
    from concourse import mybir as _mybir
    from concourse.bass_utils import run_bass_kernel_spmd as _run

    nc = _bacc.Bacc("TRN2", target_bir_lowering=False, num_devices=1)
    arrays, args = {}, []
    for name in _INS:
        a = _np.ascontiguousarray(inputs[name])
        arrays[f"in_{name}_dram"] = a
        args.append(nc.dram_tensor(f"in_{name}_dram", a.shape, _mybir.dt.from_np(a.dtype), kind="ExternalInput").ap())
    for name, a in shape_constants().items():
        arrays[f"in_{name}_dram"] = a
        args.append(nc.dram_tensor(f"in_{name}_dram", a.shape, _mybir.dt.from_np(a.dtype), kind="ExternalInput").ap())
    for i, shape in enumerate(_OUTS):
        args.append(nc.dram_tensor(f"out_{i}_dram", shape, F32, kind="ExternalOutput").ap())
    hybrid_step(nc, *args)
    r = _run(nc, [arrays], core_ids=[0])
    return tuple(r.results[0][f"out_{i}_dram"] for i in range(len(_OUTS)))
```

```python
from contextlib import ExitStack

import concourse.bass as bass
from concourse import mybir
from concourse.bass import DynSlice, IndirectOffsetOnAxis

ALU = mybir.AluOpType
ACT = mybir.ActivationFunctionType
F32 = mybir.dt.float32
U32 = mybir.dt.uint32
AX_X = mybir.AxisListType.X

P = 128
D = 1024
DK = D // P
EPS = 1e-6
NS = 32
NB = 8
TS = 4
SEQ = 512
NT = NS + SEQ
HALF = NT // 2
TILES = 1 + SEQ // P
MEM = 256
HIST = 15
PG = 4
H = 8
NOPE, ROPE, VD = 64, 32, 64
QD = NOPE + ROPE
QL, KL = 384, 256
XH, XD = 4, 128
PAGES, PAGE = 16, 128
PGRP = 4
LATW = KL + ROPE
OFF_U, OFF_CQ, OFF_CKV, OFF_KR, OFF_QX, OFF_G = 0, 512, 896, 1152, 1184, 1696
EH, NKEY, TOPK = 8, 128, 16
ITS = 17
RING = 8
VCRED = 16 - RING
Q_LOADS = [0, 1, 2, 3] + list(range(16))
EARLY = 4
Q_STEPS = 6
PICK_ROW = 10
KV_UNITS = XH // 2 + H + SEQ // P
NEG = -3.0e38
MLA_SCALE = float(QD) ** -0.5
MEM_SCALE = float(XD) ** -0.5


def rows(t):
    return NS if t == 0 else P


def cols(t):
    return slice(0, NS) if t == 0 else slice(NS + (t - 1) * P, NS + t * P)


def slot(t):
    return (t - 1) % TILES


STREAM = [("qkv", 0, 256), ("qkv", 256, 256), ("qkv", 512, 160),
          ("u", 0, 256), ("u", 256, 256), ("qx", 0, 256), ("qx", 256, 256),
          ("mk", 0, 256), ("mk", 256, 256), ("mv", 0, 256), ("mv", 256, 256)]
WRING = 4


def stream_units():
    for j, (what, c, w) in enumerate(STREAM):
        if what == "qkv":
            for t in range(TILES):
                yield j, what, c, w, t
        elif what in ("u", "qx"):
            for f in range(w // P):
                for half in range(2):
                    yield j, what, c // P + f, f, half
        else:
            for m in range(2):
                yield j, what, c, w, m


UNITS = list(stream_units())
LAST_QKV = max(n for n, u in enumerate(UNITS) if u[1] == "qkv")
LAST_U = max(n for n, u in enumerate(UNITS) if u[1] == "u")
ATT = [("mla", q, h, P * (q + 1)) for q in range(4) for h in range(H)]
ATT += [("mem", q, h, MEM) for q in range(4) for h in range(XH)]


def att_groups():
    out = []
    for n, (kind, q, h, _) in enumerate(ATT):
        if h == 0:
            out.append([kind, q, n, n])
        out[-1][3] = n
    return out


GROUPS = att_groups()
GROUP_OF = {n: g for g, (_, _, a, b) in enumerate(GROUPS) for n in range(a, b + 1)}


def hybrid_step(nc, x_prompt, x_sample, cache_lat, cache_kr, state_pool, cache_mk, cache_mv, page_table,
                mem_prompt, attn_norm, w_in, q_norm, kv_norm, w_q_up, w_uk, w_uv, w_pool_grp, pool_scale,
                mem_norm, w_mem_k, w_mem_v, w_pool_out, w_mla_out, w_x_out, w_o, ffn_norm, w_peer_q,
                peer_k1, peer_k2, peer_u, peer_v, final_norm, c_ident, c_causal, c_smask, c_trig,
                c_cnt, c_iota, y_p, y_s, lat_p, kr_p, pool_p, mk_p, mv_p, lat_s, kr_s, pool_s):
    with ExitStack() as ctx:
        sem = lambda name: ctx.enter_context(nc.semaphore(name))
        ARENA = 207 * 1024
        arena = ctx.enter_context(nc.sbuf_tensor("arena", [P, ARENA // 4], F32))
        bank = ctx.enter_context(nc.psum_tensor("bank", [P, 8, 512], F32))

        def at(kb, shape, dt=F32):
            n = 1
            for s in shape:
                n *= s
            a = int(kb * 256)
            assert a == kb * 256 and a + n <= ARENA // 4, (kb, shape)
            v = arena[:, a:a + n]
            if dt != F32:
                v = v.bitcast(dt)
            if len(shape) > 1:
                names = "abcd"[:len(shape)]
                v = v.rearrange(f"p ({' '.join(names)}) -> p {' '.join(names)}",
                                **{n: s for n, s in zip(names, shape)})
            return v

        ident = at(0, [2, P])
        eye = ident[:, 0]
        causal = at(1, [P])
        smask = at(1.5, [NB, NS])
        trig = at(2.5, [TILES, 32])
        cntfix = at(3.25, [PG, 16])
        iota16 = at(3.5, [16])
        gattn = at(3.75, [DK])
        gmem = at(3.78125, [DK])
        gq = at(3.8125, [3])
        pscale = at(3.84375, [PG])
        ss = at(4, [16])
        std = at(4.0625, [16])
        rstd = at(4.125, [16])
        pagetab = at(4.25, [P], mybir.dt.int32)
        gkv = at(4.75, [KL])
        gfin = at(6, [D])
        gffn = at(10, [D])
        junk = at(14, [D])
        nmax, rsum, rinv, nmax0 = at(18, [64]), at(18.25, [64]), at(18.5, [64]), at(4.75 + 1, [64])
        smx, ssum, srec, smx0 = at(18.75, [16]), at(18.8125, [16]), at(18.875, [16]), at(18.9375, [16])
        mmx, mmx0, msum, mrec = at(19, [4]), at(19.015625, [4]), at(19.03125, [8]), at(19.0625, [4])
        eps = at(19.078125, [1])
        spare = at(19.09375, [8])
        unew = at(19.25, [PG, NS])
        xnT = at(20, [DK, NT])
        pyT = at(37, [4, NT])
        moT = at(45.5, [4, NT])
        xoT = at(54, [4, NT])
        qxT = at(62.5, [4, NT])
        qT = at(71, [H, NT])
        cT = at(88, [2, NT])
        krT = at(92.25, [NT])
        cqkv = at(94.5, [TILES, 672])
        wuk = at(107.75, [2, 512])
        wuv = at(111.75, [2, 512])
        wring = at(115.75, [WRING, DK, 256])
        mnT = at(147.75, [DK, MEM])
        wqup = at(155.75, [3, 768])
        xin = at(164.75, [3, D])
        krp = at(205, [TILES, 96])
        uP = at(178.75, [PG, HIST + SEQ])
        uS = at(187, [PG, NB, HIST + TS])
        hist = at(189.5, [512])
        uout = at(191.5, [2, 512])
        mkv = at(195.5, [2, 2, 512])
        rot_a, rot_b = at(203.5, [H, ROPE]), at(191.5, [H, ROPE])
        qnT = at(164.75, [3, NT])
        qtm = at(147.75, [2, 768])
        dT = at(155.75, [PG, NT])
        wpool = at(171.5, [PG, P])
        psum_a = at(164.75, [SEQ + HIST])
        psum_b = at(167, [SEQ + HIST])
        ssum_a = at(169.25, [NB, HIST + TS])
        ssum_b = at(170, [NB, HIST + TS])
        pages = at(115.75, [2 * 4, PGRP, LATW])
        wukT = at(45.5, [H, KL])
        qrot = at(52, [NB, H, TS])
        qlat = at(56, [2, NB, H, TS])
        latT = at(164, [2, 2, 512])
        krpT = at(172, [2, 512])
        scor = at(176, [2080])
        prob = at(184.25, [2080])
        probT = at(60, [17, NS])
        olat = at(203.5, [KL])
        olatT = at(54, [2, H, NB, TS])
        osmp = at(58, [512])
        smem = at(115.75, [4, 2, 2, 512])
        smT = at(147.75, [XH, MEM])
        sms = at(151.75, [XH, MEM])
        smpT = at(155.75, [XH, 2, TS])
        smo = at(156, [512])
        kT = at(170, [H, SEQ])
        vtm = at(158, [4, 512])
        mkT = at(166, [XH, MEM])
        prb = at(142, [3, 512])
        prbT = at(148, [2, 4, P])
        otm = at(152, [2, 512])
        wmg = at(62.5, [2, 3, 12, P])
        mgT = at(98.5, [DK, NT])
        sig = at(115.5, [2, 2, HALF])
        mtmp = at(119.75, [2, HALF])
        wo = at(122, [DK, D])
        hall = at(167, [TILES, D])
        hn = at(187, [TILES, D])
        hnT = at(20, [DK, NT])
        wpq = at(37, [2, DK, P])
        qp = at(45, [2, NT])
        keysT = at(49.25, [2, P])
        keys = at(50.25, [2, P])
        scores = at(93, [ITS, 4, NKEY])
        uring = at(61, [RING, D])
        vring = at(127, [RING, D])
        hA, hB = at(6, [D]), at(14, [D])
        diag = at(159, [16, P])
        sc = at(54.5, [4, NKEY])
        cand = at(56.5, [2, 256])
        onehot = at(58.5, [32, 16])
        val = at(51.25, [4, 16])
        vix = at(51.5, [4, 16], U32)
        vixf = at(51.75, [4, 16])
        top, top0 = at(52.0, [2, 16]), at(52.125, [2, 16])
        sel = at(52.25, [2, 16], U32)
        sela = at(52.375, [2, 16], U32)
        selb = at(52.5, [2, 16], U32)
        selaf = at(52.625, [2, 16])
        selbf = at(52.75, [2, 16])
        e1 = at(52.875, [2, 16])
        e2 = at(53.0, [2, 16])
        gexp = at(53.125, [2, 16])
        gs2 = at(53.25, [8])
        gr2 = at(53.375, [8])
        idN = at(53.5, [32], U32)
        idA = at(53.625, [32], U32)
        idB = at(53.75, [16], U32)
        gN = at(53.875, [32])
        gB = at(54.0, [16])
        act_a = at(54.125, [16])
        act_g = at(54.25, [16])
        wts = at(54.375, [16])
        outb = at(61, [2, D])

        ld_const, ld_gain, ld_w, ld_state = sem("ld_const"), sem("ld_gain"), sem("ld_w"), sem("ld_state")
        zeroed = sem("zeroed")
        ld_x = [sem(f"ld_x{i}") for i in range(3)]
        sqrt_done, xs_done, xT_mm, xT_ev = map(sem, ("sqrt_done", "xs_done", "xT_mm", "xT_ev"))
        ld_ring = [sem(f"ld_ring{i}") for i in range(WRING)]
        st_mm, st_ev = sem("st_mm"), sem("st_ev")
        rstd_read, q_sqrt, q_norm_done, kr_done, c_mm, c_ev_d, c_ev_a = map(
            sem, ("rstd_read", "q_sqrt", "q_norm_done", "kr_done", "c_mm", "c_ev_d", "c_ev_a"))
        qu_mm, qu_ev, qu_rope, qt_mm, qt_ev = map(sem, ("qu_mm", "qu_ev", "qu_rope", "qt_mm", "qt_ev"))
        hi_mm, hi_ev, uo_mm, uo_ev, pool_d, pool_mm, pool_ev = map(
            sem, ("hi_mm", "hi_ev", "uo_mm", "uo_ev", "pool_d", "pool_mm", "pool_ev"))
        ld_pool = sem("ld_pool")
        uk_mm, uk_ev, ql_mm, ql_ev = map(sem, ("uk_mm", "uk_ev", "ql_mm", "ql_ev"))
        ld_page = [sem(f"ld_page{i}") for i in range(8)]
        pt_mm, pt_ev, pt_ed, ps_mm, ps_ev, ps_max, ps_exp, pp_mm, pp_ev, pv_free, pv_mm, pv_ev, po_mm, po_ev = map(
            sem, ("pt_mm", "pt_ev", "pt_ed", "ps_mm", "ps_ev", "ps_max", "ps_exp", "pp_mm", "pp_ev", "pv_free",
                  "pv_mm", "pv_ev", "po_mm", "po_ev"))
        so_mm, so_ev, sot_mm, sot_ev = map(sem, ("so_mm", "so_ev", "sot_mm", "sot_ev"))
        ld_sm0 = 16 * PGRP * NB // 2
        (mt_mm, mt_ev, ms_mm, ms_max, ms_exp, mp_mm, mp_ev, mo_mm, mo_ev, mx_mm, mx_ev) = map(
            sem, ("mt_mm", "mt_ev", "ms_mm", "ms_max", "ms_exp", "mp_mm", "mp_ev", "mo_mm", "mo_ev",
                  "mx_mm", "mx_ev"))
        kv_mm, kv_ev, krk_done = sem("kv_mm"), sem("kv_ev"), sem("krk_done")
        (at_mm, at_max, at_exp, at_tm, at_te, at_pv, at_oe, at_xm, at_xe) = map(
            sem, ("at_mm", "at_max", "at_exp", "at_tm", "at_te", "at_pv", "at_oe", "at_xm", "at_xe"))
        ld_mg = [sem(f"ld_mg{i}") for i in range(2)]
        mg_mm, mg_sig, mg_ev = sem("mg_mm"), sem("mg_sig"), sem("mg_ev")
        ld_wo, wo_mm, wo_ev = sem("ld_wo"), sem("wo_mm"), sem("wo_ev")
        hn_rep, h_sqrt, h_norm, hT_mm, hT_ev = map(sem, ("hn_rep", "h_sqrt", "h_norm", "hT_mm", "hT_ev"))
        ld_keys, key_mm, key_ev = sem("ld_keys"), sem("key_mm"), sem("key_ev")
        ld_pq = [sem(f"ld_pq{i}") for i in range(2)]
        pq_mm, pq_ev, sc_mm, sc_ev = map(sem, ("pq_mm", "pq_ev", "sc_mm", "sc_ev"))
        u_in = [sem(f"u_in{i}") for i in range(RING)]
        U0 = 16 * PGRP * NB // 2
        v_in = [sem(f"v_in{i}") for i in range(RING)]
        (tk_gap, tk_exp, id_next, id_a, id_b, g_b, gelu_done, w_done, diag_done, u_free, v_free,
         acc_free, h_a, h_b) = map(sem, (
            "tk_gap", "tk_exp", "id_next", "id_a", "id_b", "g_b", "gelu_done", "w_done", "diag_done",
            "u_free", "v_free", "acc_free", "h_a", "h_b"))
        f_sqrt, f_out = sem("f_sqrt"), sem("f_out")
        st_y = [sem("st_y0"), sem("st_y1")]
        stored, st_lat, st_pool = sem("stored"), sem("st_lat"), sem("st_pool")
        dve_chain, act_chain = sem("dve_chain"), sem("act_chain")
        carrier = sem("carrier")

        block = ctx.enter_context(nc.Block())

        @block.sync
        def _(sp):
            n_store = 0

            def store(dst, src):
                nonlocal n_store
                n_store += 1
                sp.dma_start(dst, src).then_inc(stored, 16)

            def load_x(i):
                if i >= 3:
                    sp.wait_ge(xT_mm, 2 * (i - 2))
                dst = xin[:, i % 3]
                if i == 0:
                    sp.dma_start(dst[0:NS], x_sample.rearrange("b t d -> (b t) d")).then_inc(ld_x[0], 16)
                elif i < TILES:
                    sp.dma_start(dst, x_prompt[0, (i - 1) * P:i * P]).then_inc(ld_x[i % 3], 16)
                else:
                    m = i - TILES
                    sp.dma_start(dst, mem_prompt[0, m * P:(m + 1) * P]).then_inc(ld_x[i % 3], 16)

            def load_stream(j):
                what, c, w = STREAM[j]
                if j >= WRING:
                    last = max(n for n, u in enumerate(UNITS) if u[0] == j - WRING)
                    sp.wait_ge(st_mm, last + 1)
                if what in ("qkv", "u", "qx"):
                    c += {"qkv": OFF_CQ, "u": OFF_U, "qx": OFF_QX}[what]
                    src = w_in[0][:, c:c + w]
                else:
                    src = (w_mem_k if what == "mk" else w_mem_v)[0].rearrange("d h e -> d (h e)")[:, c:c + w]
                sp.dma_start(wring[:, j % WRING, :, 0:w], src.rearrange("(k p) n -> p k n", p=P)).then_inc(
                    ld_ring[j % WRING], 16)

            sp.dma_start(ident[:], c_ident.rearrange("a p n -> p a n")).then_inc(ld_const, 16)
            sp.dma_start(gattn[:], attn_norm[0].rearrange("(k p) -> p k", p=P), allow_slow_non_contiguous=True).then_inc(ld_const, 16)
            sp.dma_start(gmem[:], mem_norm[0].rearrange("(k p) -> p k", p=P), allow_slow_non_contiguous=True).then_inc(ld_const, 16)
            for i in range(3):
                load_x(i)
            load_stream(0)
            load_stream(1)
            for i in range(3, 7):
                load_x(i)
                if i < 5:
                    load_stream(i - 1)
            sp.dma_start(causal[:], c_causal).then_inc(ld_gain, 16)
            sp.dma_start(smask[0:NS], c_smask).then_inc(ld_gain, 16)
            sp.dma_start(trig[:], c_trig).then_inc(ld_gain, 16)
            sp.dma_start(cntfix[:], c_cnt).then_inc(ld_gain, 16)
            sp.dma_start(iota16[:], c_iota).then_inc(ld_gain, 16)
            sp.dma_start(gq[:], q_norm[0].rearrange("(k p) -> p k", p=P), allow_slow_non_contiguous=True).then_inc(ld_gain, 16)
            sp.dma_start(pscale[:], pool_scale[0].rearrange("(k p) -> p k", p=P), allow_slow_non_contiguous=True).then_inc(ld_gain, 16)
            sp.dma_start(gkv[:], kv_norm.to_broadcast([P, KL])).then_inc(ld_gain, 16)
            sp.dma_start(gffn[:], ffn_norm.to_broadcast([P, D])).then_inc(ld_gain, 16)
            sp.dma_start(pagetab[0:1], page_table.rearrange("(a b) n -> a (b n)", a=1)).then_inc(ld_gain, 16)
            sp.dma_start(hist[0:NB * HIST], state_pool[0].rearrange("b t c -> (b t) c")).then_inc(ld_state, 16)
            store(pool_s[0][:, 0:HIST - TS], state_pool[0][:, TS:HIST])
            sp.dma_start(wqup[:], w_q_up[0].rearrange("(k p) h e -> p k (h e)", p=P)).then_inc(ld_w, 16)
            sp.dma_start(wuk[:], w_uk[0].rearrange("(k p) h e -> p k (h e)", p=P)).then_inc(ld_w, 16)
            sp.dma_start(wuv[:], w_uv[0].rearrange("(k p) h e -> p k (h e)", p=P)).then_inc(ld_w, 16)
            for j in range(4, len(STREAM)):
                load_stream(j)
            sp.wait_ge(st_ev, len(UNITS))
            for k, dst in enumerate((mk_p, mv_p)):
                store(dst[0, 0].rearrange("(m p) h e -> p m (h e)", p=P), mkv[:, k])
            sp.wait_ge(q_norm_done, 10)
            sp.wait_ge(kr_done, 1)
            for dst, src in ((lat_s[0].rearrange("b t c -> (b t) c"), cqkv[0:NS, 0, QL:QL + KL]),
                             (lat_p[0, 0].rearrange("(t p) c -> p t c", p=P), cqkv[:, 1:, QL:QL + KL]),
                             (kr_s[0].rearrange("b t c -> (b t) c"), krp[0:NS, 0, NOPE:QD]),
                             (kr_p[0, 0].rearrange("(t p) c -> p t c", p=P), krp[:, 1:, NOPE:QD])):
                sp.dma_start(dst, src).then_inc(st_lat, 16)
            sp.wait_ge(qu_mm, 2 * TILES)
            sp.dma_start(wpool[:], w_pool_grp[0].rearrange("g c d -> c g d")).then_inc(ld_pool, 16)
            sp.wait_ge(uo_ev, 2)
            for b in range(NB):
                sp.dma_start(pool_s[0, b, HIST - TS:HIST], uout[b * TS:(b + 1) * TS, 0]).then_inc(st_pool, 16)
            sp.dma_start(pool_p[0, 0], uout[0:HIST, 1]).then_inc(st_pool, 16)
            sp.wait_ge(qt_mm, 2 * TILES)

            def load_group(b, g):
                s = (b % 2) * 4 + g
                if b >= 2:
                    sp.wait_ge(pv_free, 4 * (b - 2) + g + 1)
                for k in range(PGRP):
                    n = b * PAGES + g * PGRP + k
                    page = sp.value_load(pagetab[0:1, n:n + 1], min_val=0, max_val=cache_lat.shape[1] - 1)
                    sp.dma_start(pages[:, s, k, 0:KL],
                                 cache_lat[0][DynSlice(page, 1)].rearrange("a p c -> (a p) c")).then_inc(ld_page[s], 16)

            sp.wait_ge(ld_gain, 16 * 10)
            for b in range(NB):
                for g in range(4):
                    load_group(b, g)
            sp.wait_ge(pv_mm, NB)
            for b in range(NB):
                if b >= 4:
                    sp.wait_ge(mo_mm, b - 3)
                    sp.wait_ge(mt_mm, 2 * (b - 3))
                for k, src in enumerate((cache_mk, cache_mv)):
                    sp.dma_start(smem[:, b % 4, k], src[0, b].rearrange("(m p) h e -> p m (h e)", p=P)).then_inc(
                        ld_page[b % 4], 16)
            def load_merge(f):
                if f >= 2:
                    sp.wait_ge(mg_mm, 3 * (f - 1))
                for i, wout in enumerate((w_pool_out, w_mla_out, w_x_out)):
                    c = OFF_G + i * D + f * P
                    sp.dma_start(wmg[:, f % 2, i, 0:8], w_in[0][:, c:c + P].rearrange("(k p) n -> p k n", p=P)).then_inc(
                        ld_mg[f % 2], 16)
                    sp.dma_start(wmg[:, f % 2, i, 8:12],
                                 wout[0][:, f * P:(f + 1) * P].rearrange("(k p) n -> p k n", p=P)).then_inc(
                        ld_mg[f % 2], 16)

            sp.wait_ge(at_mm, len(ATT))
            sp.wait_ge(at_pv, len(ATT))
            sp.wait_ge(at_xm, len(GROUPS))
            sp.wait_ge(st_lat, 16 * 4)
            load_merge(0)
            load_merge(1)
            sp.dma_start(wo[:], w_o[0].rearrange("(k p) n -> p k n", p=P)).then_inc(ld_wo, 16)
            sp.dma_start(hall[0:NS, slot(0)], x_sample.rearrange("b t d -> (b t) d")).then_inc(ld_wo, 16)
            sp.dma_start(hall[:, 0:TILES - 1], x_prompt[0].rearrange("(t p) d -> p t d", p=P)).then_inc(ld_wo, 16)
            for f in range(2, DK):
                load_merge(f)
            sp.wait_ge(mg_mm, 3 * DK)
            sp.dma_start(keys[:, 0], peer_k1[0]).then_inc(ld_keys, 16)
            sp.dma_start(keys[:, 1], peer_k2[0]).then_inc(ld_keys, 16)
            wq = w_peer_q[0].rearrange("(k p) h (a c) -> p k (h a) c", p=P, a=2)
            for i, j in enumerate(Q_LOADS):
                if i >= 2:
                    sp.wait_ge(pq_mm, i - 1)
                sp.dma_start(wpq[:, i % 2], wq[:, :, j]).then_inc(ld_pq[i % 2], 16)
            sp.wait_ge(w_done, 2 * ITS - 1)
            sp.dma_start(gfin[:], final_norm.rearrange("(a d) -> a d", a=1).to_broadcast([P, D])).then_inc(ld_gain, 16)
            for n in range(TILES):
                t = (n + 1) % TILES
                sp.wait_ge(f_out, n + 1)
                dst = y_s.rearrange("b t d -> (b t) d") if t == 0 else y_p[0, (t - 1) * P:t * P]
                sp.dma_start(dst, outb[0:rows(t), n % 2]).then_inc(st_y[n % 2], 16)
            sp.wait_ge(st_y[0], 48)
            sp.wait_ge(st_y[1], 32)
            sp.wait_ge(st_pool, 16 * (NB + 1))
            sp.wait_ge(st_lat, 16 * 4)
            sp.wait_ge(stored, 16 * n_store)

        @block.gpsimd
        def _(pool):
            pool.memset(ss[:], 1.0).then_inc(zeroed, 1)
            pool.memset(cqkv[:, 0], 0.0).then_inc(zeroed, 1)
            pool.memset(krp[:], 0.0).then_inc(zeroed, 1)
            pool.memset(uP[:, :, 0:HIST], 0.0).then_inc(zeroed, 1)
            pool.memset(eps[:], EPS).then_inc(zeroed, 1)
            pool.memset(spare[:, 0:1], 0.0).then_inc(u_free, RING)
            pool.memset(spare[:, 1:2], 0.0).then_inc(v_free, 16)
            pool.memset(spare[:, 2:3], 0.0).then_inc(acc_free, 2)

            pool.wait_ge(ld_gain, 16 * 10)
            pool.wait_ge(qt_mm, 2 * TILES)
            for b in range(NB):
                for g in range(4):
                    s = (b % 2) * 4 + g
                    if b >= 2:
                        pool.wait_ge(pv_free, 4 * (b - 2) + g + 1)
                    for k in range(PGRP):
                        n = b * PAGES + g * PGRP + k
                        page = pool.value_load(pagetab[0:1, n:n + 1], min_val=0, max_val=cache_kr.shape[1] - 1)
                        pool.dma_start(pages[:, s, k, KL:LATW],
                                       cache_kr[0][DynSlice(page, 1)].rearrange("a p c -> (a p) c")).then_inc(
                            u_in[s], 16)

            def gather(ring, land, k, table, ix):
                pool.sem_inc(carrier, 1)
                pool.indirect_dma_start(out=ring[:, k % RING], out_offset=None, in_=table[0],
                                        in_offset=IndirectOffsetOnAxis(ap=ix, axis=0)).then_inc(land[k % RING], 16)

            pool.wait_ge(id_next, 1)
            for k in range(16):
                pool.wait_ge(u_free, k + 1)
                gather(uring, u_in, k, peer_u, idN[:, k:k + 1])

            def half_1(it):
                pool.wait_ge(id_a, it + 1)
                for k in range(16):
                    pool.wait_ge(u_free, it * 32 + (16 + k + 1))
                    gather(uring, u_in, k, peer_u, idA[:, 16 + k:17 + k])
                    pool.wait_ge(v_free, it * 32 + (k + 1 + VCRED))
                    gather(vring, v_in, k, peer_v, idA[:, k:k + 1])

            def half_2(it, last):
                pool.wait_ge(id_b, it + 1)
                if not last:
                    pool.wait_ge(id_next, it + 2)
                for k in range(16):
                    if not last:
                        pool.wait_ge(u_free, it * 32 + (32 + k + 1))
                        gather(uring, u_in, k, peer_u, idN[:, k:k + 1])
                    pool.wait_ge(v_free, it * 32 + (16 + k + 1 + VCRED))
                    gather(vring, v_in, k, peer_v, idB[:, k:k + 1])

            with nc.gpsimd.Fori(0, ITS - 1) as it:
                half_1(it)
                half_2(it, False)
            half_1(ITS - 1)
            half_2(ITS - 1, True)

        @block.tensor
        def _(pe):
            def turn(dst, src, n):
                return pe.transpose(dst, src, eye[0:n, 0:n])

            def sum_k(dst, lhs, rhs, n):
                for k in range(n):
                    last = pe.matmul(dst, lhs(k), rhs(k), start=(k == 0), stop=(k == n - 1))
                return last

            pe.wait_ge(ld_const, 48)
            def turn_x(i):
                r = NS if i == 0 else P
                pe.wait_ge(xs_done, i + 1)
                for c in range(2):
                    n = 2 * i + c
                    if n >= 4:
                        pe.wait_ge(xT_ev, n - 3)
                    for k in range(4):
                        last = turn(bank[:, n % 4, k * P:k * P + r],
                                    xin[0:r, i % 3, (4 * c + k) * P:(4 * c + k + 1) * P], r)
                    last.then_inc(xT_mm, 1)

            def stream(n):
                j, what, c, w, m = UNITS[n]
                if n == 0 or UNITS[n - 1][0] != j:
                    pe.wait_ge(ld_ring[j % WRING], 16 * (j // WRING + 1))
                if n >= 4:
                    pe.wait_ge(st_ev, n - 3)
                b = 4 + n % 4
                wt = wring[:, j % WRING]
                if what == "qkv":
                    pe.wait_ge(xT_ev, 2 * (m + 1))
                    last = sum_k(bank[0:rows(m), b, 0:w], lambda k: xnT[:, k, cols(m)], lambda k: wt[:, k, 0:w], DK)
                elif what in ("u", "qx"):
                    last = sum_k(bank[:, b, 0:HALF], lambda k: wt[:, k, w * P:(w + 1) * P],
                                 lambda k: xnT[:, k, m * HALF:(m + 1) * HALF], DK)
                else:
                    last = sum_k(bank[:, b, 0:w], lambda k: mnT[:, k, m * P:(m + 1) * P], lambda k: wt[:, k, 0:w], DK)
                last.then_inc(st_mm, 1)

            for i in range(5):
                turn_x(i)
                stream(i)
            turn_x(5)
            for n in range(5, 10):
                stream(n)
            turn_x(6)
            pe.wait_ge(xT_ev, 14)
            for n in range(10, LAST_U + 1):
                stream(n)
            def turn_c(t):
                r = rows(t)
                pe.wait_ge(q_norm_done, 2 * (t + 1))
                pe.wait_ge(kr_done, 1)
                b = 2 * (t % 2)
                if t >= 2:
                    pe.wait_ge(c_ev_d, t - 1)
                    pe.wait_ge(c_ev_a, t - 1)
                for k in range(3):
                    last = turn(bank[:, b, k * P:k * P + r], cqkv[0:r, t, k * P:(k + 1) * P], r)
                last.then_inc(c_mm, 1)
                for k in range(2):
                    turn(bank[:, b + 1, k * P:k * P + r], cqkv[0:r, t, QL + k * P:QL + (k + 1) * P], r)
                turn(bank[0:QD, b + 1, 2 * P:2 * P + r], krp[0:r, t], r).then_inc(c_mm, 1)

            rest = list(range(LAST_U + 1, len(UNITS)))
            for t in range(TILES):
                stream(rest[t])
                turn_c(t)
            for n in rest[TILES:]:
                stream(n)
            pe.wait_ge(ld_w, 48)
            pe.wait_ge(st_ev, len(UNITS))
            pe.wait_ge(c_ev_d, TILES)
            pe.wait_ge(c_ev_a, TILES)
            for t in range(TILES + 1):
                if t < TILES:
                    for c in range(2):
                        n = 2 * t + c
                        if n >= 4:
                            pe.wait_ge(qu_ev, n - 3)
                        sum_k(bank[0:rows(t), 4 + n % 4, 0:384], lambda k: qnT[:, k, cols(t)],
                              lambda k: wqup[:, k, c * 384:(c + 1) * 384], 3).then_inc(qu_mm, 1)
                if t >= 1:
                    pe.wait_ge(qu_rope, t)
                    r = rows(t - 1)
                    for c in range(2):
                        n = 2 * (t - 1) + c
                        if n >= 4:
                            pe.wait_ge(qt_ev, n - 3)
                        for k in range(4):
                            h = 4 * c + k
                            last = turn(bank[0:QD, n % 4, k * P:k * P + r],
                                        qtm[0:r, (t - 1) % 2, h * QD:(h + 1) * QD], r)
                        last.then_inc(qt_mm, 1)
            pe.wait_ge(ld_state, 16)
            pe.wait_ge(qt_ev, 2 * TILES)
            for g in range(PG):
                last = turn(bank[:, 0, g * P:g * P + NB * HIST], hist[0:NB * HIST, g * P:(g + 1) * P], NB * HIST)
            last.then_inc(hi_mm, 1)
            for g in range(PG):
                last = turn(bank[0:NS, 1, g * P:(g + 1) * P], unew[:, g], P)
            last.then_inc(uo_mm, 1)
            for g in range(PG):
                last = turn(bank[0:HIST, 2, g * P:(g + 1) * P], uP[:, g, SEQ:SEQ + HIST], P)
            last.then_inc(uo_mm, 1)
            pe.wait_ge(hi_ev, 1)
            pe.wait_ge(uo_ev, 2)
            for n in range(4):
                for i in range(4):
                    h, c = 2 * n + i // 2, i % 2
                    last = turn(bank[0:NOPE, n, i * P:(i + 1) * P], wuk[:, c, h * NOPE:(h + 1) * NOPE], P)
                last.then_inc(uk_mm, 1)
            pe.wait_ge(qu_ev, 2 * TILES)
            pe.wait_ge(uk_ev, 4)
            for h in range(H):
                for c in range(2):
                    last = pe.matmul(bank[:, 4, (h * 2 + c) * NS:(h * 2 + c + 1) * NS],
                                     wukT[0:NOPE, h, c * P:(c + 1) * P], qT[0:NOPE, h, 0:NS], start=True, stop=True)
            last.then_inc(ql_mm, 1)
            pe.wait_ge(ql_ev, 3)
            pe.wait_ge(ld_pool, 16)
            for n in range(2 * PG):
                g, half = n // 2, n % 2
                pe.wait_ge(pool_d, g + 1)
                if n >= 4:
                    pe.wait_ge(pool_ev, n - 3)
                pe.matmul(bank[:, 4 + n % 4, 0:HALF], wpool[:, g], dT[:, g, half * HALF:(half + 1) * HALF],
                          start=True, stop=True).then_inc(pool_mm, 1)

            def page_turns(b, g):
                n = 4 * b + g
                pe.wait_ge(ld_page[n % 8], 16 * PGRP * (b // 2 + 1))
                pe.wait_ge(u_in[n % 8], 16 * PGRP * (b // 2 + 1))
                if n >= 1:
                    pe.wait_ge(pt_ev, n)
                    pe.wait_ge(pt_ed, 2 * n)
                for c in range(2):
                    for k in range(PGRP):
                        last = turn(bank[:, c, k * P:(k + 1) * P], pages[:, n % 8, k, c * P:(c + 1) * P], P)
                    last.then_inc(pt_mm, 1)
                for k in range(PGRP):
                    last = turn(bank[0:QD, 2, k * P:(k + 1) * P], pages[:, n % 8, k, LATW - QD:LATW], P)
                last.then_inc(pt_mm, 1)

            def page_scores(b, g):
                n, m = 4 * b + g, 5 * b + g
                if g < 4:
                    pe.wait_ge(pt_ev, n + 1)
                    pe.wait_ge(pt_ed, 2 * (n + 1))
                if m >= 2:
                    pe.wait_ge(ps_ev, m - 1)
                w = 512 if g < 4 else NS
                dst = bank[0:NS, 3 + m % 2, 0:w]
                kc = (lambda c: latT[:, n % 2, c]) if g < 4 else (lambda c: cT[:, c, 0:NS])
                kr = krpT[NOPE:QD, n % 2] if g < 4 else krT[NOPE:QD, 0:NS]
                for c in range(2):
                    pe.matmul(dst, qlat[:, c, b].rearrange("p h t -> p (h t)"), kc(c), start=(c == 0), stop=False)
                pe.matmul(dst, qrot[NOPE:QD, b].rearrange("p h t -> p (h t)"), kr, start=False,
                          stop=True).then_inc(ps_mm, 1)

            def page_probs(b):
                pe.wait_ge(ps_exp, b + 1)
                if b >= 1:
                    pe.wait_ge(pp_ev, 2 * b)
                    pe.wait_ge(po_ev, b)
                for k in range(PAGES):
                    last = turn(bank[:, 5, k * NS:(k + 1) * NS], prob[0:NS, k * P:(k + 1) * P], NS)
                last.then_inc(pp_mm, 1)
                turn(bank[0:NS, 6, 0:NS], prob[0:NS, PAGES * P:PAGES * P + NS], NS).then_inc(pp_mm, 1)

            def page_values(b):
                pe.wait_ge(pp_ev, 2 * (b + 1))
                if b >= 1:
                    pe.wait_ge(pv_ev, b)
                for k in range(PAGES):
                    s = (b % 2) * 4 + k // PGRP
                    last = pe.matmul(bank[0:NS, 7, 0:KL], probT[:, k], pages[:, s, k % PGRP, 0:KL],
                                     start=(k == 0), stop=False)
                    if k % PGRP == PGRP - 1:
                        last.then_inc(pv_free, 1)
                pe.matmul(bank[0:NS, 7, 0:KL], probT[0:NS, PAGES], cqkv[0:NS, 0, QL:QL + KL], start=False,
                          stop=True).then_inc(pv_mm, 1)

            def page_out(b):
                pe.wait_ge(pv_ev, b + 1)
                for c in range(2):
                    last = turn(bank[:, 6, 64 + c * NS:64 + (c + 1) * NS], olat[0:NS, c * P:(c + 1) * P], NS)
                last.then_inc(po_mm, 1)

            pe.wait_ge(pool_ev, 2 * PG)
            for b in range(NB + 1):
                if b < NB:
                    page_turns(b, 0)
                    page_turns(b, 1)
                    page_scores(b, 0)
                    page_turns(b, 2)
                    page_scores(b, 1)
                if b >= 1:
                    page_probs(b - 1)
                if b < NB:
                    page_turns(b, 3)
                    page_scores(b, 2)
                if b >= 1:
                    page_values(b - 1)
                if b < NB:
                    page_scores(b, 3)
                if b >= 1:
                    page_out(b - 1)
                if b < NB:
                    page_scores(b, 4)
            pe.wait_ge(po_ev, NB)
            pe.wait_ge(ps_ev, 5 * NB)
            for h in range(H):
                for c in range(2):
                    last = pe.matmul(bank[0:NS, 3, h * VD:(h + 1) * VD], olatT[:, c, h].rearrange("p b t -> p (b t)"),
                                     wuv[:, c, h * VD:(h + 1) * VD], start=(c == 0), stop=(c == 1))
            last.then_inc(so_mm, 1)
            pe.wait_ge(so_ev, 1)
            for c in range(4):
                last = turn(bank[:, 4, c * NS:(c + 1) * NS], osmp[0:NS, c * P:(c + 1) * P], NS)
            last.then_inc(sot_mm, 1)

            pe.wait_ge(pt_ev, 4 * NB)
            pe.wait_ge(pt_ed, 8 * NB)
            def mem_turns(b):
                pe.wait_ge(ld_page[b % 4], ld_sm0 + 32 * (b // 4 + 1))
                if b >= 1:
                    pe.wait_ge(mt_ev, 2 * b)
                for i in range(2):
                    for k in range(4):
                        h, m = 2 * i + k // 2, k % 2
                        last = turn(bank[:, i, k * P:(k + 1) * P], smem[:, b % 4, 0, m, h * XD:(h + 1) * XD], P)
                    last.then_inc(mt_mm, 1)

            def mem_scores(b):
                pe.wait_ge(mt_ev, 2 * (b + 1))
                if b >= 1:
                    pe.wait_ge(ms_exp, XH * b)
                for h in range(XH):
                    last = pe.matmul(bank[0:TS, 2 + h // 2, (h % 2) * MEM:(h % 2 + 1) * MEM],
                                     qxT[:, h, b * TS:(b + 1) * TS], smT[:, h], start=True, stop=True)
                last.then_inc(ms_mm, 1)

            def mem_probs(b):
                pe.wait_ge(ms_exp, XH * (b + 1))
                if b >= 1:
                    pe.wait_ge(mp_ev, b)
                for h in range(XH):
                    for m in range(2):
                        last = turn(bank[:, 5, (h * 2 + m) * TS:(h * 2 + m + 1) * TS],
                                    sms[0:TS, h, m * P:(m + 1) * P], TS)
                last.then_inc(mp_mm, 1)

            def mem_values(b):
                pe.wait_ge(mp_ev, b + 1)
                if b >= 1:
                    pe.wait_ge(mo_ev, b)
                for h in range(XH):
                    for m in range(2):
                        last = pe.matmul(bank[0:TS, 6, h * XD:(h + 1) * XD], smpT[:, h, m],
                                         smem[:, b % 4, 1, m, h * XD:(h + 1) * XD],
                                         start=(m == 0), stop=(m == 1))
                last.then_inc(mo_mm, 1)

            def mem_out(b):
                pe.wait_ge(mo_ev, b + 1)
                if b >= 1:
                    pe.wait_ge(mx_ev, b)
                for c in range(4):
                    last = turn(bank[:, 7, c * TS:(c + 1) * TS], smo[0:TS, c * P:(c + 1) * P], TS)
                last.then_inc(mx_mm, 1)

            def prompt_kv(n):
                if n >= 1:
                    pe.wait_ge(kv_ev, n)
                if n < 2:
                    for k in range(4):
                        h, m = 2 * n + k // 2, k % 2
                        last = turn(bank[:, 4, k * P:(k + 1) * P], mkv[:, 0, m, h * XD:(h + 1) * XD], P)
                elif n < 10:
                    h = n - 2
                    last = sum_k(bank[0:NOPE, 4], lambda k: wuk[:, k, h * NOPE:(h + 1) * NOPE],
                                 lambda k: cT[:, k, NS:NT], 2)
                else:
                    t = n - 10
                    last = sum_k(bank[:, 4], lambda k: cT[:, k, cols(t + 1)], lambda k: wuv[:, k], 2)
                last.then_inc(kv_mm, 1)

            pe.wait_ge(sot_ev, 1)
            mem_turns(0)
            for b in range(NB + 2):
                if b < NB:
                    mem_scores(b)
                if b < KV_UNITS // 2:
                    prompt_kv(2 * b)
                if 1 <= b <= NB:
                    mem_probs(b - 1)
                if b + 1 < NB:
                    mem_turns(b + 1)
                if b < KV_UNITS // 2:
                    prompt_kv(2 * b + 1)
                if b >= 2:
                    mem_out(b - 2)
                if 1 <= b <= NB:
                    mem_values(b - 1)

            def att_scores(u):
                kind, q, h, L = ATT[u]
                if u >= 3:
                    pe.wait_ge(at_exp, u - 2)
                dst = bank[:, u % 3, 0:L]
                if kind == "mla":
                    pe.matmul(dst, qT[0:QD, h, cols(q + 1)], kT[0:QD, h, 0:L], start=True, stop=True).then_inc(at_mm, 1)
                else:
                    pe.matmul(dst, qxT[:, h, cols(q + 1)], mkT[:, h], start=True, stop=True).then_inc(at_mm, 1)

            def att_turn(u):
                L = ATT[u][3]
                pe.wait_ge(at_exp, u + 1)
                if u >= 2:
                    pe.wait_ge(at_te, u - 1)
                for k in range(L // P):
                    last = turn(bank[:, 3 + u % 2, k * P:(k + 1) * P], prb[:, u % 3, k * P:(k + 1) * P], P)
                last.then_inc(at_tm, 1)

            def att_values(u):
                kind, q, h, L = ATT[u]
                g = GROUP_OF[u]
                pe.wait_ge(at_te, u + 1)
                if h == 0 and g >= 2:
                    pe.wait_ge(at_oe, g - 1)
                if kind == "mla":
                    last = sum_k(bank[:, 5 + g % 2, h * VD:(h + 1) * VD], lambda k: prbT[:, u % 2, k],
                                 lambda k: vtm[:, k, h * VD:(h + 1) * VD], L // P)
                else:
                    last = sum_k(bank[:, 5 + g % 2, h * XD:(h + 1) * XD], lambda k: prbT[:, u % 2, k],
                                 lambda k: mkv[:, 1, k, h * XD:(h + 1) * XD], L // P)
                last.then_inc(at_pv, 1)

            def att_out(g):
                pe.wait_ge(at_oe, g + 1)
                if g >= 1:
                    pe.wait_ge(at_xe, g)
                for c in range(4):
                    last = turn(bank[:, 7, c * P:(c + 1) * P], otm[:, g % 2, c * P:(c + 1) * P], P)
                last.then_inc(at_xm, 1)

            pe.wait_ge(kv_ev, KV_UNITS)
            pe.wait_ge(mx_ev, NB)
            pe.wait_ge(krk_done, 1)
            for u in range(len(ATT) + 5):
                if u < len(ATT):
                    att_scores(u)
                if 2 <= u <= len(ATT) + 1:
                    att_turn(u - 2)
                if 3 <= u <= len(ATT) + 2:
                    att_values(u - 3)
                for g, (_, _, _, end) in enumerate(GROUPS):
                    if u - 5 == end:
                        att_out(g)

            pe.wait_ge(at_xe, len(GROUPS))
            for n in range(3 * DK):
                f, i = n // 3, n % 3
                if i == 0:
                    pe.wait_ge(ld_mg[f % 2], 16 * 6 * (f // 2 + 1))
                if n >= 2:
                    pe.wait_ge(mg_ev, n - 1)
                src = (pyT, moT, xoT)[i]
                for half in range(2):
                    span = slice(half * HALF, (half + 1) * HALF)
                    sum_k(bank[:, 4 * (n % 2) + half, 0:HALF], lambda k: wmg[:, f % 2, i, k],
                          lambda k: xnT[:, k, span], DK)
                for half in range(2):
                    span = slice(half * HALF, (half + 1) * HALF)
                    last = sum_k(bank[:, 4 * (n % 2) + 2 + half, 0:HALF], lambda k: wmg[:, f % 2, i, 8 + k],
                                 lambda k: src[:, k, span], 4)
                last.then_inc(mg_mm, 1)
            pe.wait_ge(mg_ev, 3 * DK)
            pe.wait_ge(ld_wo, 48)
            def resid(i):
                t = (i + 1) % TILES
                for c in range(2):
                    n = 2 * i + c
                    if n >= 4:
                        pe.wait_ge(wo_ev, n - 3)
                    sum_k(bank[0:rows(t), n % 4], lambda k: mgT[:, k, cols(t)],
                          lambda k: wo[:, k, c * 512:(c + 1) * 512], DK).then_inc(wo_mm, 1)

            def turn_h(i):
                r = rows((i + 1) % TILES)
                pe.wait_ge(h_norm, i + 1)
                for c in range(2):
                    n = 2 * i + c
                    if n >= 4:
                        pe.wait_ge(hT_ev, n - 3)
                    for k in range(4):
                        last = turn(bank[:, 4 + n % 4, k * P:k * P + r], hn[0:r, i, (4 * c + k) * P:(4 * c + k + 1) * P], r)
                    last.then_inc(hT_mm, 1)

            resid(0)
            resid(1)
            pe.wait_ge(ld_keys, 32)
            for a in range(2):
                last = turn(bank[:, 7, a * P:(a + 1) * P], keys[:, a], P)
            last.then_inc(key_mm, 1)
            turn_h(0)
            pe.wait_ge(hT_ev, 2)
            for j in range(EARLY):
                pe.wait_ge(ld_pq[j % 2], 16 * (j // 2 + 1))
                sum_k(bank[:, 6, j * P:(j + 1) * P], lambda k: wpq[:, j % 2, k], lambda k: hnT[:, k, cols(1)],
                      DK).then_inc(pq_mm, 1)
            pe.wait_ge(key_ev, 1)
            pe.wait_ge(pq_ev, 1)
            for j in range(EARLY):
                last = pe.matmul(bank[:, 7, j * P:(j + 1) * P], qp[:, 0, j * P:(j + 1) * P], keysT[:, j % 2],
                                 start=True, stop=True)
            last.then_inc(sc_mm, 1)
            resid(2)
            pe.wait_ge(sc_ev, 1)
            turn_h(1)
            for i in range(3, TILES):
                resid(i)
                turn_h(i - 1)
            turn_h(TILES - 1)

            def queries(j):
                i = EARLY + j
                pe.wait_ge(ld_pq[i % 2], 16 * (i // 2 + 1))
                pe.wait_ge(pq_ev, j + 1)
                for half in range(2):
                    last = sum_k(bank[:, 4 + half, 0:HALF], lambda k: wpq[:, i % 2, k],
                                 lambda k: hnT[:, k, half * HALF:(half + 1) * HALF], DK)
                last.then_inc(pq_mm, 1)

            def key_scores(j):
                pe.wait_ge(pq_ev, j + 2)
                pe.wait_ge(sc_ev, j + 1)
                for t in range(1, TILES):
                    pe.matmul(bank[:, 6, (t - 1) * P:t * P], qp[:, j % 2, cols(t)], keysT[:, j % 2], start=True, stop=True)
                pe.matmul(bank[0:NS, 7, 0:P], qp[:, j % 2, 0:NS], keysT[:, j % 2], start=True, stop=True).then_inc(sc_mm, 1)

            def weigh(it, b, j=None):
                pe.wait_ge(acc_free, it * 2 + (b + 1))
                for k in range(16):
                    if j is not None and k == 7:
                        queries(j)
                    if j is not None and k == 12:
                        key_scores(j)
                    pe.wait_ge(diag_done, it * 32 + (16 * b + k + 1))
                    pe.wait_ge(v_in[k % RING], it * 64 + 16 * (2 * b + k // RING + 1))
                    for c in range(2):
                        last = pe.matmul(bank[:, 2 * b + c], diag[:, k], vring[:, k % RING, c * 512:(c + 1) * 512],
                                         start=(k == 0), stop=(k == 15))
                    last.then_inc(v_free, 1)

            pe.wait_ge(hT_ev, 2 * TILES)
            pe.wait_ge(wo_ev, 2 * TILES)
            for j in range(5):
                if j < 4:
                    queries(j)
                if j >= 1:
                    key_scores(j - 1)
            for it in range(Q_STEPS):
                weigh(it, 0, 4 + 2 * it)
                weigh(it, 1, 5 + 2 * it)
            with nc.tensor.Fori(Q_STEPS, ITS) as it:
                weigh(it, 0)
                weigh(it, 1)
        @block.scalar
        def _(act):
            chain = 0

            def link(ins):
                nonlocal chain
                chain += 1
                ins.then_inc(act_chain, 1)
                act.wait_ge(act_chain, chain)

            def copy(dst, src, scale=1.0):
                return act.activation(dst, src, ACT.Copy, scale=scale)

            def root_mean(r, col, src, width):
                link(act.activation(junk[0:r, 0:width], src, ACT.Square, accum_out=ss[0:r, col:col + 1]))
                return act.activation(std[0:r, col:col + 1], ss[0:r, col:col + 1], ACT.Sqrt, scale=1.0 / width,
                                      bias=eps[0:r])

            act.wait_ge(zeroed, 5)

            def squares(i):
                act.wait_ge(ld_x[i % 3], 16 * (i // 3 + 1))
                r = NS if i == 0 else P
                root_mean(r, i, xin[0:r, i % 3], D).then_inc(sqrt_done, 1)

            def stream_out(n):
                j, what, c, w, m = UNITS[n]
                act.wait_ge(st_mm, n + 1)
                b = 4 + n % 4
                if what == "qkv":
                    last = copy(cqkv[0:rows(m), m, c:c + w], bank[0:rows(m), b, 0:w])
                elif what == "qx":
                    last = copy(qxT[:, c, m * HALF:(m + 1) * HALF], bank[:, b, 0:HALF])
                elif what == "u":
                    if m == 0:
                        copy(uS[:, c, :, HIST:HIST + TS], bank[:, b, 0:NS].rearrange("p (b t) -> p b t", t=TS))
                        copy(unew[:, c], bank[:, b, 0:NS])
                        last = copy(uP[:, c, HIST:HIST + HALF - NS], bank[:, b, NS:HALF])
                    else:
                        last = copy(uP[:, c, HIST + HALF - NS:HIST + SEQ], bank[:, b, 0:HALF])
                else:
                    last = copy(mkv[:, 0 if what == "mk" else 1, m, c:c + w], bank[:, b, 0:w])
                last.then_inc(st_ev, 1)

            for i in range(3):
                squares(i)
            for i in range(3, 7):
                squares(i)
                stream_out(i - 3)
            for n in range(4, LAST_QKV + 1):
                stream_out(n)
            act.wait_ge(st_ev, LAST_QKV + 1)
            for t in range(TILES):
                root_mean(rows(t), 0, cqkv[0:rows(t), t, 0:QL], QL).then_inc(q_sqrt, 1)
                act.wait_ge(q_sqrt, 2 * t + 1)
                act.wait_ge(rstd_read, 2 * t + 1)
                root_mean(rows(t), 0, cqkv[0:rows(t), t, QL:QL + KL], KL).then_inc(q_sqrt, 1)
                act.wait_ge(rstd_read, 2 * t + 2)
            for n in range(LAST_QKV + 1, LAST_U + 1):
                stream_out(n)

            def out_c(t):
                r = rows(t)
                act.wait_ge(c_mm, 2 * (t + 1))
                b = 2 * (t % 2) + 1
                copy(cT[:, :, cols(t)], bank[:, b, 0:2 * P].rearrange("p (k r) -> p k r", k=2)[:, :, 0:r])
                copy(krT[NOPE:QD, cols(t)], bank[NOPE:QD, b, 2 * P:2 * P + r]).then_inc(c_ev_a, 1)

            rest = list(range(LAST_U + 1, len(UNITS)))
            for t in range(TILES):
                stream_out(rest[t])
                out_c(t)
            for n in rest[TILES:]:
                stream_out(n)
            for t in range(TILES + 1):
                if t < TILES:
                    r = rows(t)
                    if t >= 2:
                        act.wait_ge(qt_mm, 2 * (t - 1))
                    for c in range(2):
                        n = 2 * t + c
                        act.wait_ge(qu_mm, n + 1)
                        copy(qtm[0:r, t % 2, c * 384:(c + 1) * 384], bank[0:r, 4 + n % 4, 0:384]).then_inc(qu_ev, 1)
                if t >= 1:
                    r = rows(t - 1)
                    for c in range(2):
                        n = 2 * (t - 1) + c
                        act.wait_ge(qt_mm, n + 1)
                        copy(qT[0:QD, 4 * c:4 * c + 4, cols(t - 1)],
                             bank[0:QD, n % 4].rearrange("p (k r) -> p k r", k=4)[:, :, 0:r]).then_inc(qt_ev, 1)
            act.wait_ge(hi_mm, 1)
            for g in range(PG):
                last = copy(uS[:, g, :, 0:HIST], bank[:, 0, g * P:g * P + NB * HIST].rearrange("p (b t) -> p b t", b=NB))
            last.then_inc(hi_ev, 1)
            for n in range(4):
                act.wait_ge(uk_mm, n + 1)
                copy(wukT[0:NOPE, 2 * n:2 * n + 2].rearrange("p a b -> p (a b)"), bank[0:NOPE, n]).then_inc(uk_ev, 1)
            act.wait_ge(ql_mm, 1)
            for c in range(2):
                src = bank[:, 4].rearrange("p (h c b t) -> p c b h t", h=H, c=2, b=NB)[:, c]
                copy(qlat[:, c], src).then_inc(ql_ev, 1)
            for n in range(2 * PG):
                act.wait_ge(pool_mm, n + 1)
                act.activation(pyT[:, n // 2, (n % 2) * HALF:(n % 2 + 1) * HALF], bank[:, 4 + n % 4, 0:HALF], ACT.Copy,
                               scale=pscale[:, n // 2:n // 2 + 1]).then_inc(pool_ev, 1)

            def turn_out(n):
                act.wait_ge(pt_mm, 3 * n + 1)
                if n >= 2:
                    act.wait_ge(ps_mm, 5 * ((n - 2) // 4) + (n - 2) % 4 + 1)
                copy(latT[:, n % 2, 0], bank[:, 0]).then_inc(pt_ev, 1)

            def score_out(b, g):
                m = 5 * b + g
                act.wait_ge(ps_mm, m + 1)
                w = 512 if g < 4 else NS
                copy(scor[0:NS, g * 512:g * 512 + w], bank[0:NS, 3 + m % 2, 0:w]).then_inc(ps_ev, 1)

            act.wait_ge(st_pool, 16 * (NB + 1))
            def page_exp(b):
                act.wait_ge(ps_max, b + 1)
                if b >= 1:
                    act.wait_ge(pp_mm, 2 * b)
                act.activation(prob[0:NS], scor[0:NS], ACT.Exp, scale=MLA_SCALE, bias=smx[0:NS, b:b + 1],
                               accum_out=ssum[0:NS, b:b + 1]).then_inc(ps_exp, 1)

            for b in range(NB + 1):
                if b < NB:
                    turn_out(4 * b)
                    turn_out(4 * b + 1)
                if b >= 1:
                    page_exp(b - 1)
                if b < NB:
                    if b >= 1:
                        act.wait_ge(ps_exp, b)
                    score_out(b, 0)
                    turn_out(4 * b + 2)
                    score_out(b, 1)
                    turn_out(4 * b + 3)
                    for g in range(2, 5):
                        score_out(b, g)
            act.wait_ge(sot_mm, 1)
            copy(moT[:, :, 0:NS], bank[:, 4, 0:4 * NS].rearrange("p (c n) -> p c n", c=4)).then_inc(sot_ev, 1)

            def mem_keys_out(b):
                if b >= 1:
                    act.wait_ge(ms_mm, b)
                for i in range(2):
                    act.wait_ge(mt_mm, 2 * b + i + 1)
                    copy(smT[:, 2 * i:2 * i + 2].rearrange("p a b -> p (a b)"), bank[:, i]).then_inc(mt_ev, 1)

            def prompt_kv_out(n):
                act.wait_ge(kv_mm, n + 1)
                if n < 2:
                    dst, r = mkT[:, 2 * n:2 * n + 2].rearrange("p a b -> p (a b)"), P
                elif n < 10:
                    dst, r = kT[0:NOPE, n - 2], NOPE
                else:
                    dst, r = vtm[:, n - 10], P
                copy(dst, bank[0:r, 4]).then_inc(kv_ev, 1)

            mem_keys_out(0)
            for b in range(NB + 2):
                if b < KV_UNITS // 2:
                    prompt_kv_out(2 * b)
                if b < NB:
                    act.wait_ge(ms_max, b + 1)
                    if b >= 1:
                        act.wait_ge(mp_mm, b)
                    for h in range(XH):
                        act.activation(sms[0:TS, h], bank[0:TS, 2 + h // 2, (h % 2) * MEM:(h % 2 + 1) * MEM], ACT.Exp,
                                       scale=MEM_SCALE, bias=mmx[0:TS, h:h + 1],
                                       accum_out=msum[0:TS, 4 * (b % 2) + h:4 * (b % 2) + h + 1]).then_inc(ms_exp, 1)
                if b + 1 < NB:
                    mem_keys_out(b + 1)
                if b < KV_UNITS // 2:
                    prompt_kv_out(2 * b + 1)
                if b >= 2:
                    act.wait_ge(mx_mm, b - 1)
                    copy(xoT[:, :, (b - 2) * TS:(b - 1) * TS], bank[:, 7, 0:4 * TS].rearrange("p (c n) -> p c n", c=4)).then_inc(
                        mx_ev, 1)

            for u in range(len(ATT) + 6):
                if u < len(ATT):
                    kind, q, h, L = ATT[u]
                    act.wait_ge(at_max, u + 1)
                    if u >= 3:
                        act.wait_ge(at_tm, u - 2)
                    act.activation(prb[:, u % 3, 0:L], bank[:, u % 3, 0:L], ACT.Exp,
                                   scale=MLA_SCALE if kind == "mla" else MEM_SCALE, bias=nmax[:, u:u + 1],
                                   accum_out=rsum[:, u:u + 1]).then_inc(at_exp, 1)
                if 2 <= u <= len(ATT) + 1:
                    L = ATT[u - 2][3]
                    act.wait_ge(at_tm, u - 1)
                    if u >= 4:
                        act.wait_ge(at_pv, u - 3)
                    copy(prbT[:, u % 2, 0:L // P].rearrange("p a b -> p (a b)"),
                         bank[:, 3 + u % 2, 0:L]).then_inc(at_te, 1)
                for g, (kind, q, _, end) in enumerate(GROUPS):
                    if u - 5 == end:
                        act.wait_ge(at_xm, g + 1)
                        dst = moT if kind == "mla" else xoT
                        copy(dst[:, :, cols(q + 1)], bank[:, 7].rearrange("p (c n) -> p c n", c=4)).then_inc(at_xe, 1)

            for n in range(3 * DK):
                act.wait_ge(mg_mm, n + 1)
                if n >= 2:
                    act.wait_ge(mg_ev, n - 1)
                b = 4 * (n % 2)
                act.activation(sig[:, n % 2], bank[:, b:b + 2, 0:HALF], ACT.Sigmoid).then_inc(mg_sig, 1)

            def resid_mean(i):
                t = (i + 1) % TILES
                act.wait_ge(wo_ev, 2 * (i + 1))
                if i >= 1:
                    act.wait_ge(h_norm, i)
                root_mean(rows(t), 0, hall[0:rows(t), i], D).then_inc(h_sqrt, 1)

            def turn_h_out(i):
                t = (i + 1) % TILES
                r = rows(t)
                for c in range(2):
                    n = 2 * i + c
                    act.wait_ge(hT_mm, n + 1)
                    copy(hnT[:, 4 * c:4 * c + 4, cols(t)],
                         bank[:, 4 + n % 4].rearrange("p (k r) -> p k r", k=4)[:, :, 0:r]).then_inc(hT_ev, 1)

            def query_out(j):
                act.wait_ge(pq_mm, EARLY + j + 1)
                act.wait_ge(sc_mm, max(j, 1))
                copy(qp[:, j % 2].rearrange("p (a b) -> p a b", a=2), bank[:, 4:6, 0:HALF]).then_inc(pq_ev, 1)

            def scores_out(j):
                pair, s = j // 4, j % 4
                t0 = 1 if pair == 0 else 0
                act.wait_ge(sc_mm, j + 2)
                copy(scores[:, 4 * pair + t0:4 * pair + 4, s], bank[:, 6, t0 * P:].rearrange("p (t k) -> p t k", k=P))
                copy(scores[32 * pair:32 * pair + 32, ITS - 1, s], bank[0:NS, 7, 0:P]).then_inc(
                    sc_ev, 1 if j < 15 else 5)

            def picked_exp(n):
                act.wait_ge(tk_gap, n)
                act.activation(gexp[:], top[:], ACT.Exp).then_inc(tk_exp, 1)

            def diagonals(it, b, last_step=False):
                act.wait_ge(w_done, it * 2 + (b + 1))
                for k in range(16):
                    act.wait_ge(v_free, it * 32 + (16 * b + k + 1))
                    act.sem_inc(carrier, 1)
                    act.activation(diag[:, k], ident[:, 1 if last_step else 0], ACT.Copy,
                                   scale=wts[:, k:k + 1]).then_inc(diag_done, 1)

            def tile_copy(dst, it, done):
                act.sem_inc(carrier, 1)
                if isinstance(it, int):
                    src = hn[:, (it + 1) % 4 if it < ITS - 2 else slot(0)]
                else:
                    src = hn[:, DynSlice((it + 1) % 4, 1)].rearrange("p a d -> p (a d)")
                act.activation(dst, src, ACT.Copy).then_inc(done, 1)

            resid_mean(0)
            act.wait_ge(key_mm, 1)
            copy(keysT.rearrange("p a b -> p (a b)"), bank[:, 7, 0:2 * P]).then_inc(key_ev, 1)
            turn_h_out(0)
            act.wait_ge(pq_mm, EARLY)
            copy(qp[:, 0, 0:EARLY * P], bank[:, 6]).then_inc(pq_ev, 1)
            resid_mean(1)
            act.wait_ge(sc_mm, 1)
            copy(scores[:, 0].rearrange("p a b -> p (a b)"), bank[:, 7]).then_inc(sc_ev, 1)
            copy(hA[:], hn[:, 0]).then_inc(h_a, 1)
            resid_mean(2)
            turn_h_out(1)
            picked_exp(1)
            resid_mean(3)
            turn_h_out(2)
            resid_mean(4)
            turn_h_out(3)
            turn_h_out(4)
            act.wait_ge(hn_rep, 1)
            copy(hB[:], hn[:, 0]).then_inc(h_b, 1)
            query_out(0)
            query_out(1)
            scores_out(0)
            act.wait_ge(u_free, RING + 16)
            act.activation(act_g[:], act_a[:], ACT.Gelu).then_inc(gelu_done, 1)
            query_out(2)
            scores_out(1)
            query_out(3)
            scores_out(2)
            scores_out(3)

            def one_step(it, j=None):
                diagonals(it, 0)
                tile_copy(hA[:], it, h_a)
                if j is not None:
                    query_out(j)
                    scores_out(j)
                picked_exp(it + 2)
                act.wait_ge(u_free, it * 32 + (RING + 32))
                act.activation(act_g[:], act_a[:], ACT.Gelu).then_inc(gelu_done, 1)
                diagonals(it, 1)
                tile_copy(hB[:], it, h_b)
                if j is not None:
                    query_out(j + 1)
                    scores_out(j + 1)
                act.wait_ge(u_free, it * 32 + (RING + 48))
                act.activation(act_g[:], act_a[:], ACT.Gelu).then_inc(gelu_done, 1)

            for it in range(Q_STEPS):
                one_step(it, 4 + 2 * it)
            with nc.scalar.Fori(Q_STEPS, ITS - 2) as it:
                one_step(it)
            one_step(ITS - 2)
            last = ITS - 1
            diagonals(last, 0, True)
            act.wait_ge(u_free, last * 32 + (RING + 32))
            act.activation(act_g[:], act_a[:], ACT.Gelu).then_inc(gelu_done, 1)
            diagonals(last, 1, True)
            for n in range(TILES):
                t = (n + 1) % TILES
                act.wait_ge(acc_free, 2 * ITS + (2 if t == 0 else 0))
                if n >= 1:
                    act.wait_ge(f_out, n)
                root_mean(rows(t), 0, hall[0:rows(t), slot(t)], D).then_inc(f_sqrt, 1)

        @block.vector
        def _(dve):
            chain = 0

            def link(ins):
                nonlocal chain
                chain += 1
                ins.then_inc(dve_chain, 1)
                dve.wait_ge(dve_chain, chain)

            tt, ts, stt = dve.tensor_tensor, dve.tensor_scalar, dve.scalar_tensor_tensor

            dve.wait_ge(zeroed, 5)
            dve.wait_ge(ld_const, 48)

            def scale_x(i):
                r = NS if i == 0 else P
                dve.wait_ge(sqrt_done, i + 1)
                link(dve.reciprocal(rstd[0:r, i:i + 1], std[0:r, i:i + 1]))
                ts(xin[0:r, i % 3], xin[0:r, i % 3], rstd[0:r, i:i + 1], None, ALU.mult).then_inc(xs_done, 1)

            def out_x(i):
                r = NS if i == 0 else P
                for c in range(2):
                    n = 2 * i + c
                    dve.wait_ge(xT_mm, n + 1)
                    src = bank[:, n % 4].rearrange("p (k r) -> p k r", k=4)[:, :, 0:r]
                    g = (gattn if i < TILES else gmem)[:, 4 * c:4 * c + 4].unsqueeze(2).to_broadcast([P, 4, r])
                    dst = xnT[:, 4 * c:4 * c + 4, cols(i)] if i < TILES else \
                        mnT[:, 4 * c:4 * c + 4, (i - TILES) * P:(i - TILES + 1) * P]
                    tt(dst, src, g, ALU.mult).then_inc(xT_ev, 1)

            for i in range(8):
                if i < 7:
                    scale_x(i)
                if i >= 1:
                    out_x(i - 1)

            dve.wait_ge(ld_gain, 16 * 10)
            for t in range(TILES):
                r = rows(t)
                dve.wait_ge(q_sqrt, 2 * t + 1)
                dve.reciprocal(rstd[0:r, 0:1], std[0:r, 0:1]).then_inc(rstd_read, 1)
                dve.wait_ge(rstd_read, 2 * t + 1)
                ts(cqkv[0:r, t, 0:QL], cqkv[0:r, t, 0:QL], rstd[0:r, 0:1], None, ALU.mult).then_inc(q_norm_done, 1)
                dve.wait_ge(q_sqrt, 2 * t + 2)
                dve.reciprocal(rstd[0:r, 1:2], std[0:r, 0:1]).then_inc(rstd_read, 1)
                dve.wait_ge(rstd_read, 2 * t + 2)
                stt(cqkv[0:r, t, QL:QL + KL], cqkv[0:r, t, QL:QL + KL], rstd[0:r, 1:2], gkv[0:r], ALU.mult,
                    ALU.mult).then_inc(q_norm_done, 1)

            def rope(dst, src, cos, sin, ta, tb):
                half = ROPE // 2
                x1, x2 = src[..., 0:half], src[..., half:ROPE]
                tt(ta[..., 0:half], x1, cos, ALU.mult)
                tt(ta[..., half:ROPE], x2, cos, ALU.mult)
                tt(tb[..., 0:half], x2, sin, ALU.mult)
                link(tt(tb[..., half:ROPE], x1, sin, ALU.mult))
                tt(dst[..., 0:half], ta[..., 0:half], tb[..., 0:half], ALU.subtract)
                return tt(dst[..., half:ROPE], ta[..., half:ROPE], tb[..., half:ROPE], ALU.add)

            rope(krp[:, :, NOPE:QD], cqkv[:, :, QL + KL:QL + KL + ROPE], trig[:, :, 0:16], trig[:, :, 16:32],
                 rot_a[:, 0:TILES], rot_b[:, 0:TILES]).then_inc(kr_done, 1)
            for t in range(TILES):
                r = rows(t)
                dve.wait_ge(c_mm, 2 * t + 1)
                src = bank[:, 2 * (t % 2), 0:3 * P].rearrange("p (k r) -> p k r", k=3)[:, :, 0:r]
                tt(qnT[:, :, cols(t)], src, gq.unsqueeze(2).to_broadcast([P, 3, r]), ALU.mult).then_inc(c_ev_d, 1)
            for t in range(TILES):
                r = rows(t)
                dve.wait_ge(qu_ev, 2 * (t + 1))
                q = qtm[0:r, t % 2].rearrange("p (h e) -> p h e", h=H)[:, :, NOPE:QD]
                cs = [trig[0:r, t, 16 * k:16 * k + 16].unsqueeze(1).to_broadcast([r, H, 16]) for k in range(2)]
                dve.wait_ge(*((qu_rope, t) if t else (kr_done, 1)))
                rope(q, q, cs[0], cs[1], rot_a[0:r], rot_b[0:r]).then_inc(qu_rope, 1)
            for k, r in enumerate((NS, HIST)):
                dve.wait_ge(uo_mm, k + 1)
                dve.tensor_copy(uout[0:r, k], bank[0:r, 1 + k]).then_inc(uo_ev, 1)
            dve.wait_ge(qt_ev, 2 * TILES)
            dve.tensor_copy(qrot[NOPE:QD], qT[NOPE:QD, :, 0:NS].rearrange("p h (b t) -> p b h t", b=NB)).then_inc(ql_ev, 1)
            dve.wait_ge(hi_ev, 1)
            dve.wait_ge(st_mm, len(UNITS))
            dve.wait_ge(qu_mm, 2 * TILES)
            for g in range(PG):
                n, w = HIST + SEQ, 2 << g
                sP, sS = uP[:, g], uS[:, g]
                if g:
                    dve.wait_ge(pool_d, g)
                for step in range(g + 1):
                    sh = 1 << step
                    lo = 2 * sh - 1
                    dP, dS = ((psum_a, ssum_a), (psum_b, ssum_b))[step % 2]
                    tt(dP[:, lo:n], sP[:, lo:n], sP[:, lo - sh:n - sh], ALU.add)
                    link(tt(dS[:, :, lo:], sS[:, :, lo:], sS[:, :, lo - sh:HIST + TS - sh], ALU.add))
                    sP, sS = dP, dS
                link(tt(sP[:, HIST:HIST + 16], sP[:, HIST:HIST + 16], cntfix[:, g], ALU.mult))
                stt(dT[:, g, NS:NT], sP[:, HIST:n], 1.0 / w, uP[:, g, HIST:n], ALU.mult, ALU.subtract)
                stt(dT[:, g, 0:NS].rearrange("p (b t) -> p b t", b=NB), sS[:, :, HIST:], 1.0 / w,
                    uS[:, g, :, HIST:], ALU.mult, ALU.subtract).then_inc(pool_d, 1)
            dve.wait_ge(c_ev_a, TILES)

            dve.wait_ge(st_pool, 16 * (NB + 1))
            def keys_out(b, g):
                n = 4 * b + g
                dve.wait_ge(pt_mm, 3 * n + 2)
                if n >= 2:
                    dve.wait_ge(ps_mm, 5 * ((n - 2) // 4) + (n - 2) % 4 + 1)
                dve.tensor_copy(latT[:, n % 2, 1], bank[:, 1]).then_inc(pt_ed, 1)
                dve.wait_ge(pt_mm, 3 * n + 3)
                dve.tensor_copy(krpT[NOPE:QD, n % 2], bank[NOPE:QD, 2]).then_inc(pt_ed, 1)

            def largest(b):
                dve.wait_ge(ps_ev, 5 * (b + 1))
                new = scor[0:NS, PAGES * PAGE:PAGES * PAGE + NS]
                link(tt(new, new, smask[0:NS, b], ALU.add))
                link(dve.reduce_max(smx0[0:NS, b:b + 1], scor[0:NS], AX_X))
                ts(smx[0:NS, b:b + 1], smx0[0:NS, b:b + 1], -MLA_SCALE, None, ALU.mult).then_inc(ps_max, 1)

            for b in range(NB + 1):
                a = b - 1
                if b < NB:
                    keys_out(b, 0)
                if b >= 1:
                    largest(a)
                if b < NB:
                    keys_out(b, 1)
                    keys_out(b, 2)
                if b >= 1:
                    dve.wait_ge(pp_mm, 2 * a + 1)
                    if a >= 1:
                        dve.wait_ge(pv_mm, a)
                    dve.tensor_copy(probT[:, 0:PAGES].rearrange("p a b -> p (a b)"), bank[:, 5]).then_inc(pp_ev, 1)
                    dve.wait_ge(pp_mm, 2 * a + 2)
                    dve.tensor_copy(probT[0:NS, PAGES], bank[0:NS, 6, 0:NS]).then_inc(pp_ev, 1)
                if b < NB:
                    keys_out(b, 3)
                if b >= 1:
                    link(dve.reciprocal(srec[0:NS, a:a + 1], ssum[0:NS, a:a + 1]))
                    dve.wait_ge(pv_mm, a + 1)
                    ts(olat[0:NS], bank[0:NS, 7, 0:KL], srec[0:NS, a:a + 1], None, ALU.mult).then_inc(pv_ev, 1)
                    dve.wait_ge(po_mm, a + 1)
                    dve.tensor_copy(olatT[:, :, :, a], bank[:, 6, 64:64 + 2 * NS].rearrange(
                        "p (c h t) -> p c h t", c=2, h=H)).then_inc(po_ev, 1)
            dve.wait_ge(so_mm, 1)
            dve.tensor_copy(osmp[0:NS], bank[0:NS, 3]).then_inc(so_ev, 1)

            dve.tensor_copy(kT[NOPE:QD], krT[NOPE:QD, NS:NT].unsqueeze(1).to_broadcast([ROPE, H, SEQ])).then_inc(krk_done, 1)

            for b in range(NB + 1):
                if b < NB:
                    dve.wait_ge(ms_mm, b + 1)
                    link(dve.reduce_max(mmx0[0:TS], bank[0:TS, 2:4].rearrange("p a (h m) -> p (a h) m", h=2), AX_X))
                    if b >= 1:
                        dve.wait_ge(ms_exp, XH * b)
                    ts(mmx[0:TS], mmx0[0:TS], -MEM_SCALE, None, ALU.mult).then_inc(ms_max, 1)
                if b >= 1:
                    dve.wait_ge(mp_mm, b)
                    if b >= 2:
                        dve.wait_ge(mo_mm, b - 1)
                    dve.tensor_copy(smpT.rearrange("p h m t -> p (h m t)"), bank[:, 5, 0:XH * 2 * TS]).then_inc(mp_ev, 1)
                    s = 4 * ((b - 1) % 2)
                    if b >= 2:
                        dve.wait_ge(mo_ev, b - 1)
                    link(dve.reciprocal(mrec[0:TS], msum[0:TS, s:s + 4]))
                    dve.wait_ge(mo_mm, b)
                    if b >= 2:
                        dve.wait_ge(mx_mm, b - 1)
                    tt(smo[0:TS].rearrange("p (h e) -> p h e", h=XH), bank[0:TS, 6].rearrange("p (h e) -> p h e", h=XH),
                       mrec[0:TS].unsqueeze(2).to_broadcast([TS, XH, XD]), ALU.mult).then_inc(mo_ev, 1)

            for u in range(len(ATT) + 4):
                if u < len(ATT):
                    kind, q, h, L = ATT[u]
                    dve.wait_ge(at_mm, u + 1)
                    if kind == "mla":
                        d = bank[:, u % 3, L - P:L]
                        link(tt(d, d, causal[:], ALU.add))
                    link(dve.reduce_max(nmax0[:, u:u + 1], bank[:, u % 3, 0:L], AX_X))
                    ts(nmax[:, u:u + 1], nmax0[:, u:u + 1], -(MLA_SCALE if kind == "mla" else MEM_SCALE), None,
                       ALU.mult).then_inc(at_max, 1)
                for g, (kind, q, first, end) in enumerate(GROUPS):
                    if u - 4 == end:
                        n = end - first + 1
                        dve.wait_ge(at_exp, end + 1)
                        link(dve.reciprocal(rinv[:, first:end + 1], rsum[:, first:end + 1]))
                        dve.wait_ge(at_pv, end + 1)
                        if g >= 2:
                            dve.wait_ge(at_xm, g - 1)
                        tt(otm[:, g % 2].rearrange("p (h e) -> p h e", h=n),
                           bank[:, 5 + g % 2].rearrange("p (h e) -> p h e", h=n),
                           rinv[:, first:end + 1].unsqueeze(2).to_broadcast([P, n, 512 // n]), ALU.mult).then_inc(at_oe, 1)

            for n in range(3 * DK):
                f, i = n // 3, n % 3
                dve.wait_ge(mg_sig, n + 1)
                b = 4 * (n % 2) + 2
                out = mgT[:, f].rearrange("p (a b) -> p a b", a=2)
                if i == 0:
                    if f == 0:
                        dve.wait_ge(st_lat, 16 * 4)
                    tt(out, sig[:, n % 2], bank[:, b:b + 2, 0:HALF], ALU.mult).then_inc(mg_ev, 1)
                    dve.wait_ge(mg_ev, n + 1)
                else:
                    link(tt(mtmp[:], sig[:, n % 2], bank[:, b:b + 2, 0:HALF], ALU.mult))
                    tt(out, out, mtmp[:], ALU.add).then_inc(mg_ev, 1)
                    dve.wait_ge(mg_ev, n + 1)
            dve.wait_ge(ld_wo, 48)
            for q in range(1, 4):
                dve.memset(hall[32 * q:32 * q + 32, slot(0)], 0.0)
            def resid(i):
                r = rows((i + 1) % TILES)
                for c in range(2):
                    n = 2 * i + c
                    dve.wait_ge(wo_mm, n + 1)
                    part = hall[0:r, i, c * 512:(c + 1) * 512]
                    tt(part, part, bank[0:r, n % 4], ALU.add).then_inc(wo_ev, 1)
                dve.wait_ge(h_sqrt, i + 1)
                link(dve.reciprocal(rstd[0:r, i:i + 1], std[0:r, 0:1]))
                stt(hn[0:r, i], hall[0:r, i], rstd[0:r, i:i + 1], gffn[0:r], ALU.mult, ALU.mult).then_inc(h_norm, 1)

            def step(ins):
                dve.drain()

            def top16(values, indices, source):
                step(dve.max(values[:, 0:8], source))
                step(dve.max_index(indices[:, 0:8], values[:, 0:8], source))
                step(dve.match_replace(source, values[:, 0:8], source, NEG))
                step(dve.max(values[:, 8:16], source))
                step(dve.max_index(indices[:, 8:16], values[:, 8:16], source))

            def pick_sides(at_step):
                step(dve.tensor_copy(sc.rearrange("p a b -> p (a b)"),
                                     scores[:, DynSlice(at_step, 1)].rearrange("p x a b -> p (x a b)")))
                for q in range(4):
                    top16(val[:, q], vix[:, q], sc[:, q])
                step(dve.tensor_copy(vixf[:], vix[:]))

            def pick_pairs(n):
                for h in range(2):
                    step(tt(cand[:, h].rearrange("p (a b) -> p a b", a=16), val[:, 2 * h].unsqueeze(2).to_broadcast([P, 16, 16]),
                            val[:, 2 * h + 1].unsqueeze(1).to_broadcast([P, 16, 16]), ALU.add))
                for h in range(2):
                    top16(top0[:, h], sel[:, h], cand[:, h])
                tt(top[:], top0[:], top0[:, :, 0:1].to_broadcast([P, 2, 16]), ALU.subtract).then_inc(tk_gap, 1)
                ts(sela[:], sel[:], 4, None, ALU.logical_shift_right)
                step(ts(selb[:], sel[:], 15, None, ALU.bitwise_and))
                dve.tensor_copy(selaf[:], sela[:])
                step(dve.tensor_copy(selbf[:], selb[:]))
                for side, pos, dst in ((0, selaf, e1), (1, selbf, e2)):
                    step(tt(onehot[:], pos.rearrange("p a b -> p (a b)").unsqueeze(2).to_broadcast([P, 32, 16]),
                            iota16.unsqueeze(1).to_broadcast([P, 32, 16]), ALU.is_equal))
                    for h in range(2):
                        part = onehot[:, 16 * h:16 * h + 16]
                        last = tt(part, part, vixf[:, 2 * h + side].unsqueeze(1).to_broadcast([P, 16, 16]), ALU.mult)
                    step(last)
                    step(dve.reduce_sum(dst.rearrange("p a b -> p (a b)"), onehot[:], AX_X))
                stt(idN[:].rearrange("p (a b) -> p a b", a=2), e1[:], float(NKEY), e2[:], ALU.mult, ALU.add).then_inc(id_next, 1)
                dve.wait_ge(tk_exp, n)
                step(dve.reduce_sum(gs2[:, 0:2], gexp[:], AX_X))
                step(dve.reciprocal(gr2[:, 0:2], gs2[:, 0:2]))
                step(tt(gN.rearrange("p (a b) -> p a b", a=2), gexp[:], gr2[:, 0:2].unsqueeze(2).to_broadcast([P, 2, 16]),
                        ALU.mult))

            def products(land0, h, ready, n, k0=0, k1=16):
                if k0 == 0:
                    dve.wait_ge(ready, n)
                for k in range(k0, k1):
                    dve.wait_ge(u_in[k % RING], land0 + U0 + 16 * (k // RING + 1))
                    dve.tensor_tensor_reduce(uring[:, k % RING], uring[:, k % RING], h[:], 1.0, 0.0, ALU.mult, ALU.add,
                                             act_a[:, k:k + 1]).then_inc(u_free, 1)

            def weights(n, diags, gates):
                dve.wait_ge(gelu_done, n)
                if diags is not None:
                    dve.wait_ge(diag_done, diags)
                tt(wts[:], act_g[:], gates, ALU.mult).then_inc(w_done, 1)

            def add_sum(it, b):
                dve.wait_ge(v_free, it * 32 + 16 * (b + 2))
                dve.wait_ge(acc_free, it * 2 + (b + 2))
                if isinstance(it, int):
                    y = hall[:, it % 4 if it < ITS - 1 else slot(0)]
                else:
                    y = hall[:, DynSlice(it % 4, 1)].rearrange("p a d -> p (a d)")
                tt(y, y, bank[:, 2 * b:2 * b + 2].rearrange("p a b -> p (a b)"), ALU.add).then_inc(acc_free, 1)

            def hand_over():
                dve.tensor_copy(idA[:], idN[:]).then_inc(id_a, 1)
                dve.tensor_copy(gB[:], gN[:, 16:32]).then_inc(g_b, 1)

            resid(0)
            resid(1)
            dve.wait_ge(sc_ev, 1)
            pick_sides(0)
            resid(2)
            pick_pairs(1)
            hand_over()
            dve.wait_ge(id_a, 1)
            dve.tensor_copy(idB[:], idA[:, 16:32]).then_inc(id_b, 1)
            resid(3)
            resid(4)
            dve.wait_ge(h_norm, TILES)
            for q in range(1, 4):
                last = dve.tensor_copy(hn[32 * q:32 * q + 32, slot(0)], hn[0:32, slot(0)])
            last.then_inc(hn_rep, 1)
            products(0, hA, h_a, 1)
            weights(1, None, gN[:, 0:16])

            def one_step(it):
                first = isinstance(it, int) and it == 0
                if first:
                    products(it * 64 + 32, hB, h_b, it + 1, 0, PICK_ROW)
                dve.wait_ge(w_done, it * 2 + 1)
                dve.wait_ge(sc_ev, (it + 1) // 4 * 4 + 5)
                dve.wait_ge(g_b, it + 1)
                pick_sides(it + 1)
                if not first:
                    products(it * 64 + 32, hB, h_b, it + 1, 0, PICK_ROW)
                pick_pairs(it + 2)
                products(it * 64 + 32, hB, h_b, it + 1, PICK_ROW, 16)
                weights(it * 2 + 2, it * 32 + 16, gB[:])
                add_sum(it, 0)
                dve.wait_ge(w_done, it * 2 + 2)
                hand_over()
                products(it * 64 + 64, hA, h_a, it + 2)
                weights(it * 2 + 3, it * 32 + 32, gN[:, 0:16])
                add_sum(it, 1)
                dve.wait_ge(id_a, it + 2)
                dve.tensor_copy(idB[:], idA[:, 16:32]).then_inc(id_b, 1)

            one_step(0)
            with nc.vector.Fori(1, ITS - 2) as it:
                one_step(it)
            one_step(ITS - 2)
            last = ITS - 1
            products(last * 64 + 32, hB, h_b, last + 1)
            dve.wait_ge(g_b, last + 1)
            weights(last * 2 + 2, last * 32 + 16, gB[:])
            def final(n):
                t = (n + 1) % TILES
                r = rows(t)
                dve.wait_ge(f_sqrt, n + 1)
                link(dve.reciprocal(rstd[0:r, 8 + n % 2:9 + n % 2], std[0:r, 0:1]))
                if n >= 2:
                    dve.wait_ge(st_y[n % 2], 16 * (n // 2))
                stt(outb[0:r, n % 2], hall[0:r, slot(t)], rstd[0:r, 8 + n % 2:9 + n % 2], gfin[0:r], ALU.mult,
                    ALU.mult).then_inc(f_out, 1)

            dve.wait_ge(ld_gain, 16 * 11)
            for n in range(TILES - 1):
                final(n)
            add_sum(last, 0)
            add_sum(last, 1)
            final(TILES - 1)

_INS = ["x_prompt", "x_sample", "cache_kv_latent", "cache_k_rope", "state_pool", "cache_mem_k", "cache_mem_v",
        "page_table", "mem_prompt", "attn_norm", "w_in", "q_norm", "kv_norm", "w_q_up", "w_uk", "w_uv",
        "w_pool_grp", "pool_scale", "mem_norm", "w_mem_k", "w_mem_v", "w_pool_out", "w_mla_out", "w_x_out",
        "w_o", "ffn_norm", "w_peer_q", "peer_k1", "peer_k2", "peer_u", "peer_v", "final_norm"]
_OUTS = [(1, SEQ, D), (NB, TS, D), (1, 1, SEQ, KL), (1, 1, SEQ, ROPE), (1, 1, HIST, 512),
         (1, 1, MEM, XH, XD), (1, 1, MEM, XH, XD), (1, NB, TS, KL), (1, NB, TS, ROPE), (1, NB, HIST, 512)]


def shape_constants():
    import numpy as np
    f = np.float32
    p = np.arange(P)
    fold = ((p[:, None] % NS == p[None, :]) & (p[None, :] < NS)).astype(f)
    ident = np.stack([np.eye(P, dtype=f), fold])
    causal = np.where(p[None, :] <= p[:, None], 0.0, -1.0e30).astype(f)
    row_t, col = np.arange(NS) % TS, np.arange(NS)
    smask = np.full((NS, NB, NS), -1.0e30, f)
    for b in range(NB):
        own = (col[None, :] // TS == b) & (col[None, :] % TS <= row_t[:, None])
        smask[:, b][own] = 0.0
    inv = np.power(f(10000.0), -np.arange(16, dtype=f) / f(16)).astype(f)
    pos = np.zeros((TILES, P), f)
    pos[0, :NS] = 2048 + np.arange(NS) % TS
    pos[1:] = np.arange(SEQ).reshape(TILES - 1, P)
    ang = (pos[:, :, None] * inv).astype(f)
    trig = np.ascontiguousarray(np.concatenate([np.cos(ang), np.sin(ang)], -1).astype(f).transpose(1, 0, 2))
    w = np.array([2, 4, 8, 16], f)[:, None]
    cnt = np.broadcast_to((w / np.minimum(np.arange(16, dtype=f) + 1, w)).astype(f), (P, PG, 16)).copy()
    iota = np.broadcast_to(np.arange(16, dtype=f), (P, 16)).copy()
    return {"c_ident": ident, "c_causal": causal, "c_smask": smask, "c_trig": trig,
            "c_cnt": cnt, "c_iota": iota}


def kernel(**inputs):
    import numpy as _np
    import concourse.bacc as _bacc
    from concourse import mybir as _mybir
    from concourse.bass_utils import run_bass_kernel_spmd as _run

    nc = _bacc.Bacc("TRN2", target_bir_lowering=False, num_devices=1)
    arrays, args = {}, []
    for name in _INS:
        a = _np.ascontiguousarray(inputs[name])
        arrays[f"in_{name}_dram"] = a
        args.append(nc.dram_tensor(f"in_{name}_dram", a.shape, _mybir.dt.from_np(a.dtype), kind="ExternalInput").ap())
    for name, a in shape_constants().items():
        arrays[f"in_{name}_dram"] = a
        args.append(nc.dram_tensor(f"in_{name}_dram", a.shape, _mybir.dt.from_np(a.dtype), kind="ExternalInput").ap())
    for i, shape in enumerate(_OUTS):
        args.append(nc.dram_tensor(f"out_{i}_dram", shape, F32, kind="ExternalOutput").ap())
    hybrid_step(nc, *args)
    r = _run(nc, [arrays], core_ids=[0])
    return tuple(r.results[0][f"out_{i}_dram"] for i in range(len(_OUTS)))
```
